# Optimizing a Trainium2 kernel written in Bass

```python
import math
import functools
import jax
import jax.numpy as jnp
from jax import lax
import numpy as np

D_MODEL = 1024
BATCH = 1
SEQ = 128
DEPTH = 2
DEC_BATCH = 1
DEC_SEQ = 512
PAST_LEN = 128

GRID_W = 64
EPS = 1e-6
ROPE_THETA = 10000.0
ROPE_DIM = 32
Q_BLOCK = 128
F32 = jnp.float32

H_A = 4
DK_A = ROPE_DIM
DV_A = 2 * DK_A
W_A = H_A * DV_A
H_B = 8
NOPE_B = 64
ROPE_B = ROPE_DIM
DV_B = 64
W_B = H_B * DV_B
Q_RANK_B = 256
KV_RANK_B = 128
H_C = 4
DK_C = 64
DV_C = 64
W_QK_C = H_C * DK_C
W_C = H_C * DV_C
CONV_C = 3
CHUNK_C = 64

MIX_W = W_A + W_B + W_C

A_Q = 0
A_K = A_Q + H_A * 2 * DK_A
A_V = A_K + H_A * 2 * DK_A
B_QC = A_V + W_A
B_KVC = B_QC + Q_RANK_B
B_KR = B_KVC + KV_RANK_B
C_QKV = B_KR + ROPE_B
C_G = C_QKV + 2 * W_QK_C + W_C
C_BF = C_G + W_C
C_BB = C_BF + H_C
C_AF = C_BB + H_C
C_AB = C_AF + H_C
P_IN = C_AB + H_C

PEER_HEADS = 8
N_KEYS = 128
N_EXPERTS = N_KEYS * N_KEYS
PEER_TOPK = 16
PEER_DQ = 256
PEER_BLOCK = 128

kernel_name = 'hybrid_diffusion_prefix_step'

def rms_norm(x, g):
    xf = x.astype(F32)
    y = xf * lax.rsqrt(jnp.mean(xf * xf, axis=-1, keepdims=True) + EPS)
    return (y * g.astype(F32)).astype(x.dtype)

def l2_norm(x):
    xf = x.astype(F32)
    return xf * lax.rsqrt(jnp.sum(xf * xf, axis=-1, keepdims=True) + EPS)

def modulation(cvec, w_mod, b_mod):
    m = (jax.nn.silu(cvec) @ w_mod + b_mod)[:, None, :]
    return jnp.split(m, 6, axis=-1)

def axial_rope_tables(n_tokens, dim):
    rows = n_tokens // GRID_W
    t = jnp.arange(rows * GRID_W)
    row = (t // GRID_W).astype(F32)
    col = (t % GRID_W).astype(F32)
    n_freq = dim // 4
    freqs = ROPE_THETA ** (-jnp.arange(n_freq, dtype=F32) / n_freq)
    ar = row[:, None] * freqs
    ac = col[:, None] * freqs
    ang = jnp.concatenate([ar, ar, ac, ac], axis=-1)
    return jnp.cos(ang), jnp.sin(ang)

def apply_rope(x, cos, sin):
    shape = (cos.shape[0],) + (1,) * (x.ndim - 3) + (cos.shape[1],)
    cos = cos.reshape(shape).astype(x.dtype)
    sin = sin.reshape(shape).astype(x.dtype)
    x1r, x2r, x1c, x2c = jnp.split(x, 4, axis=-1)
    rot = jnp.concatenate([-x2r, x1r, -x2c, x1c], axis=-1)
    return x * cos + rot * sin

def map_query_blocks(fn, *qs):
    b, s = qs[0].shape[:2]
    nb = s // Q_BLOCK
    blocks = tuple(jnp.moveaxis(q.reshape((b, nb, Q_BLOCK) + q.shape[2:]), 1, 0) for q in qs)
    out = lax.map(lambda t: fn(*t), blocks)
    out = jnp.moveaxis(out, 0, 1)
    return out.reshape((b, s) + out.shape[3:])

def diff_attention(q, k, v, lam):
    scale = DK_A ** -0.5
    def block(qb):
        sc = jnp.einsum('bqhmd,bshmd->bmhqs', qb, k).astype(F32) * scale
        p = jax.nn.softmax(sc, axis=-1)
        a = p[:, 0] - lam * p[:, 1]
        return jnp.einsum('bhqs,bshd->bqhd', a.astype(v.dtype), v)
    return map_query_blocks(block, q)

def mla_attention(q_nope, q_rope, k_nope, k_rope, v):
    scale = (NOPE_B + ROPE_B) ** -0.5
    def block(qn, qr):
        sc = (jnp.einsum('bqhd,bshd->bhqs', qn, k_nope) + jnp.einsum('bqhd,bsd->bhqs', qr, k_rope)).astype(F32) * scale
        p = jax.nn.softmax(sc, axis=-1)
        return jnp.einsum('bhqs,bshd->bqhd', p.astype(v.dtype), v)
    return map_query_blocks(block, q_nope, q_rope)

def short_conv(x, w):
    ch = x.shape[-1]
    pad = CONV_C // 2
    return lax.conv_general_dilated(x, w[:, None, :].astype(x.dtype), window_strides=(1,), padding=[(pad, pad)], dimension_numbers=('NWC', 'WIO', 'NWC'), feature_group_count=ch)

def gated_delta_chunked(q, k, v, beta, g, s0):
    b, s, h, _ = q.shape
    nc = s // CHUNK_C
    def chunks(t):
        t = t.reshape((b, nc, CHUNK_C, h) + t.shape[3:])
        return jnp.moveaxis(jnp.moveaxis(t, 1, 0), 3, 2)
    q, k, v, beta, g = (chunks(t) for t in (q, k, v, beta, g))
    gc = jnp.cumsum(g, axis=-1)
    strict = jnp.tril(jnp.ones((CHUNK_C, CHUNK_C), dtype=bool), -1)
    incl = jnp.tril(jnp.ones((CHUNK_C, CHUNK_C), dtype=bool))
    diff = gc[..., :, None] - gc[..., None, :]
    dec_strict = jnp.where(strict, jnp.exp(jnp.where(strict, diff, 0.0)), 0.0)
    dec_incl = jnp.where(incl, jnp.exp(jnp.where(incl, diff, 0.0)), 0.0)
    lower = jnp.eye(CHUNK_C, dtype=F32) + beta[..., :, None] * jnp.einsum('...id,...jd->...ij', k, k) * dec_strict
    solve = functools.partial(lax.linalg.triangular_solve, left_side=True, lower=True, unit_diagonal=True)
    u = solve(lower, beta[..., None] * v)
    wk = solve(lower, (beta * jnp.exp(gc))[..., None] * k)
    qk = jnp.einsum('...id,...jd->...ij', q, k) * dec_incl
    q_dec = q * jnp.exp(gc)[..., None]
    k_dec = k * jnp.exp(gc[..., -1:] - gc)[..., None]
    g_last = jnp.exp(gc[..., -1])[..., None, None]
    def step(state, xs):
        u_c, wk_c, qk_c, qd_c, kd_c, gl_c = xs
        w = u_c - wk_c @ state
        o = qd_c @ state + qk_c @ w
        state = gl_c * state + jnp.swapaxes(kd_c, -1, -2) @ w
        return state, o
    s_fin, o = lax.scan(step, s0, (u, wk, qk, q_dec, k_dec, g_last))
    o = jnp.moveaxis(jnp.moveaxis(o, 2, 3), 0, 1).reshape(b, s, h, -1)
    return o, s_fin

def token_mixers(h, p, layer, ctx, rope):
    b, s, _ = h.shape
    proj = h @ p['w_in']
    qa = proj[..., A_Q:A_K].reshape(b, s, H_A, 2, DK_A)
    ka = proj[..., A_K:A_V].reshape(b, s, H_A, 2, DK_A)
    va = proj[..., A_V:B_QC].reshape(b, s, H_A, DV_A)
    q_b = (rms_norm(proj[..., B_QC:B_KVC], p['g_qc']) @ p['w_uq']).reshape(b, s, H_B, NOPE_B + ROPE_B)
    qn_b = q_b[..., :NOPE_B]
    qr_b = q_b[..., NOPE_B:]
    ckv = rms_norm(proj[..., B_KVC:B_KR], p['g_kvc'])
    kr_b = proj[..., B_KR:C_QKV]
    qkv = jax.nn.silu(short_conv(proj[..., C_QKV:C_G], p['conv_c']))
    qc = l2_norm(qkv[..., :W_QK_C].reshape(b, s, H_C, DK_C)) * (DK_C ** -0.5)
    kc = l2_norm(qkv[..., W_QK_C:2 * W_QK_C].reshape(b, s, H_C, DK_C))
    vc = qkv[..., 2 * W_QK_C:].reshape(b, s, H_C, DV_C).astype(F32)
    gate_c = proj[..., C_G:C_BF].reshape(b, s, H_C, DV_C).astype(F32)
    pf = proj[..., C_BF:P_IN].astype(F32)
    beta_f = jax.nn.sigmoid(pf[..., 0:H_C])
    beta_b = jax.nn.sigmoid(pf[..., H_C:2 * H_C])
    g_f = -jnp.exp(p['a_log_f'].astype(F32)) * jax.nn.softplus(pf[..., 2 * H_C:3 * H_C] + p['dt_bias_f'].astype(F32))
    g_b = -jnp.exp(p['a_log_b'].astype(F32)) * jax.nn.softplus(pf[..., 3 * H_C:4 * H_C] + p['dt_bias_b'].astype(F32))
    if rope is not None:
        cos, sin = rope
        qa = apply_rope(qa, cos, sin)
        ka = apply_rope(ka, cos, sin)
        qr_b = apply_rope(qr_b, cos, sin)
        kr_b = apply_rope(kr_b, cos, sin)
    if ctx is None:
        ka_all, va_all, ckv_all, kr_all = ka, va, ckv, kr_b
        s0_f = jnp.zeros((b, H_C, DK_C, DV_C), F32)
        s0_b = jnp.zeros((b, H_C, DK_C, DV_C), F32)
    else:
        c_ak, c_av, c_ckv, c_kr, c_sf, c_sb = ctx
        ka_all = jnp.concatenate([c_ak, ka], axis=1)
        va_all = jnp.concatenate([c_av, va], axis=1)
        ckv_all = jnp.concatenate([c_ckv, ckv], axis=1)
        kr_all = jnp.concatenate([c_kr, kr_b], axis=1)
        s0_f = c_sf.astype(F32)
        s0_b = c_sb.astype(F32)
    lam_init = 0.8 - 0.6 * math.exp(-0.3 * layer)
    lam = (jnp.exp(jnp.sum(p['lam_q1'] * p['lam_k1']).astype(F32))
           - jnp.exp(jnp.sum(p['lam_q2'] * p['lam_k2']).astype(F32)) + lam_init)
    out_a = diff_attention(qa, ka_all, va_all, lam)
    out_a = (rms_norm(out_a, p['g_subln']) * (1.0 - lam_init)).reshape(b, s, W_A)
    kv = (ckv_all @ p['w_ukv']).reshape(b, -1, H_B, NOPE_B + DV_B)
    out_b = mla_attention(qn_b, qr_b, kv[..., :NOPE_B], kr_all, kv[..., NOPE_B:]).reshape(b, s, W_B)
    o_f, s_f = gated_delta_chunked(qc, kc, vc, beta_f, g_f, s0_f)
    o_b, s_b = gated_delta_chunked(jnp.flip(qc, 1), jnp.flip(kc, 1), jnp.flip(vc, 1), jnp.flip(beta_b, 1), jnp.flip(g_b, 1), s0_b)
    o_c = rms_norm(o_f + jnp.flip(o_b, 1), p['g_onorm']) * jax.nn.silu(gate_c)
    out_c = o_c.astype(h.dtype).reshape(b, s, W_C)
    mixed = jnp.concatenate([out_a, out_b, out_c], axis=-1) @ p['w_out']
    if ctx is None:
        return mixed, (ka, va, ckv, kr_b, s_f.astype(h.dtype), s_b.astype(h.dtype))
    return mixed, None

def peer_ffn(h, w_pq, peer_keys, peer_u, peer_v):
    b, s, d = h.shape
    n = b * s
    t = h.reshape(n, d)
    q = (t @ w_pq).reshape(n, PEER_HEADS, 2, PEER_DQ // 2)
    sub = jnp.einsum('nhpd,hpkd->nhpk', q, peer_keys).astype(F32)
    sc, ix = lax.top_k(sub, PEER_TOPK)
    cand = (sc[:, :, 0, :, None] + sc[:, :, 1, None, :]).reshape(n, PEER_HEADS, PEER_TOPK * PEER_TOPK)
    cand_ix = (ix[:, :, 0, :, None] * N_KEYS + ix[:, :, 1, None, :]).reshape(n, PEER_HEADS, PEER_TOPK * PEER_TOPK)
    best, pos = lax.top_k(cand, PEER_TOPK)
    experts = jnp.take_along_axis(cand_ix, pos, axis=-1)
    gates = jax.nn.softmax(best, axis=-1).astype(h.dtype)
    nb = n // PEER_BLOCK
    def block(args):
        tb, eb, gb = args
        act = jax.nn.gelu(jnp.einsum('nd,nhkd->nhk', tb, peer_u[eb]))
        return jnp.einsum('nhk,nhkd->nd', gb * act, peer_v[eb])
    out = lax.map(block, (t.reshape(nb, PEER_BLOCK, d),
                          experts.reshape(nb, PEER_BLOCK, PEER_HEADS, PEER_TOPK),
                          gates.reshape(nb, PEER_BLOCK, PEER_HEADS, PEER_TOPK)))
    return out.reshape(b, s, d)

def trunk_layer(x, cvec, p, layer, ctx, rope):
    sh1, sc1, gt1, sh2, sc2, gt2 = modulation(cvec, p['w_mod'], p['b_mod'])
    h = rms_norm(x, p['g_norm1']) * (1 + sc1) + sh1
    mix, ctx_out = token_mixers(h, p, layer, ctx, rope)
    x = x + gt1 * mix
    h = rms_norm(x, p['g_norm2']) * (1 + sc2) + sh2
    x = x + gt2 * peer_ffn(h, p['w_pq'], p['peer_keys'], p['peer_u'], p['peer_v'])
    return x, ctx_out

def setup_inputs(seed: int = 0) -> dict:
    key = jax.random.key(seed)
    ks = iter(jax.random.split(key, 64))
    def nrm(shape, scale=1.0):
        return jax.random.normal(next(ks), shape, F32) * scale
    def gain(shape):
        return 1.0 + nrm(shape, 0.02)
    def a_log():
        return jnp.log(jax.random.uniform(next(ks), (DEPTH, H_C), F32, 0.5, 4.0))
    def dt_bias():
        dt = jnp.exp(jax.random.uniform(next(ks), (DEPTH, H_C), F32, math.log(1e-3), math.log(1e-1)))
        return dt + jnp.log(-jnp.expm1(-dt))
    L, D = DEPTH, D_MODEL
    return {
        'x_prompt': nrm((BATCH, SEQ, D)),
        'x_sample': nrm((DEC_BATCH, DEC_SEQ, D)),
        'cache_a_k': nrm((DEC_BATCH, L, PAST_LEN, H_A, 2, DK_A)),
        'cache_a_v': nrm((DEC_BATCH, L, PAST_LEN, H_A, DV_A)),
        'cache_b_ckv': nrm((DEC_BATCH, L, PAST_LEN, KV_RANK_B)),
        'cache_b_krope': nrm((DEC_BATCH, L, PAST_LEN, ROPE_B)),
        'state_c_fwd': nrm((DEC_BATCH, L, H_C, DK_C, DV_C), 0.1),
        'state_c_bwd': nrm((DEC_BATCH, L, H_C, DK_C, DV_C), 0.1),
        'c': nrm((DEC_BATCH, D)),
        'c_ctx': nrm((D,)),
        'w_mod': nrm((L, D, 6 * D), 0.5 * D ** -0.5),
        'b_mod': nrm((L, 6 * D), 0.01),
        'g_norm1': gain((L, D)),
        'w_in': nrm((L, D, P_IN), D ** -0.5),
        'lam_q1': nrm((L, DK_A), 0.1),
        'lam_k1': nrm((L, DK_A), 0.1),
        'lam_q2': nrm((L, DK_A), 0.1),
        'lam_k2': nrm((L, DK_A), 0.1),
        'g_subln': gain((L, DV_A)),
        'g_qc': gain((L, Q_RANK_B)),
        'w_uq': nrm((L, Q_RANK_B, H_B * (NOPE_B + ROPE_B)), Q_RANK_B ** -0.5),
        'g_kvc': gain((L, KV_RANK_B)),
        'w_ukv': nrm((L, KV_RANK_B, H_B * (NOPE_B + DV_B)), KV_RANK_B ** -0.5),
        'conv_c': nrm((L, CONV_C, 2 * W_QK_C + W_C), CONV_C ** -0.5),
        'a_log_f': a_log(),
        'a_log_b': a_log(),
        'dt_bias_f': dt_bias(),
        'dt_bias_b': dt_bias(),
        'g_onorm': gain((L, DV_C)),
        'w_out': nrm((L, MIX_W, D), MIX_W ** -0.5),
        'g_norm2': gain((L, D)),
        'w_pq': nrm((L, D, PEER_HEADS * PEER_DQ), D ** -0.5),
        'peer_keys': nrm((L, PEER_HEADS, 2, N_KEYS, PEER_DQ // 2), (PEER_DQ // 2) ** -0.5),
        'peer_u': nrm((L, N_EXPERTS, D), D ** -0.5),
        'peer_v': nrm((L, N_EXPERTS, D), 0.5),
        'g_final': gain((D,)),
    }

def reference(x_prompt, x_sample, cache_a_k, cache_a_v, cache_b_ckv, cache_b_krope, state_c_fwd, state_c_bwd,
              c, c_ctx, w_mod, b_mod, g_norm1, w_in, lam_q1, lam_k1, lam_q2, lam_k2, g_subln, g_qc, w_uq,
              g_kvc, w_ukv, conv_c, a_log_f, a_log_b, dt_bias_f, dt_bias_b, g_onorm, w_out, g_norm2, w_pq,
              peer_keys, peer_u, peer_v, g_final):
    def layer_params(l):
        return {'w_mod': w_mod[l], 'b_mod': b_mod[l], 'g_norm1': g_norm1[l], 'w_in': w_in[l],
                'lam_q1': lam_q1[l], 'lam_k1': lam_k1[l], 'lam_q2': lam_q2[l], 'lam_k2': lam_k2[l],
                'g_subln': g_subln[l], 'g_qc': g_qc[l], 'w_uq': w_uq[l], 'g_kvc': g_kvc[l], 'w_ukv': w_ukv[l],
                'conv_c': conv_c[l], 'a_log_f': a_log_f[l], 'a_log_b': a_log_b[l],
                'dt_bias_f': dt_bias_f[l], 'dt_bias_b': dt_bias_b[l], 'g_onorm': g_onorm[l],
                'w_out': w_out[l], 'g_norm2': g_norm2[l], 'w_pq': w_pq[l], 'peer_keys': peer_keys[l],
                'peer_u': peer_u[l], 'peer_v': peer_v[l]}

    y_p = x_prompt
    ctx_outs = []
    for l in range(DEPTH):
        y_p, co = trunk_layer(y_p, c_ctx[None, :], layer_params(l), l, None, None)
        ctx_outs.append(co)
    y_prompt = rms_norm(y_p, g_final)
    new_a_k = jnp.stack([co[0] for co in ctx_outs], axis=1)
    new_a_v = jnp.stack([co[1] for co in ctx_outs], axis=1)
    new_b_ckv = jnp.stack([co[2] for co in ctx_outs], axis=1)
    new_b_krope = jnp.stack([co[3] for co in ctx_outs], axis=1)
    new_state_fwd = jnp.stack([co[4] for co in ctx_outs], axis=1)
    new_state_bwd = jnp.stack([co[5] for co in ctx_outs], axis=1)

    rope = axial_rope_tables(x_sample.shape[1], ROPE_DIM)
    y_s = x_sample
    for l in range(DEPTH):
        ctx = (cache_a_k[:, l], cache_a_v[:, l], cache_b_ckv[:, l], cache_b_krope[:, l], state_c_fwd[:, l], state_c_bwd[:, l])
        y_s, _ = trunk_layer(y_s, c, layer_params(l), l, ctx, rope)
    y_sample = rms_norm(y_s, g_final)
    return (y_prompt, y_sample, new_a_k, new_a_v, new_b_ckv, new_b_krope, new_state_fwd, new_state_bwd)


_drawn_inputs = setup_inputs


def setup_inputs(seed=0):
    import zlib

    import numpy as np

    out = dict(_drawn_inputs(seed))
    spreads = {}
    factors = {'cache_b_ckv': 4.014,
     'cache_b_krope': 5.734,
     'state_c_fwd': 5.545,
     'state_c_bwd': 4.071,
     'lam_q1': 5.314,
     'lam_k1': 4.687,
     'lam_q2': 3.878,
     'lam_k2': 2.814,
     'g_subln': 6.81,
     'g_qc': 8.0,
     'g_kvc': 2.859,
     'g_onorm': 7.727,
     'g_norm2': 3.246,
     'g_final': 2.942}
    for name, (base, spread) in spreads.items():
        noise = np.random.default_rng([zlib.crc32(name.encode()), seed]).standard_normal(out[name].shape)
        drawn = base * np.exp(spread * noise) if base else spread * noise
        out[name] = jnp.asarray(drawn.astype(out[name].dtype))
    for name, factor in factors.items():
        out[name] = (out[name] * factor).astype(out[name].dtype)
    return out
```

```python
import math
from contextlib import ExitStack

import numpy as np

import concourse.bass as bass
from concourse import mybir

F32 = mybir.dt.float32
U32 = mybir.dt.uint32
ALU = mybir.AluOpType
ACT = mybir.ActivationFunctionType
AX = mybir.AxisListType

P = 128
D, L = 1024, 2
LAYERS = L
KT = D // P
NT = 5
TOK = NT * P
EPS = 1e-6
QA, KA, VA, QC, KVC, KR, GATE, BF, TM = 0, 256, 512, 768, 1024, 1152, 1184, 1440, 1456
TM_CHUNKS = [(0, 512), (512, 1024), (1024, TM)]
FM_CHUNKS = [(0, 512), (512, 768)]
MOD_CHUNKS = 12
WCH = 512
LINE = 644
HA, HB, HC = 4, 8, 4
KEYS = 6 * P
NH, NK, TOPK = 8, 128, 16
SLOTS = NH * TOPK
RING = 8
R_SUB, R_QC, R_KVC, R_ON, R_LAM, R_ALOG, R_DT, R_LI, R_OFF, R_END = 0, 64, 320, 448, 512, 640, 648, 656, 658, 659
V_BMOD, V_G1, V_G2, V_CONV, V_END = 0, 48, 56, 64, 82
NEG = -3.0e38


def kcol(t):
    return 0 if t == 0 else P * (t + 1)


class Chain:

    def __init__(self, eng, sem):
        self.eng, self.sem, self.n = eng, sem, 0

    def mark(self, ins):
        self.n += 1
        ins.then_inc(self.sem, 1)
        return self.n

    def wait(self, n):
        self.eng.wait_ge(self.sem, n)

    def link(self, ins):
        self.wait(self.mark(ins))


class Prog:

    def __init__(self, nc, dram):
        self.nc, self.d = nc, dram
        self.sems = {}
        self.first = None

    def sem(self, name):
        if name not in self.sems:
            self.sems[name] = self.nc.alloc_semaphore(name)
        return self.sems[name]

    def sb(self, ctx, name, shape, dt=F32):
        return ctx.enter_context(self.nc.sbuf_tensor(name, shape, dt))


def bc(ap, axis, n):
    a = ap.unsqueeze(axis)
    shape = list(a.shape)
    shape[axis] = n
    return a.to_broadcast(shape)


def start(p):
    nc, d, sem = p.nc, p.d, p.sem
    with nc.Block() as block:
        @block.sync
        def _(sp):
            sp.dma_start(p.cons[:, :], d["consts"]).then_inc(sem("load_const"), 16)
            sp.dma_start(p.rope[:, :, :, :], d["rope"]).then_inc(sem("load_const"), 16)
            sp.dma_start(p.sc[:, :, :], d["cond"]).then_inc(sem("load_cond"), 16)
            sp.dma_start(p.x[:, 0, :], d["xp"]).then_inc(sem("load_const"), 16)
            sp.dma_start(p.x[:, 1:NT, :], d["xs"]).then_inc(sem("load_const"), 16)
            sp.wait_ge(sem("load_const"), 64)

        @block.scalar
        def _(act):
            act.wait_ge(sem("load_cond"), 16)
            nc.scalar.activation(p.sc[:, :, :], p.sc[:, :, :], ACT.Silu).then_inc(sem("silu_c"), 1)
            act.wait_ge(sem("silu_c"), 1)


def mod_and_project(p, lay):
    nc, d, sem = p.nc, p.d, p.sem
    ps = p.ps
    wsem = [sem(f"load_w{i}") for i in range(3)]
    n_chunks = MOD_CHUNKS + len(TM_CHUNKS) + len(FM_CHUNKS)

    jobs = []
    for c, (a, b) in enumerate(TM_CHUNKS):
        for t in range(NT):
            jobs.append(("tm", MOD_CHUNKS + c, t, a, b))
    for c, (a, b) in enumerate(FM_CHUNKS):
        for blk in range(a // P, b // P):
            for g in range(2):
                jobs.append(("fm", MOD_CHUNKS + len(TM_CHUNKS) + c, g, blk, blk - a // P))

    jobs_until = {job[1]: j + 1 for j, job in enumerate(jobs)}

    def w_arrived(pe, c):
        pe.wait_ge(wsem[c % 3], 16 * (c // 3 + 1))

    with nc.Block() as block:
        @block.sync
        def _(sp):
            sp.dma_start(p.vec[:, :], d["vecs"][bass.ds(lay, 1)].rearrange("a p n -> p (a n)")).then_inc(sem("load_vec"), 16)
            sp.dma_start(p.row[:, :], d["rows"][bass.ds(lay, 1)].to_broadcast([P, R_END])).then_inc(sem("load_row"), 16)
            for c in range(n_chunks):
                if c >= MOD_CHUNKS + 3:
                    sp.wait_ge(sem("proj"), jobs_until[c - 3])
                elif c >= 3:
                    sp.wait_ge(sem("w_used"), c - 2)
                if c < MOD_CHUNKS:
                    src = d["w_mod"][bass.ds(lay, 1), :, :, c * WCH:(c + 1) * WCH]
                    w = WCH
                elif c < MOD_CHUNKS + len(TM_CHUNKS):
                    a, b = TM_CHUNKS[c - MOD_CHUNKS]
                    src = d["w_in_tm"][bass.ds(lay, 1), :, :, a:b]
                    w = b - a
                else:
                    a, b = FM_CHUNKS[c - MOD_CHUNKS - len(TM_CHUNKS)]
                    src = d["w_in_fm"][bass.ds(lay, 1), :, :, a:b]
                    w = b - a
                sp.dma_start(p.wring[:, c % 3, :, 0:w], src.rearrange("a p k n -> p (a k) n")).then_inc(wsem[c % 3], 16)

        @block.scalar
        def _(act):
            for t in range(NT):
                if t >= 1:
                    act.wait_ge(sem("square1"), t)
                nc.scalar.activation(p.junk[:, :], p.x[:, t, :], ACT.Square,
                                     accum_out=p.ss1[:, t:t + 1]).then_inc(sem("square1"), 1)
            act.wait_ge(sem("square1"), NT)
            nc.scalar.activation(p.rt1[:, 0:NT], p.ss1[:, 0:NT], ACT.Sqrt, bias=p.eps[:, 0:1],
                                 scale=1.0 / D).then_inc(sem("root1"), 1)
            for j, (kind, c, i, a, b) in enumerate(jobs):
                if j % 2 == 0:
                    act.wait_ge(sem("proj"), j + 1)
                    dst, src = proj_evac(p, j, kind, i, a, b)
                    nc.scalar.activation(dst, src, ACT.Copy).then_inc(sem("proj_out_act"), 1)

        @block.vector
        def _(dve):
            own = Chain(dve, sem("dve_mod"))
            nc.vector.memset(p.qkvT[:, :, 0:1], 0.0)
            nc.vector.memset(p.qkvT[:, :, 129:131], 0.0)
            nc.vector.memset(p.qkvT[:, :, LINE - 1:LINE], 0.0)
            dve.wait_ge(sem("root1"), 1)
            own.link(nc.vector.reciprocal(p.rt1[:, 0:NT], p.rt1[:, 0:NT]))
            dve.wait_ge(sem("load_vec"), 16)
            dve.wait_ge(sem("w_used"), MOD_CHUNKS)
            own.link(nc.vector.tensor_tensor(p.mod[:, :, :], ps[0][:, 0:96].rearrange("p (n g) -> p n g", g=2),
                                             bc(p.vec[:, V_BMOD:V_BMOD + 48], 2, 2), ALU.add))
            own.mark(nc.vector.scalar_tensor_tensor(out=p.A1[:, :, :], in0=p.mod[:, 8:16, :], scalar=1.0,
                                                    in1=bc(p.vec[:, V_G1:V_G1 + 8], 2, 2), op0=ALU.add, op1=ALU.mult))
            own.link(nc.vector.scalar_tensor_tensor(out=p.A2[:, :, :], in0=p.mod[:, 32:40, :], scalar=1.0,
                                                    in1=bc(p.vec[:, V_G2:V_G2 + 8], 2, 2), op0=ALU.add, op1=ALU.mult))

            def scaled(t):
                if t >= 2:
                    dve.wait_ge(sem("turned1"), t - 1)
                nc.vector.tensor_scalar(p.xn[:, t % 2, :], p.x[:, t, :], p.rt1[:, t:t + 1], None,
                                        ALU.mult).then_inc(sem("scaled1"), 1)

            scaled(0)
            for t in range(NT):
                if t + 1 < NT:
                    scaled(t + 1)
                dve.wait_ge(sem("turned1"), t + 1)
                g = 0 if t == 0 else 1
                for k in range(KT):
                    nc.vector.tensor_scalar(p.hT[:, k, t * P:(t + 1) * P],
                                            ps[1 + 2 * (t % 2) + k // 4][:, (k % 4) * P:(k % 4 + 1) * P],
                                            p.A1[:, k, g:g + 1], p.mod[:, k, g:g + 1],
                                            ALU.mult, ALU.add).then_inc(sem("h_ready"), 1)
            for j, (kind, c, i, a, b) in enumerate(jobs):
                if j % 2 == 1:
                    dve.wait_ge(sem("proj"), j + 1)
                    dst, src = proj_evac(p, j, kind, i, a, b)
                    nc.vector.tensor_copy(dst, src).then_inc(sem("proj_out_dve"), 1)

        @block.tensor
        def _(pe):
            for c in range(MOD_CHUNKS):
                w_arrived(pe, c)
                for b in range(4):
                    col = 2 * (4 * c + b)
                    for k in range(KT):
                        last = nc.tensor.matmul(ps[0][:, col:col + 2], p.wring[:, c % 3, k, b * P:(b + 1) * P],
                                                p.sc[:, k, :], start=(k == 0), stop=(k == KT - 1))
                last.then_inc(sem("w_used"), 1)
            for t in range(NT):
                pe.wait_ge(sem("scaled1"), t + 1)
                if t >= 2:
                    pe.wait_ge(sem("h_ready"), KT * (t - 1))
                for k in range(KT):
                    last = nc.tensor.transpose(ps[1 + 2 * (t % 2) + k // 4][:, (k % 4) * P:(k % 4 + 1) * P],
                                               p.xn[:, t % 2, k * P:(k + 1) * P], p.ident)
                last.then_inc(sem("turned1"), 1)
            chunk = -1
            for j, (kind, c, i, a, b) in enumerate(jobs):
                if c != chunk:
                    w_arrived(pe, c)
                    chunk = c
                if j == 0:
                    pe.wait_ge(sem("h_ready"), KT * NT)
                if j >= 8:
                    pe.wait_ge(sem("proj_out_act" if j % 2 == 0 else "proj_out_dve"), (j - 8) // 2 + 1)
                bank = ps[j % 8]
                for k in range(KT):
                    if kind == "tm":
                        last = nc.tensor.matmul(bank[:, 0:b - a], p.hT[:, k, i * P:(i + 1) * P],
                                                p.wring[:, c % 3, k, 0:b - a], start=(k == 0), stop=(k == KT - 1))
                    else:
                        lo, hi = (0, P) if i == 0 else (P, TOK)
                        last = nc.tensor.matmul(bank[:, 0:hi - lo], p.wring[:, c % 3, k, b * P:(b + 1) * P],
                                                p.hT[:, k, lo:hi], start=(k == 0), stop=(k == KT - 1))
                last.then_inc(sem("proj"), 1)


def proj_evac(p, j, kind, i, a, b):
    bank = p.ps[j % 8]
    if kind == "tm":
        return p.proj[:, i, a:b], bank[:, 0:b - a]
    if i == 0:
        return p.qkvT[:, a, 1:1 + P], bank[:, 0:P]
    return p.qkvT[:, a, 131:131 + 4 * P], bank[:, :]


def conv(p):
    nc, sem, ps = p.nc, p.sem, p.ps
    with nc.Block() as block:
        @block.vector
        def _(dve):
            own = Chain(dve, sem("dve_conv"))
            for pair in range(3):
                for tap in range(3):
                    for b in (2 * pair, 2 * pair + 1):
                        w = p.vec[:, V_CONV + 3 * b + tap:V_CONV + 3 * b + tap + 1]
                        x = p.qkvT[:, b, tap:tap + LINE - 2]
                        if tap == 0:
                            n = own.mark(nc.vector.tensor_scalar(p.convd[:, b, :], x, w, None, ALU.mult))
                        else:
                            own.wait(6 * pair + 2 * tap - 1 + b % 2)
                            n = own.mark(nc.vector.scalar_tensor_tensor(
                                out=p.convd[:, b, :], in0=x, scalar=w, in1=p.convd[:, b, :],
                                op0=ALU.mult, op1=ALU.add))

        @block.scalar
        def _(act):
            for b in range(6):
                act.wait_ge(sem("dve_conv"), 6 * (b // 2) + 5 + b % 2)
                nc.scalar.activation(p.convd[:, b, :], p.convd[:, b, :], ACT.Silu).then_inc(sem("conv_silu"), 1)
            nc.scalar.activation(p.proj[:, :, GATE:BF], p.proj[:, :, GATE:BF], ACT.Silu).then_inc(sem("gate_silu"), 1)
            act.wait_ge(sem("gate_silu"), 1)
            for t in range(NT):
                for h, (a, b) in enumerate(((0, 512), (512, 768))):
                    act.wait_ge(sem("conv_turned"), 2 * t + h + 1)
                    nc.scalar.activation(p.qkv[:, t, a:b], ps[(2 * t + h) % 8][:, 0:b - a],
                                         ACT.Copy).then_inc(sem("qkv_out"), 1)

        @block.tensor
        def _(pe):
            for t in range(NT):
                lo = 0 if t == 0 else 130 + P * (t - 1)
                for h, (a, b) in enumerate(((0, 4), (4, 6))):
                    j = 2 * t + h
                    pe.wait_ge(sem("conv_silu"), b)
                    if j >= 8:
                        pe.wait_ge(sem("qkv_out"), j - 7)
                    for k in range(a, b):
                        last = nc.tensor.transpose(ps[j % 8][:, (k - a) * P:(k - a + 1) * P],
                                                   p.convd[:, k, lo:lo + P], p.ident)
                    last.then_inc(sem("conv_turned"), 1)


def delta(p, lay):
    nc, sem, ps = p.nc, p.sem, p.ps
    steps = [(0, 0)] + [(t, NT - t) for t in range(1, NT)]
    S4 = [P, HC, P]

    def tile_of(s, d):
        return steps[s][d]

    def heads(ap, n=HC):
        return ap.rearrange("p (h n) -> p h n", h=n)

    with nc.Block() as block:
        @block.sync
        def _(sp):
            sp.wait_ge(sem("states_zero"), 1)
            sp.wait_ge(sem("step0"), 1)
            sp.wait_ge(sem("step1"), 1)
            for d, name in enumerate(("sf", "sb")):
                sp.dma_start(p.d["out_" + name][bass.ds(lay, 1)].rearrange("l h d v -> d (l h) v"),
                             p.state[:, d, :, :]).then_inc(sem("store"), 16)
            sp.wait_ge(sem("store"), 32)
            for d, name in enumerate(("sf", "sb")):
                sp.dma_start(p.state[:, d, :, :],
                             p.d["in_" + name][bass.ds(lay, 1)].rearrange("l h d v -> d (l h) v")).then_inc(sem("load_state"), 16)

        @block.gpsimd
        def _(pool):
            nc.gpsimd.memset(p.state[:, :, :, :], 0.0).then_inc(sem("states_zero"), 1)
            for s in range(NT):
                for lvl in range(7):
                    for d in range(2):
                        pool.wait_ge(sem(f"lt_ready{d}"), s + 1)
                        n = 7 * s + lvl
                        if n >= 2:
                            pool.wait_ge(sem(f"t1{d}"), n - 1)
                        nc.gpsimd.tensor_tensor(p.mlt[:, d, lvl_buf(n), :, :], p.lt[:, d, :, :],
                                                bc(p.lmask[:, d, lvl, :], 1, HC), ALU.mult).then_inc(sem(f"mlt{d}"), 1)

        @block.scalar
        def _(act):
            act.wait_ge(sem("squares_d"), NT)
            nc.scalar.activation(p.rd[:, :, :], p.ssd[:, :, :], ACT.Sqrt, bias=p.eps[:, 0:1]).then_inc(sem("root_d"), 1)
            act.wait_ge(sem("zabs"), 1)
            nc.scalar.activation(p.sp1[:, :, :], p.zab[:, :, :], ACT.Exp, scale=-1.0).then_inc(sem("exp_small"), 1)
            nc.scalar.activation(p.bet[:, :, :], p.proj[:, :, BF:BF + 8], ACT.Exp, scale=-1.0).then_inc(sem("exp_small"), 1)
            nc.scalar.activation(p.eal[:, :], p.row[:, R_ALOG:R_ALOG + 8], ACT.Exp).then_inc(sem("exp_small"), 1)
            act.wait_ge(sem("exp_small"), 3)
            nc.scalar.activation(p.sp1[:, :, :], p.sp1[:, :, :], ACT.Ln, bias=p.one[:, 0:1]).then_inc(sem("ln_small"), 1)
            act.wait_ge(sem("gcol_out"), 1)
            nc.scalar.activation(p.egc[:, :, :], p.gcol[:, :, :], ACT.Exp).then_inc(sem("egc"), 1)
            for s in range(NT):
                for d in range(2):
                    act.wait_ge(sem(f"kq_turned{d}"), s + 1)
                    if s >= 1:
                        act.wait_ge(sem(f"kk{d}"), s)
                    nc.scalar.activation(p.kT[:, d, :], ps[4 * d + 2][0:64, :], ACT.Copy).then_inc(sem(f"kqT{d}"), 1)
                    nc.scalar.activation(p.qT[:, d, :], ps[4 * d + 3][0:64, :], ACT.Copy).then_inc(sem(f"kqT{d}"), 1)
                for d in range(2):
                    act.wait_ge(sem(f"diff{d}"), s + 1)
                    if s >= 1:
                        act.wait_ge(sem(f"prep{d}"), 5 * s)
                    nc.scalar.activation(p.dec[:, d, :, :], p.dif[:, d, :, :], ACT.Exp).then_inc(sem(f"dec{d}"), 1)
                    if s >= 1:
                        act.wait_ge(sem(f"step{d}"), s)
                    nc.scalar.activation(p.egr[:, d, :, :], heads(ps[4 * d][0:64, :]), ACT.Exp).then_inc(sem(f"egr{d}"), 1)
                for lvl in range(7):
                    for d in range(2):
                        n = 7 * s + lvl
                        act.wait_ge(sem(f"t1{d}"), n + 1)
                        if n >= 1:
                            act.wait_ge(sem(f"t2{d}"), n)
                        nc.scalar.activation(p.t1s[:, d, :], ps[4 * d][:, :], ACT.Copy).then_inc(sem(f"t1s{d}"), 1)
                for d in range(2):
                    act.wait_ge(sem(f"wk{d}"), s + 1)
                    nc.scalar.activation(p.nwk[:, d, :], ps[4 * d + 2][0:64, :], ACT.Copy, scale=-1.0).then_inc(sem(f"nwk{d}"), 1)
            act.wait_ge(sem("squares_o"), NT)
            nc.scalar.activation(p.sso[:, :, :], p.sso[:, :, :], ACT.Sqrt, bias=p.eps[:, 0:1],
                                 scale=1.0 / 64).then_inc(sem("root_o"), 1)

        @block.vector
        def _(dve):
            own = Chain(dve, sem("dve_delta"))
            nc.vector.memset(p.oC[:, :, :], 0.0)
            for t in range(NT):
                if t >= 1:
                    dve.wait_ge(sem("squares_d"), t)
                own.link(nc.vector.tensor_tensor(p.junk[:, 0:512], p.qkv[:, t, 0:512], p.qkv[:, t, 0:512], ALU.mult))
                nc.vector.tensor_reduce(p.ssd[:, t, :], heads(p.junk[:, 0:512], 8), AX.X, ALU.add).then_inc(sem("squares_d"), 1)
            own.link(nc.vector.tensor_tensor(p.zz[:, :, :], p.proj[:, :, BF + 8:BF + 16],
                                             bc(p.row[:, R_DT:R_DT + 8], 1, NT), ALU.add))
            nc.vector.scalar_tensor_tensor(out=p.zab[:, :, :], in0=p.zz[:, :, :], scalar=-1.0, in1=p.zz[:, :, :],
                                           op0=ALU.mult, op1=ALU.max).then_inc(sem("zabs"), 1)
            dve.wait_ge(sem("root_d"), 1)
            own.link(nc.vector.reciprocal(p.rd[:, :, :], p.rd[:, :, :]))
            own.link(nc.vector.tensor_scalar(p.rd[:, :, 0:4], p.rd[:, :, 0:4], 0.125, None, ALU.mult))
            for t in range(NT):
                nc.vector.tensor_tensor(heads(p.qkv[:, t, 0:512], 8), heads(p.qkv[:, t, 0:512], 8),
                                        bc(p.rd[:, t, :], 2, 64), ALU.mult).then_inc(sem("qk_unit"), 1)
            dve.wait_ge(sem("exp_small"), 3)
            own.link(nc.vector.tensor_scalar(p.bet[:, :, :], p.bet[:, :, :], 1.0, None, ALU.add))
            own.link(nc.vector.reciprocal(p.bet[:, :, :], p.bet[:, :, :]))
            dve.wait_ge(sem("ln_small"), 1)
            own.link(nc.vector.scalar_tensor_tensor(out=p.g[:, :, :], in0=p.zz[:, :, :], scalar=0.0, in1=p.sp1[:, :, :],
                                                    op0=ALU.max, op1=ALU.add))
            nc.vector.scalar_tensor_tensor(out=p.g[:, :, :], in0=p.g[:, :, :], scalar=-1.0, in1=bc(p.eal[:, :], 1, NT),
                                           op0=ALU.mult, op1=ALU.mult).then_inc(sem("g_ready"), 1)
            dve.wait_ge(sem("gcol"), 1)
            nc.vector.tensor_copy(p.gcol[:, :, :], ps[0][:, 0:NT * 8].rearrange("p (t c) -> p t c", t=NT)).then_inc(sem("gcol_out"), 1)
            dve.wait_ge(sem("egc"), 1)
            own.link(nc.vector.tensor_tensor(p.begc[:, :, :], p.bet[:, :, :], p.egc[:, :, :], ALU.mult))
            for s in range(NT):
                for d in range(2):
                    t, c = tile_of(s, d), 4 * d
                    last = P - 1 if d == 0 else 0
                    kh = heads(p.qkv[:, t, 256:512])
                    dve.wait_ge(sem(f"rows{d}"), s + 1)
                    own.link(nc.vector.tensor_tensor(p.dif[:, d, :, :], heads(ps[4 * d][:, :]),
                                                     bc(p.gcol[:, t, c:c + 4], 2, P), ALU.subtract))
                    nc.vector.tensor_scalar(p.dif[:, d, :, :], p.dif[:, d, :, :], 0.0, None, ALU.min).then_inc(sem(f"diff{d}"), 1)
                    if s >= 1:
                        dve.wait_ge(sem(f"wk{d}"), s)
                        dve.wait_ge(sem(f"step{d}"), s)
                    nc.vector.tensor_tensor(p.rv[:, d, :, :], heads(p.qkv[:, t, 512:768]),
                                            bc(p.bet[:, t, c:c + 4], 2, 64), ALU.mult).then_inc(sem(f"prep{d}"), 1)
                    nc.vector.tensor_tensor(p.rk[:, d, :, :], kh,
                                            bc(p.begc[:, t, c:c + 4], 2, 64), ALU.mult).then_inc(sem(f"prep{d}"), 1)
                for d in range(2):
                    t, c = tile_of(s, d), 4 * d
                    last = P - 1 if d == 0 else 0
                    kh = heads(p.qkv[:, t, 256:512])
                    dve.wait_ge(sem(f"dec{d}"), s + 1)
                    own.link(nc.vector.tensor_tensor(p.kd[:, d, :, :], kh,
                                                         p.dec[:, d, :, last:last + 1].to_broadcast([P, HC, 64]), ALU.mult))
                    own.link(nc.vector.tensor_tensor(p.dec[:, d, :, :], p.dec[:, d, :, :], bc(p.imask[:, d, :], 1, HC), ALU.mult))
                    dve.wait_ge(sem(f"kk{d}"), s + 1)
                    own.link(nc.vector.tensor_tensor(p.lt[:, d, :, :], heads(ps[4 * d + 2][:, :]), p.dec[:, d, :, :], ALU.mult))
                    nc.vector.tensor_tensor(p.lt[:, d, :, :], heads(ps[4 * d + 1][:, :]), p.lt[:, d, :, :], ALU.mult).then_inc(sem(f"lt_ready{d}"), 1)
                    nc.vector.tensor_tensor(p.qk[:, d, :, :], heads(ps[4 * d + 3][:, :]), p.dec[:, d, :, :], ALU.mult).then_inc(sem(f"prep{d}"), 1)
                    dve.wait_ge(sem(f"egr{d}"), s + 1)
                    dve.wait_ge(sem(f"kqT{d}"), 2 * s + 2)
                    nc.vector.tensor_tensor(p.qd[:, d, :, :], heads(p.qT[:, d, :]), p.egr[:, d, :, :], ALU.mult).then_inc(sem(f"prep{d}"), 1)
                    nc.vector.tensor_copy(p.X[:, d, :, :], bc(p.ident, 1, HC)).then_inc(sem(f"prep{d}"), 1)
                    nc.vector.tensor_copy(p.XT[:, d, :, :], bc(p.ident, 1, HC)).then_inc(sem(f"x{d}"), 1)
                for lvl in range(7):
                    for d in range(2):
                        n = 7 * s + lvl
                        dve.wait_ge(sem(f"t2{d}"), n + 1)
                        if lvl < 6:
                            nc.vector.tensor_tensor(p.X[:, d, :, :], p.X[:, d, :, :], heads(ps[4 * d][:, :]), ALU.subtract).then_inc(sem(f"x{d}"), 1)
                        nc.vector.tensor_tensor(p.XT[:, d, :, :], p.XT[:, d, :, :], heads(ps[4 * d + 1][:, :]), ALU.subtract).then_inc(sem(f"x{d}"), 1)
                for d in range(2):
                    t = tile_of(s, d)
                    last = P - 1 if d == 0 else 0
                    dve.wait_ge(sem(f"w{d}"), s + 1)
                    nc.vector.tensor_copy(p.w[:, d, :, :], heads(ps[4 * d + 1][:, 0:256])).then_inc(sem(f"w_out{d}"), 1)
                    dve.wait_ge(sem(f"od{d}"), s + 1)
                    own.link(nc.vector.tensor_tensor(p.oC[:, t, :], p.oC[:, t, :], ps[4 * d + 1][:, 256:512], ALU.add))
                    own.link(nc.vector.tensor_tensor(p.state[:, d, :, :], p.state[:, d, :, :],
                                                     p.egr[:, d, :, last:last + 1].to_broadcast([64, HC, 64]), ALU.mult))
                    nc.vector.tensor_tensor(p.state[:, d, :, :], p.state[:, d, :, :], heads(ps[4 * d + 2][0:64, 0:256]),
                                            ALU.add).then_inc(sem(f"step{d}"), 1)
                if s == 0:
                    dve.wait_ge(sem("load_state"), 32)
            own.wait(own.n)
            sq = p.junk[:, 0:256].rearrange("p (h n) -> p h n", h=4)
            for t in range(NT):
                if t >= 1:
                    dve.wait_ge(sem("squares_o"), t)
                own.link(nc.vector.tensor_tensor(p.junk[:, 0:256], p.oC[:, t, :], p.oC[:, t, :], ALU.mult))
                nc.vector.tensor_reduce(p.sso[:, t, :], sq, AX.X, ALU.add).then_inc(sem("squares_o"), 1)
            dve.wait_ge(sem("root_o"), 1)
            own.link(nc.vector.reciprocal(p.sso[:, :, :], p.sso[:, :, :]))
            for t in range(NT):
                o = heads(p.oC[:, t, :])
                own.link(nc.vector.tensor_tensor(o, o, bc(p.sso[:, t, :], 2, 64), ALU.mult))
                own.link(nc.vector.tensor_tensor(o, o, bc(p.row[:, R_ON:R_ON + 64], 1, HC), ALU.mult))
                own.mark(nc.vector.tensor_tensor(p.mixed[:, t, 768:1024], p.oC[:, t, :], p.proj[:, t, GATE:BF], ALU.mult))

        @block.tensor
        def _(pe):
            pe.wait_ge(sem("g_ready"), 1)
            for t in range(NT):
                for d in range(2):
                    last = nc.tensor.matmul(ps[0][:, 8 * t + 4 * d:8 * t + 4 * d + 4], p.imask[:, d, :],
                                            p.g[:, t, 4 * d:4 * d + 4], start=True, stop=True)
            last.then_inc(sem("gcol"), 1)
            pe.wait_ge(sem("gcol_out"), 1)
            pe.wait_ge(sem("qk_unit"), NT)
            for s in range(NT):
                for d in range(2):
                    t = tile_of(s, d)
                    B = ps[4 * d:4 * d + 4]
                    if s >= 1:
                        pe.wait_ge(sem(f"step{d}"), s)
                    for h in range(HC):
                        nc.tensor.transpose(B[2][0:64, h * P:(h + 1) * P], p.qkv[:, t, 256 + 64 * h:320 + 64 * h], p.ident)
                    for h in range(HC):
                        mm = nc.tensor.transpose(B[3][0:64, h * P:(h + 1) * P], p.qkv[:, t, 64 * h:64 * h + 64], p.ident)
                    mm.then_inc(sem(f"kq_turned{d}"), 1)
                    for h in range(HC):
                        nc.tensor.matmul(B[0][:, h * P:(h + 1) * P], p.g[:, t, 4 * d + h:4 * d + h + 1].to_broadcast([P, P]),
                                         p.imask[:, d, :], start=True, stop=True)
                    for h in range(HC):
                        mm = nc.tensor.matmul(B[1][:, h * P:(h + 1) * P], p.bet[:, t, 4 * d + h:4 * d + h + 1].to_broadcast([P, P]),
                                              p.ident, start=True, stop=True)
                    mm.then_inc(sem(f"rows{d}"), 1)
                for d in range(2):
                    B = ps[4 * d:4 * d + 4]
                    pe.wait_ge(sem(f"kqT{d}"), 2 * s + 2)
                    for h in range(HC):
                        k = p.kT[:, d, h * P:(h + 1) * P]
                        nc.tensor.matmul(B[2][:, h * P:(h + 1) * P], k, k, start=True, stop=True)
                    for h in range(HC):
                        mm = nc.tensor.matmul(B[3][:, h * P:(h + 1) * P], p.kT[:, d, h * P:(h + 1) * P],
                                              p.qT[:, d, h * P:(h + 1) * P], start=True, stop=True)
                    mm.then_inc(sem(f"kk{d}"), 1)
                for lvl in range(7):
                    for d in range(2):
                        B = ps[4 * d:4 * d + 4]
                        n = 7 * s + lvl
                        pe.wait_ge(sem(f"mlt{d}"), n + 1)
                        pe.wait_ge(sem(f"x{d}"), 14 * s + 1 + 2 * lvl)
                        if lvl == 0:
                            pe.wait_ge(sem(f"egr{d}"), s + 1)
                            pe.wait_ge(sem(f"prep{d}"), 5 * s + 5)
                        for h in range(HC):
                            mm = nc.tensor.matmul(B[0][:, h * P:(h + 1) * P], p.mlt[:, d, lvl_buf(n), h, :],
                                                  p.X[:, d, h, :], start=True, stop=True)
                        mm.then_inc(sem(f"t1{d}"), 1)
                    for d in range(2):
                        B = ps[4 * d:4 * d + 4]
                        n = 7 * s + lvl
                        pe.wait_ge(sem(f"t1s{d}"), n + 1)
                        if lvl < 6:
                            for h in range(HC):
                                nc.tensor.matmul(B[0][:, h * P:(h + 1) * P], p.XT[:, d, h, :],
                                                 p.t1s[:, d, h * P:(h + 1) * P], start=True, stop=True)
                        for h in range(HC):
                            mm = nc.tensor.matmul(B[1][:, h * P:(h + 1) * P], p.t1s[:, d, h * P:(h + 1) * P],
                                                  p.XT[:, d, h, :], start=True, stop=True)
                        mm.then_inc(sem(f"t2{d}"), 1)
                for d in range(2):
                    B = ps[4 * d:4 * d + 4]
                    pe.wait_ge(sem(f"x{d}"), 14 * (s + 1))
                    for h in range(HC):
                        mm = nc.tensor.matmul(B[2][0:64, h * P:(h + 1) * P], p.rk[:, d, h, :], p.XT[:, d, h, :],
                                              start=True, stop=True)
                    mm.then_inc(sem(f"wk{d}"), 1)
                if s == 1:
                    pe.wait_ge(sem("load_state"), 32)
                if s == 0:
                    pe.wait_ge(sem("states_zero"), 1)
                for d in range(2):
                    B = ps[4 * d:4 * d + 4]
                    pe.wait_ge(sem(f"nwk{d}"), s + 1)
                    for h in range(HC):
                        nc.tensor.matmul(B[1][:, h * 64:h * 64 + 64], p.XT[:, d, h, :], p.rv[:, d, h, :], start=True, stop=False)
                        mm = nc.tensor.matmul(B[1][:, h * 64:h * 64 + 64], p.nwk[:, d, h * P:(h + 1) * P],
                                              p.state[:, d, h, :], start=False, stop=True)
                    mm.then_inc(sem(f"w{d}"), 1)
                for d in range(2):
                    B = ps[4 * d:4 * d + 4]
                    pe.wait_ge(sem(f"w_out{d}"), s + 1)
                    for h in range(HC):
                        o = B[1][:, 256 + h * 64:320 + h * 64]
                        nc.tensor.matmul(o, p.qd[:, d, h, :], p.state[:, d, h, :], start=True, stop=False)
                        nc.tensor.matmul(o, p.qk[:, d, h, :], p.w[:, d, h, :], start=False, stop=True)
                    for h in range(HC):
                        mm = nc.tensor.matmul(B[2][0:64, h * 64:h * 64 + 64], p.kd[:, d, h, :], p.w[:, d, h, :],
                                              start=True, stop=True)
                    mm.then_inc(sem(f"od{d}"), 1)


def lvl_buf(n):
    return n % 2


def prepare_attention(p, lay):
    nc, d, sem, ps = p.nc, p.d, p.sem, p.ps

    def rope(own, dve, x, n, t):
        cos, sin = p.rope[:, 0, t - 1, :], p.rope[:, 1, t - 1, :]
        u = p.ru[:, 0:n * 32].rearrange("p (n c) -> p n c", c=32)
        v = p.rv2[:, 0:n * 32].rearrange("p (n c) -> p n c", c=32)
        for half in range(2):
            for q in range(2):
                a, b = 16 * half + 8 * q, 16 * half + 8 * (1 - q)
                own.mark(nc.vector.tensor_tensor(u[:, :, a:a + 8], x[:, :, b:b + 8], bc(sin[:, a:a + 8], 1, n), ALU.mult))
        own.link(nc.vector.tensor_tensor(v, x, bc(cos, 1, n), ALU.mult))
        return nc.vector.tensor_tensor(x, u, v, ALU.add)

    jobs = []
    for t in range(NT):
        jobs += [("qk", t, 0), ("low", t, 0)]
    jobs += [("qk", NT, 0), ("low", NT, 0)]
    for h in range(HB):
        jobs += [("kn", h, 0), ("kn", h, 1)]
    jobs += [("v", t, 0) for t in range(6)]
    for t in range(NT):
        jobs += [("uq", t, 0), ("uq", t, 1), ]
        if t >= 1:
            jobs += [("qt", t - 1, 0), ("qt", t - 1, 1)]
    jobs += [("qt", NT - 1, 0), ("qt", NT - 1, 1)]
    at = {job: j for j, job in enumerate(jobs)}

    with nc.Block() as block:
        @block.sync
        def _(sp):
            one = bass.ds(lay, 1)
            sp.dma_start(p.cak[:, :], d["cache_a_k"][one].rearrange("l p n -> p (l n)")).then_inc(sem("load_cache"), 16)
            sp.dma_start(p.cav[:, :], d["cache_a_v"][one].rearrange("l p n -> p (l n)")).then_inc(sem("load_cache"), 16)
            sp.dma_start(p.cckv[:, :], d["cache_ckv"][one].rearrange("l p n -> p (l n)")).then_inc(sem("load_cache"), 16)
            sp.dma_start(p.ckr[:, 64:96], d["cache_kr"][one].rearrange("l p n -> p (l n)")).then_inc(sem("load_cache"), 16)
            sp.dma_start(p.wuq[:, :, :], d["w_uq"][one].rearrange("l p k n -> p (l k) n")).then_inc(sem("load_wuq"), 16)
            sp.dma_start(p.wukn[:, :], d["w_ukn"][one].rearrange("l p n -> p (l n)")).then_inc(sem("load_wuk"), 16)
            sp.dma_start(p.wukv[:, :], d["w_ukv"][one].rearrange("l p n -> p (l n)")).then_inc(sem("load_wuk"), 16)
            sp.dma_start(d["out_ak"][one].rearrange("l p n -> p (l n)"), p.proj[:, 0, KA:VA]).then_inc(sem("store_ctx"), 16)
            sp.dma_start(d["out_av"][one].rearrange("l p n -> p (l n)"), p.proj[:, 0, VA:QC]).then_inc(sem("store_ctx"), 16)
            sp.wait_ge(sem("low_norm"), 1)
            sp.dma_start(d["out_ckv"][one].rearrange("l p n -> p (l n)"), p.proj[:, 0, KVC:KR]).then_inc(sem("store_ctx"), 16)
            sp.dma_start(d["out_kr"][one].rearrange("l p n -> p (l n)"), p.proj[:, 0, KR:GATE]).then_inc(sem("store_ctx"), 16)
            sp.wait_ge(sem("store_ctx"), 64)

        @block.gpsimd
        def _(pool):
            nc.gpsimd.memset(p.krp[:, :, 0:64], 0.0).then_inc(sem("pads"), 1)
            nc.gpsimd.memset(p.ckr[:, 0:64], 0.0).then_inc(sem("pads"), 1)

        @block.scalar
        def _(act):
            act.wait_ge(sem("squares_l"), 2 * NT)
            nc.scalar.activation(p.rl[:, 0, :], p.ssl[:, 0, :], ACT.Sqrt, bias=p.eps[:, 0:1], scale=1.0 / 256).then_inc(sem("root_l"), 1)
            nc.scalar.activation(p.rl[:, 1, :], p.ssl[:, 1, :], ACT.Sqrt, bias=p.eps[:, 0:1], scale=1.0 / 128).then_inc(sem("root_l"), 1)
            for j, (kind, t, half) in enumerate(jobs):
                b = ps[j % 8]
                act.wait_ge(sem("p_mm"), j + 1)
                tc, kc = (t * P, kcol(t) if t < NT else P)
                if kind == "qk":
                    if t < NT:
                        nc.scalar.activation(p.qTa[:, :, tc:tc + P], b[:, 0:256].rearrange("p (b n) -> p b n", b=2), ACT.Copy)
                    last = nc.scalar.activation(p.kTa[:, :, kc:kc + P], b[:, 256:512].rearrange("p (b n) -> p b n", b=2), ACT.Copy)
                elif kind == "low":
                    if t < NT:
                        nc.scalar.activation(p.qcT[:, :, tc:tc + P], b[:, 0:256].rearrange("p (b n) -> p b n", b=2), ACT.Copy)
                    nc.scalar.activation(p.ckvT[:, kc:kc + P], b[:, 256:384], ACT.Copy)
                    last = nc.scalar.activation(p.kTb[64:96, :, kc:kc + P], bc(b[64:96, 384:512], 1, HB), ACT.Copy)
                elif kind == "kn":
                    lo, hi = (0, 512) if half == 0 else (512, KEYS)
                    last = nc.scalar.activation(p.kTb[0:64, t, lo:hi], b[0:64, 0:hi - lo], ACT.Copy)
                elif kind == "v":
                    last = nc.scalar.activation(p.vb[:, t, :], b[:, :], ACT.Copy)
                elif kind == "uq":
                    if t >= 2:
                        act.wait_ge(sem("p_mm"), at[("qt", t - 2, 1)] + 1)
                    last = nc.scalar.activation(p.qb[:, t % 2, half * 384:half * 384 + 384], b[:, 0:384], ACT.Copy)
                else:
                    last = nc.scalar.activation(p.qTb[:, 4 * half:4 * half + 4, tc:tc + P],
                                                b[0:96, :].rearrange("p (h n) -> p h n", h=4), ACT.Copy)
                last.then_inc(sem("p_ev"), 1)

        @block.vector
        def _(dve):
            own = Chain(dve, sem("dve_prep"))
            for t in range(NT):
                if t >= 1:
                    dve.wait_ge(sem("squares_l"), 2 * t)
                for i, (a, b) in enumerate(((QC, KVC), (KVC, KR))):
                    nc.vector.tensor_tensor_reduce(out=p.junk[:, 256 * i:256 * i + b - a], in0=p.proj[:, t, a:b], in1=p.proj[:, t, a:b],
                                                   scale=1.0, scalar=0.0, op0=ALU.mult, op1=ALU.add,
                                                   accum_out=p.ssl[:, i, t:t + 1]).then_inc(sem("squares_l"), 1)
            for i in range(2):
                q1 = R_LAM + 64 * i
                nc.vector.tensor_tensor_reduce(out=p.junk[:, 512 + 32 * i:544 + 32 * i], in0=p.row[:, q1:q1 + 32], in1=p.row[:, q1 + 32:q1 + 64],
                                               scale=1.0, scalar=0.0, op0=ALU.mult, op1=ALU.add,
                                               accum_out=p.lam[:, i:i + 1]).then_inc(sem("lam_dot"), 1)
            dve.wait_ge(sem("root_l"), 2)
            own.link(nc.vector.reciprocal(p.rl[:, :, :], p.rl[:, :, :]))
            for t in range(NT):
                nc.vector.scalar_tensor_tensor(out=p.proj[:, t, KVC:KR], in0=p.proj[:, t, KVC:KR], scalar=p.rl[:, 1, t:t + 1],
                                               in1=p.row[:, R_KVC:R_KVC + 128], op0=ALU.mult, op1=ALU.mult).then_inc(sem("low_norm"), 1)
                nc.vector.scalar_tensor_tensor(out=p.proj[:, t, QC:KVC], in0=p.proj[:, t, QC:KVC], scalar=p.rl[:, 0, t:t + 1],
                                               in1=p.row[:, R_QC:R_QC + 256], op0=ALU.mult, op1=ALU.mult).then_inc(sem("low_norm"), 1)
                if t == 0:
                    dve.wait_ge(sem("pads"), 2)
                else:
                    own.wait(own.n)
                    own.link(rope(own, dve, p.proj[:, t, QA:VA].rearrange("p (n c) -> p n c", c=32), 16, t))
                    own.link(rope(own, dve, p.proj[:, t, KR:GATE].rearrange("p (n c) -> p n c", c=32), 1, t))
                nc.vector.tensor_copy(p.krp[:, t, 64:96], p.proj[:, t, KR:GATE]).then_inc(sem("tile_prep"), 1)
            for t in range(1, NT):
                dve.wait_ge(sem("p_ev"), at[("uq", t, 1)] + 1)
                x = p.qb[:, t % 2, :].rearrange("p (h c) -> p h c", c=96)[:, :, 64:96]
                own.wait(own.n)
                rope(own, dve, x, HB, t).then_inc(sem("q_roped"), 1)
                dve.wait_ge(sem("q_roped"), t)

        @block.tensor
        def _(pe):
            for j, (kind, t, half) in enumerate(jobs):
                b = ps[j % 8]
                if j >= 8:
                    pe.wait_ge(sem("p_ev"), j - 7)
                if kind in ("qk", "low"):
                    if t < NT:
                        pe.wait_ge(sem("tile_prep"), t + 1)
                        pe.wait_ge(sem("low_norm"), 2 * t + 2)
                    else:
                        pe.wait_ge(sem("load_cache"), 64)
                        pe.wait_ge(sem("pads"), 2)
                if kind == "qk":
                    cols = ([p.proj[:, t, QA + P * i:QA + P * (i + 1)] for i in range(4)] if t < NT
                            else [None, None, p.cak[:, 0:128], p.cak[:, 128:256]])
                    for i, c in enumerate(cols):
                        if c is not None:
                            last = nc.tensor.transpose(b[:, i * P:(i + 1) * P], c, p.ident)
                elif kind == "low":
                    cols = ([p.proj[:, t, QC:QC + P], p.proj[:, t, QC + P:KVC], p.proj[:, t, KVC:KR], p.krp[:, t, :]] if t < NT
                            else [None, None, p.cckv[:, :], p.ckr[:, :]])
                    for i, c in enumerate(cols):
                        if c is not None:
                            last = nc.tensor.transpose(b[0:c.shape[1], i * P:(i + 1) * P], c, p.ident)
                elif kind == "kn":
                    if (t, half) == (0, 0):
                        pe.wait_ge(sem("load_wuk"), 32)
                        pe.wait_ge(sem("p_ev"), at[("low", NT, 0)] + 1)
                    lo, hi = (0, 512) if half == 0 else (512, KEYS)
                    last = nc.tensor.matmul(b[0:64, 0:hi - lo], p.wukn[:, t * 64:t * 64 + 64], p.ckvT[:, lo:hi], start=True, stop=True)
                elif kind == "v":
                    last = nc.tensor.matmul(b[:, :], p.ckvT[:, t * P:(t + 1) * P], p.wukv[:, :], start=True, stop=True)
                elif kind == "uq":
                    if (t, half) == (0, 0):
                        pe.wait_ge(sem("load_wuq"), 16)
                    for k in range(2):
                        last = nc.tensor.matmul(b[:, 0:384], p.qcT[:, k, t * P:(t + 1) * P], p.wuq[:, k, half * 384:half * 384 + 384],
                                                start=(k == 0), stop=(k == 1))
                else:
                    pe.wait_ge(sem("p_ev"), at[("uq", t, 1)] + 1)
                    if t >= 1:
                        pe.wait_ge(sem("q_roped"), t)
                    for h in range(4):
                        hh = 4 * half + h
                        last = nc.tensor.transpose(b[0:96, h * P:(h + 1) * P], p.qb[:, t % 2, hh * 96:hh * 96 + 96], p.ident)
                last.then_inc(sem("p_mm"), 1)


def attend(p):
    nc, sem, ps = p.nc, p.sem, p.ps
    maps, outs = [], []
    for t in range(NT):
        for h in range(HA):
            maps += [(t, h, 0), (t, h, 1)]
            outs.append(("a", t, h, len(maps)))
        for h in range(HB):
            maps.append((t, h, None))
            outs.append(("b", t, h, len(maps)))
    out_after = {n: (o, kind, t, h) for o, (kind, t, h, n) in enumerate(outs)}

    def keys(t):
        return (0, P) if t == 0 else (P, KEYS)

    def value(kind, t, kt, h):
        if kind == "b":
            return p.vb[:, kt, h * 64:h * 64 + 64]
        if kt == 1:
            return p.cav[:, h * 64:h * 64 + 64]
        return p.proj[:, 0 if kt == 0 else kt - 1, VA + h * 64:VA + h * 64 + 64]

    A, B = 32.0 ** -0.5, 96.0 ** -0.5
    with nc.Block() as block:
        @block.tensor
        def _(pe):
            def scores(m):
                t, h, i = maps[m]
                lo, hi = keys(t)
                s = 2 * (m % 2)
                if m >= 2:
                    pe.wait_ge(sem("a_exp"), m - 1)
                if i is None:
                    q = p.qTb[:, h, t * P:(t + 1) * P]
                    k = p.kTb[:, h, lo:hi]
                else:
                    c = 2 * h + i
                    r = 32 * (c % 4)
                    q = p.qTa[r:r + 32, c // 4, t * P:(t + 1) * P]
                    k = p.kTa[r:r + 32, c // 4, lo:hi]
                n = min(hi - lo, 512)
                last = nc.tensor.matmul(ps[s][:, 0:n], q, k[:, 0:n], start=True, stop=True)
                if hi - lo > 512:
                    last = nc.tensor.matmul(ps[s + 1][:, 0:P], q, k[:, 512:640], start=True, stop=True)
                last.then_inc(sem("a_scores"), 1)

            def turn(o):
                kind, t, h, n = outs[o]
                pe.wait_ge(sem("a_diff") if kind == "a" else sem("a_exp"),
                           t * HA + h + 1 if kind == "a" else n)
                if o >= 1:
                    pe.wait_ge(sem("a_turned_out"), o)
                src = p.prob[:, (n - 1) % 4, :]
                for j in range((keys(t)[1] - keys(t)[0]) // P):
                    last = nc.tensor.transpose(ps[4 + j // 4][:, (j % 4) * P:(j % 4 + 1) * P], src[:, j * P:(j + 1) * P], p.ident)
                last.then_inc(sem("a_turned"), 1)

            def sums(o):
                kind, t, h, n = outs[o]
                pe.wait_ge(sem("a_turned_out"), o + 1)
                if o >= 2:
                    pe.wait_ge(sem("a_out"), o - 1)
                nk = (keys(t)[1] - keys(t)[0]) // P
                for j in range(nk):
                    last = nc.tensor.matmul(ps[6 + o % 2][:, 0:64], p.probT[:, o % 2, j * P:(j + 1) * P],
                                            value(kind, t, j if t == 0 else j + 1, h), start=(j == 0), stop=(j == nk - 1))
                last.then_inc(sem("a_sums"), 1)

            o = 0
            for m in range(len(maps) + 4):
                if m < len(maps):
                    scores(m)
                if m - 1 in out_after:
                    turn(out_after[m - 1][0])
                if m - 2 in out_after:
                    sums(out_after[m - 2][0])

        @block.scalar
        def _(act):
            act.wait_ge(sem("lam_dot"), 2)
            nc.scalar.activation(p.lam[:, 2:4], p.lam[:, 0:2], ACT.Exp).then_inc(sem("lam_exp"), 1)

            def turned_out(o):
                kind, t, h, n = outs[o]
                act.wait_ge(sem("a_turned"), o + 1)
                if o >= 2:
                    act.wait_ge(sem("a_sums"), o - 1)
                nk = (keys(t)[1] - keys(t)[0])
                last = nc.scalar.activation(p.probT[:, o % 2, 0:min(nk, 512)], ps[4][:, 0:min(nk, 512)], ACT.Copy)
                if nk > 512:
                    last = nc.scalar.activation(p.probT[:, o % 2, 512:nk], ps[5][:, 0:P], ACT.Copy)
                last.then_inc(sem("a_turned_out"), 1)

            for m in range(len(maps) + 4):
                if m < len(maps):
                    t, h, i = maps[m]
                    nk = keys(t)[1] - keys(t)[0]
                    act.wait_ge(sem("a_max"), m + 1)
                    if m >= 4:
                        done = [o for o, x in enumerate(outs) if x[3] > m - 4]
                        act.wait_ge(sem("a_turned"), done[0] + 1)
                    s = 2 * (m % 2)
                    sc = p.score2(s, nk)
                    nc.scalar.activation(p.prob[:, m % 4, 0:nk], sc, ACT.Exp, bias=p.nmax[:, m % 4:m % 4 + 1],
                                         scale=B if i is None else A, accum_out=p.esum[:, m % 4:m % 4 + 1]).then_inc(sem("a_exp"), 1)
                if m - 1 in out_after:
                    turned_out(out_after[m - 1][0])
            act.wait_ge(sem("squares_a"), NT)
            nc.scalar.activation(p.ssa[:, :, :], p.ssa[:, :, :], ACT.Sqrt, bias=p.eps[:, 0:1],
                                 scale=1.0 / 64).then_inc(sem("root_a"), 1)

        @block.vector
        def _(dve):
            own = Chain(dve, sem("dve_attend"))
            dve.wait_ge(sem("lam_exp"), 1)
            own.link(nc.vector.tensor_tensor(p.lam[:, 4:5], p.lam[:, 3:4], p.lam[:, 2:3], ALU.subtract))
            own.link(nc.vector.tensor_tensor(p.lam[:, 5:6], p.lam[:, 4:5], p.row[:, R_LI:R_LI + 1], ALU.subtract))

            def max_of(m):
                t, h, i = maps[m]
                nk = keys(t)[1] - keys(t)[0]
                dve.wait_ge(sem("a_scores"), m + 1)
                if m >= 4:
                    dve.wait_ge(sem("a_exp"), m - 3)
                own.link(nc.vector.tensor_reduce(p.mx[:, m % 4:m % 4 + 1], p.score2(2 * (m % 2), nk), AX.X, ALU.max))
                nc.vector.tensor_scalar(p.nmax[:, m % 4:m % 4 + 1], p.mx[:, m % 4:m % 4 + 1], -(B if i is None else A), None,
                                        ALU.mult).then_inc(sem("a_max"), 1)

            def weigh(o):
                kind, t, h, n = outs[o]
                dve.wait_ge(sem("a_exp"), n)
                m = n - 1
                if kind == "b":
                    if o >= 8:
                        dve.wait_ge(sem("a_out"), o - 7)
                    own.mark(nc.vector.reciprocal(p.rs[:, o % 8:o % 8 + 1], p.esum[:, m % 4:m % 4 + 1]))
                    return
                nk = keys(t)[1] - keys(t)[0]
                own.mark(nc.vector.reciprocal(p.r01[:, 0:1], p.esum[:, (m - 1) % 4:(m - 1) % 4 + 1]))
                own.link(nc.vector.reciprocal(p.r01[:, 1:2], p.esum[:, m % 4:m % 4 + 1]))
                own.link(nc.vector.tensor_tensor(p.r01[:, 1:2], p.r01[:, 1:2], p.lam[:, 5:6], ALU.mult))
                own.link(nc.vector.tensor_scalar(p.prob[:, (m - 1) % 4, 0:nk], p.prob[:, (m - 1) % 4, 0:nk], p.r01[:, 0:1], None, ALU.mult))
                nc.vector.scalar_tensor_tensor(out=p.prob[:, m % 4, 0:nk], in0=p.prob[:, m % 4, 0:nk], scalar=p.r01[:, 1:2],
                                               in1=p.prob[:, (m - 1) % 4, 0:nk], op0=ALU.mult, op1=ALU.add).then_inc(sem("a_diff"), 1)

            def out(o):
                kind, t, h, n = outs[o]
                dve.wait_ge(sem("a_sums"), o + 1)
                if kind == "a":
                    nc.vector.tensor_copy(p.mixed[:, t, h * 64:h * 64 + 64], ps[6 + o % 2][:, 0:64]).then_inc(sem("a_out"), 1)
                else:
                    own.wait(own.n)
                    nc.vector.tensor_scalar(p.mixed[:, t, 256 + h * 64:320 + h * 64], ps[6 + o % 2][:, 0:64],
                                            p.rs[:, o % 8:o % 8 + 1], None, ALU.mult).then_inc(sem("a_out"), 1)

            for m in range(len(maps) + 5):
                if m < len(maps):
                    max_of(m)
                if m in out_after:
                    weigh(out_after[m][0])
                if m - 3 in out_after:
                    out(out_after[m - 3][0])
            dve.wait_ge(sem("a_out"), len(outs))
            for t in range(NT):
                x = p.mixed[:, t, 0:256]
                if t >= 1:
                    dve.wait_ge(sem("squares_a"), t)
                own.link(nc.vector.tensor_tensor(p.junk[:, 0:256], x, x, ALU.mult))
                nc.vector.tensor_reduce(p.ssa[:, t, :], p.junk[:, 0:256].rearrange("p (h n) -> p h n", h=4), AX.X,
                                        ALU.add).then_inc(sem("squares_a"), 1)
            own.link(nc.vector.tensor_scalar(p.gsub[:, :], p.row[:, R_SUB:R_SUB + 64], p.row[:, R_LI + 1:R_LI + 2], None, ALU.mult))
            dve.wait_ge(sem("root_a"), 1)
            own.link(nc.vector.reciprocal(p.ssa[:, :, :], p.ssa[:, :, :]))
            for t in range(NT):
                x = p.mixed[:, t, 0:256].rearrange("p (h n) -> p h n", h=4)
                own.link(nc.vector.tensor_tensor(x, x, bc(p.ssa[:, t, :], 2, 64), ALU.mult))
                own.mark(nc.vector.tensor_tensor(x, x, bc(p.gsub[:, :], 1, 4), ALU.mult))


def project_out(p, lay):
    nc, d, sem, ps = p.nc, p.d, p.sem, p.ps
    vecs = [p.mod[:, 16:24, :], p.A2[:, :, :], p.mod[:, 24:32, :], p.mod[:, 40:48, :]]
    units = [(v, g, half) for v in range(4) for g in range(2) for half in range(2)]

    def row_of(v, g):
        return p.gt2[:, g, :] if v == 3 else p.rows[:, v, g, :]

    with nc.Block() as block:
        @block.sync
        def _(sp):
            load_weights_out(p, sp, lay, range(0, 2))

        @block.tensor
        def _(pe):
            for t in range(NT):
                if t >= 1:
                    pe.wait_ge(sem("m_out"), 2 * t)
                for k in range(KT):
                    last = nc.tensor.transpose(ps[k // 4][:, (k % 4) * P:(k % 4 + 1) * P], p.mixed[:, t, k * P:(k + 1) * P], p.ident)
                last.then_inc(sem("m_turned"), 1)
            for u in range(len(units)):
                pe.wait_ge(sem("diag2"), u + 1)
                if u >= 2:
                    pe.wait_ge(sem("row_out"), u - 1)
                nc.tensor.matmul(ps[2 + u % 2][:, :], p.ones, p.diag4[:, u % 2, :], start=True, stop=True).then_inc(sem("row_mm"), 1)
            pe.wait_ge(sem("m_out"), 2 * NT)
            for t in range(NT):
                for c in range(2):
                    j = 2 * t + c
                    if t == 0:
                        pe.wait_ge(sem(f"load_v{c}"), 16)
                    if j >= 4:
                        pe.wait_ge(sem("res1"), j - 3)
                    for k in range(KT):
                        last = nc.tensor.matmul(ps[4 + j % 4][:, :], p.mixedT[:, k, t * P:(t + 1) * P], p.wring2[:, c, k, :],
                                                start=(k == 0), stop=(k == KT - 1))
                    last.then_inc(sem("wout_mm"), 1)
            for t in range(NT):
                pe.wait_ge(sem("h2_ready"), t + 1)
                if t >= 1:
                    pe.wait_ge(sem("h2T_out"), 2 * t)
                for k in range(KT):
                    last = nc.tensor.transpose(ps[k // 4][:, (k % 4) * P:(k % 4 + 1) * P], p.mixed[:, t, k * P:(k + 1) * P], p.ident)
                last.then_inc(sem("h2_turned"), 1)

        @block.scalar
        def _(act):
            for t in range(NT):
                act.wait_ge(sem("m_turned"), t + 1)
                for h in range(2):
                    nc.scalar.activation(p.mixedT[:, 4 * h:4 * h + 4, t * P:(t + 1) * P],
                                         ps[h].rearrange("p (k n) -> p k n", k=4), ACT.Copy).then_inc(sem("m_out"), 1)
            for u, (v, g, half) in enumerate(units):
                act.wait_ge(sem("row_mm"), u + 1)
                nc.scalar.activation(row_of(v, g)[:, half * 512:half * 512 + 512], ps[2 + u % 2], ACT.Copy).then_inc(sem("row_out"), 1)
            for t in range(NT):
                act.wait_ge(sem("res1"), 2 * t + 2)
                nc.scalar.activation(p.junk[:, :], p.x[:, t, :], ACT.Square, accum_out=p.ss1[:, t:t + 1]).then_inc(sem("square2"), 1)
                act.wait_ge(sem("square2"), t + 1)
                nc.scalar.activation(p.rt1[:, t:t + 1], p.ss1[:, t:t + 1], ACT.Sqrt, bias=p.eps[:, 0:1], scale=1.0 / D).then_inc(sem("root2"), 1)
            for t in range(NT):
                act.wait_ge(sem("h2_turned"), t + 1)
                for h in range(2):
                    nc.scalar.activation(p.h2T[:, 4 * h:4 * h + 4, t * P:(t + 1) * P],
                                         ps[h].rearrange("p (k n) -> p k n", k=4), ACT.Copy).then_inc(sem("h2T_out"), 1)

        @block.vector
        def _(dve):
            own = Chain(dve, sem("dve_out"))
            for u, (v, g, half) in enumerate(units):
                if u >= 2:
                    dve.wait_ge(sem("row_mm"), u - 1)
                nc.vector.tensor_tensor(p.diag4[:, u % 2, :].rearrange("p (k n) -> p k n", k=4), bc(p.ident, 1, 4),
                                        bc(vecs[v][:, 4 * half:4 * half + 4, g], 2, P), ALU.mult).then_inc(sem("diag2"), 1)
            dve.wait_ge(sem("row_out"), len(units))

            def norm(t):
                g = 0 if t == 0 else 1
                dve.wait_ge(sem("root2"), t + 1)
                own.link(nc.vector.reciprocal(p.rt1[:, t:t + 1], p.rt1[:, t:t + 1]))
                own.link(nc.vector.scalar_tensor_tensor(out=p.mixed[:, t, :], in0=p.x[:, t, :], scalar=p.rt1[:, t:t + 1],
                                                        in1=p.rows[:, 1, g, :], op0=ALU.mult, op1=ALU.mult))
                nc.vector.tensor_tensor(p.mixed[:, t, :], p.mixed[:, t, :], p.rows[:, 2, g, :], ALU.add).then_inc(sem("h2_ready"), 1)

            for t in range(NT):
                g = 0 if t == 0 else 1
                for c in range(2):
                    j = 2 * t + c
                    cols = slice(c * 512, c * 512 + 512)
                    dve.wait_ge(sem("wout_mm"), j + 1)
                    own.link(nc.vector.tensor_tensor(p.gated[:, cols], ps[4 + j % 4], p.rows[:, 0, g, cols], ALU.mult))
                    nc.vector.tensor_tensor(p.x[:, t, cols], p.x[:, t, cols], p.gated[:, cols], ALU.add).then_inc(sem("res1"), 1)
                if t >= 1:
                    norm(t - 1)
            norm(NT - 1)


def load_weights_out(p, sp, lay, chunks):
    for c in chunks:
        if c >= 2:
            if c < 4:
                sp.wait_ge(p.sem("wout_mm"), 2 * NT)
            else:
                sp.wait_ge(p.sem("pq_mm"), 8 * (c - 3))
        src = p.d["w_out"] if c < 2 else p.d["w_pq"]
        a = WCH * (c if c < 2 else c - 2)
        sp.dma_start(p.wring2[:, c % 2, :, :], src[bass.ds(lay, 1), :, :, a:a + WCH].rearrange("l p k n -> p (l k) n")).then_inc(p.sem(f"load_v{c % 2}"), 16)


def route(p, lay):
    nc, d, sem, ps = p.nc, p.d, p.sem, p.ps
    C = 4
    jobs = []
    for c in range(C + 1):
        if c < C:
            jobs += [("q", c, b, g) for b in range(4) for g in range(2)]
        if c >= 1:
            jobs += [("s", c - 1, t, 0) for t in range(NT)]
    at = {job: j for j, job in enumerate(jobs)}

    with nc.Block() as block:
        @block.sync
        def _(sp):
            sp.dma_start(p.keysT[:, :], d["keysT"][bass.ds(lay, 1)].rearrange("l p n -> p (l n)")).then_inc(sem("load_keys"), 16)
            load_weights_out(p, sp, lay, range(2, 6))

        @block.tensor
        def _(pe):
            for j, (kind, c, i, g) in enumerate(jobs):
                if j >= 8:
                    pe.wait_ge(sem("r_out"), j - 7)
                b = ps[j % 8]
                if kind == "q":
                    if (i, g) == (0, 0):
                        pe.wait_ge(sem(f"load_v{c % 2}"), 16 * (2 + c // 2))
                    lo, hi = (0, P) if g == 0 else (P, TOK)
                    for k in range(KT):
                        last = nc.tensor.matmul(b[:, 0:hi - lo], p.wring2[:, c % 2, k, i * P:(i + 1) * P], p.h2T[:, k, lo:hi],
                                                start=(k == 0), stop=(k == KT - 1))
                    last.then_inc(sem("pq_mm"), 1)
                else:
                    if i == 0:
                        pe.wait_ge(sem("load_keys"), 16)
                        pe.wait_ge(sem("r_out"), at[("q", c, 3, 1)] + 1)
                    for q in range(4):
                        last = nc.tensor.matmul(b[:, q * P:(q + 1) * P], p.qpT[:, c % 2, q, i * P:(i + 1) * P],
                                                p.keysT[:, (4 * c + q) * P:(4 * c + q + 1) * P], start=True, stop=True)
                    last.then_inc(sem("sc_mm"), 1)

        @block.scalar
        def _(act):
            for j, (kind, c, i, g) in enumerate(jobs):
                b = ps[j % 8]
                if kind == "q":
                    act.wait_ge(sem("pq_mm"), 8 * c + 2 * i + g + 1)
                    if c >= 2 and (i, g) == (0, 0):
                        act.wait_ge(sem("sc_mm"), NT * (c - 1))
                    lo, hi = (0, P) if g == 0 else (P, TOK)
                    nc.scalar.activation(p.qpT[:, c % 2, i, lo:hi], b[:, 0:hi - lo], ACT.Copy).then_inc(sem("r_out"), 1)
                else:
                    act.wait_ge(sem("sc_mm"), NT * c + i + 1)
                    nc.scalar.activation(p.sub[:, i, 512 * c:512 * c + 512], b, ACT.Copy).then_inc(sem("r_out"), 1)
            for t in range(NT):
                act.wait_ge(sem("centred"), t + 1)
                nc.scalar.activation(p.gat[:, t, :], p.gat[:, t, :], ACT.Exp).then_inc(sem("gate_exp"), 1)

        @block.vector
        def _(dve):
            own = Chain(dve, sem("dve_route"))

            def top16(src, n, val, idx):
                for half in range(2):
                    lo, hi = 8 * half, 8 * half + 8
                    for r in range(n):
                        m = own.mark(nc.vector.max(val(r)[:, lo:hi], src(r)))
                    own.wait(m)
                    for r in range(n):
                        own.mark(nc.vector.max_index(idx(r)[:, lo:hi], val(r)[:, lo:hi], src(r)))
                    if half == 0:
                        for r in range(n):
                            m = own.mark(nc.vector.match_replace(src(r), val(r)[:, lo:hi], src(r), NEG))
                    own.wait(own.n)

            for t in range(NT):
                dve.wait_ge(sem("r_out"), at[("s", C - 1, t, 0)] + 1)
                top16(lambda r: p.sub[:, t, r * P:(r + 1) * P], 16, lambda r: p.tv[:, r, :], lambda r: p.ti[:, r, :])
                own.link(nc.vector.tensor_copy(p.tf[:, :, :], p.ti[:, :, :]))
                cand = p.sub[:, t, :].rearrange("p (h i j) -> p h i j", h=NH, i=TOPK)
                tv = p.tv[:, :, :].rearrange("p (h s) k -> p h s k", s=2)
                tf = p.tf[:, :, :].rearrange("p (h s) k -> p h s k", s=2)
                own.link(nc.vector.tensor_tensor(cand, bc(tv[:, :, 0, :], 3, TOPK), bc(tv[:, :, 1, :], 2, TOPK), ALU.add))
                top16(lambda r: p.sub[:, t, r * 256:(r + 1) * 256], NH, lambda r: p.bv[:, r, :], lambda r: p.bi[:, r, :])
                own.mark(nc.vector.tensor_scalar(p.bij[:, 0, :, :], p.bi[:, :, :], 4, None, ALU.logical_shift_right))
                own.link(nc.vector.tensor_scalar(p.bij[:, 1, :, :], p.bi[:, :, :], 15, None, ALU.bitwise_and))
                own.link(nc.vector.tensor_copy(p.bf[:, :, :, :], p.bij[:, :, :, :]))
                pick = cand
                for s in range(2):
                    own.link(nc.vector.tensor_tensor(pick, bc(p.bf[:, s, :, :], 3, TOPK), p.io16.unsqueeze(1).unsqueeze(1).to_broadcast([P, NH, TOPK, TOPK]), ALU.is_equal))
                    own.link(nc.vector.tensor_tensor(pick, pick, bc(tf[:, :, s, :], 2, TOPK), ALU.mult))
                    own.link(nc.vector.tensor_reduce(p.ex[:, s, :, :], pick, AX.X, ALU.add))
                own.link(nc.vector.scalar_tensor_tensor(out=p.ex[:, 0, :, :], in0=p.ex[:, 0, :, :], scalar=128.0, in1=p.ex[:, 1, :, :],
                                                        op0=ALU.mult, op1=ALU.add))
                own.mark(nc.vector.tensor_scalar(p.eidx[:, t, :], p.ex[:, 0, :, :].rearrange("p h k -> p (h k)"),
                                                 p.row[:, R_OFF:R_OFF + 1], None, ALU.add))
                gat = p.gat[:, t, :].rearrange("p (h k) -> p h k", h=NH)
                nc.vector.tensor_tensor(gat, p.bv[:, :, :], p.bv[:, :, 0:1].to_broadcast([P, NH, TOPK]), ALU.subtract).then_inc(sem("centred"), 1)
                dve.wait_ge(sem("gate_exp"), t + 1)
                own.link(nc.vector.tensor_reduce(p.gs[:, :], gat, AX.X, ALU.add))
                own.link(nc.vector.reciprocal(p.gs[:, :], p.gs[:, :]))
                own.link(nc.vector.tensor_tensor(gat, gat, bc(p.gs[:, :], 2, TOPK), ALU.mult))


def experts(p, lay):
    nc, d, sem, ps = p.nc, p.d, p.sem, p.ps
    H = RING

    def tiles(eng, body):
        with eng.Fori(0, NH) as h:
            body(0, 0, h, h)
        with eng.Fori(1, NT) as t:
            with eng.Fori(0, NH) as h:
                body(t, 1, h, t * NH + h)

    with nc.Block() as block:
        @block.gpsimd
        def _(pool):
            free = pool.alloc_register("rows_free")
            pool.reg_mov(free, 1)
            staged = pool.alloc_register("halves_staged")
            pool.reg_mov(staged, 1)

            def row_is_free():
                pool.wait_ge(sem("row_free"), free)
                pool.reg_add(free, free, 1)

            def head(t, g, h, n):
                for half in range(2):
                    row_is_free()
                    cols = bass.ds(h * TOPK + half * H, H)
                    e = p.eidx[:, t, cols] if g == 0 else p.eidx[:, bass.ds(t, 1), cols].rearrange("p a n -> p (a n)")
                    nc.gpsimd.tensor_copy(p.stage[:, half, :], e).then_inc(sem("staged"), 1)
                    pool.wait_ge(sem("staged"), staged)
                    pool.reg_add(staged, staged, 1)
                    for s in range(H):
                        if s > 0:
                            row_is_free()
                        nc.gpsimd.indirect_dma_start(out=p.uv[:, s, :], out_offset=None, in_=d["peer_uv"],
                                                     in_offset=bass.IndirectOffsetOnAxis(ap=p.stage[:, half, s:s + 1], axis=0)
                                                     ).then_inc(sem(f"row_in{s}"), 16)
            tiles(pool, head)

        @block.vector
        def _(dve):
            def begin(t, g):
                src = p.mixed[:, t, :] if g == 0 else p.mixed[:, bass.ds(t, 1), :].rearrange("p a n -> p (a n)")
                nc.vector.tensor_copy(p.hcur[:, :], src).then_inc(sem("h_here"), 1)
                nc.vector.memset(p.y[:, :], 0.0).then_inc(sem("h_here"), 1)

            def head(t, g, h, n):
                dve.wait_ge(sem("h_here"), 2 * t + 2)
                for half in range(2):
                    for s in range(H):
                        dve.wait_ge(sem(f"row_in{s}"), (lay * NT * NH + n) * 32 + (half + 1) * 16)
                        nc.vector.tensor_tensor_reduce(out=p.uv[:, s, 0:D], in0=p.uv[:, s, 0:D], in1=p.hcur[:, :], scale=1.0, scalar=0.0,
                                                       op0=ALU.mult, op1=ALU.add, accum_out=p.dot[:, half, s:s + 1]).then_inc(sem("dots"), 1)
                    dve.wait_ge(sem("gelus"), 2 * n + half + 1)
                    cols = bass.ds(h * TOPK + half * H, H)
                    gat = p.gat[:, t, cols] if g == 0 else p.gat[:, bass.ds(t, 1), cols].rearrange("p a n -> p (a n)")
                    nc.vector.tensor_tensor(p.wgt[:, half, :], p.act8[:, half, :], gat, ALU.mult).then_inc(sem("weights"), 1)
                for c in range(2):
                    cols = slice(c * 512, c * 512 + 512)
                    dve.wait_ge(sem("head_sum"), n + 1)
                    nc.vector.tensor_tensor(p.y[:, cols], p.y[:, cols], ps[c], ALU.add).then_inc(sem("y_added"), 1)
                dve.wait_ge(sem("y_added"), 2 * n + 2)

            def end(t, g):
                nc.vector.tensor_tensor(p.y[:, :], p.y[:, :], p.gt2[:, g, :], ALU.mult).then_inc(sem("residual"), 1)
                dve.wait_ge(sem("residual"), 2 * t + 1)
                x = p.x[:, t, :] if g == 0 else p.x[:, bass.ds(t, 1), :].rearrange("p a n -> p (a n)")
                nc.vector.tensor_tensor(x, x, p.y[:, :], ALU.add).then_inc(sem("residual"), 1)
                dve.wait_ge(sem("residual"), 2 * t + 2)

            begin(0, 0)
            with dve.Fori(0, NH) as h:
                head(0, 0, h, h)
            end(0, 0)
            with dve.Fori(1, NT) as t:
                begin(t, 1)
                with dve.Fori(0, NH) as h:
                    head(t, 1, h, t * NH + h)
                end(t, 1)

        @block.scalar
        def _(act):
            def head(t, g, h, n):
                for half in range(2):
                    act.wait_ge(sem("dots"), n * TOPK + (half + 1) * H)
                    nc.scalar.activation(p.act8[:, half, :], p.dot[:, half, :], ACT.Gelu_apprx_tanh).then_inc(sem("gelus"), 1)
                    act.wait_ge(sem("weights"), 2 * n + half + 1)
                    for s in range(H):
                        act.wait_ge(sem("row_free"), n * TOPK + half * H + s + 1)
                        nc.scalar.activation(p.diag[:, s, :], p.ident, ACT.Copy, scale=p.wgt[:, half, s:s + 1]).then_inc(sem("diags"), 1)
            tiles(act, head)

        @block.tensor
        def _(pe):
            nc.tensor.matmul(ps[2][:, 0:8], p.ident, p.ident[:, 0:8], start=True, stop=True).then_inc(sem("row_free"), H)

            def head(t, g, h, n):
                for s in range(TOPK):
                    pe.wait_ge(sem("diags"), n * TOPK + s + 1)
                    if s == 0 and g == 1:
                        pe.wait_ge(sem("y_added"), n * 2)
                    for c in range(2):
                        mm = nc.tensor.matmul(ps[c], p.diag[:, s % H, :], p.uv[:, s % H, D + 512 * c:D + 512 * c + 512],
                                              start=(s == 0), stop=(s == TOPK - 1))
                    if s < TOPK - 1:
                        mm.then_inc(sem("row_free"), 1)
                    else:
                        mm.then_inc(sem("head_sum"), 1)
                        pe.wait_ge(sem("head_sum"), n + 1)
                        nc.tensor.matmul(ps[2][:, 0:8], p.ident, p.ident[:, 0:8], start=True, stop=True).then_inc(sem("row_free"), 1)
                if g == 0:
                    pe.wait_ge(sem("y_added"), n * 2 + 2)
            tiles(pe, head)


def finish(p):
    nc, d, sem = p.nc, p.d, p.sem
    with nc.Block() as block:
        @block.scalar
        def _(act):
            for t in range(NT):
                if t >= 1:
                    act.wait_ge(sem("square_f"), t)
                nc.scalar.activation(p.junk[:, :], p.x[:, t, :], ACT.Square, accum_out=p.ss1[:, t:t + 1]).then_inc(sem("square_f"), 1)
            act.wait_ge(sem("square_f"), NT)
            nc.scalar.activation(p.rt1[:, 0:NT], p.ss1[:, 0:NT], ACT.Sqrt, bias=p.eps[:, 0:1], scale=1.0 / D).then_inc(sem("root_f"), 1)

        @block.vector
        def _(dve):
            dve.wait_ge(sem("root_f"), 1)
            nc.vector.reciprocal(p.rt1[:, 0:NT], p.rt1[:, 0:NT]).then_inc(sem("recip_f"), 1)
            dve.wait_ge(sem("recip_f"), 1)
            dve.wait_ge(sem("load_gf"), 16)
            for t in range(NT):
                nc.vector.scalar_tensor_tensor(out=p.x[:, t, :], in0=p.x[:, t, :], scalar=p.rt1[:, t:t + 1], in1=p.tmp[:, :],
                                               op0=ALU.mult, op1=ALU.mult).then_inc(sem("y_ready"), 1)

        @block.sync
        def _(sp):
            sp.dma_start(p.tmp[:, :], d["g_final"].to_broadcast([P, D])).then_inc(sem("load_gf"), 16)
            sp.wait_ge(sem("y_ready"), 1)
            sp.dma_start(d["yp"], p.x[:, 0, :]).then_inc(sem("store_y"), 16)
            sp.wait_ge(sem("y_ready"), NT)
            sp.dma_start(d["ys"], p.x[:, 1:NT, :]).then_inc(sem("store_y"), 16)
            sp.wait_ge(sem("store_y"), 32)


def build(nc, dram, stop=None, dumps=None):
    p = Prog(nc, dram)
    with ExitStack() as ctx:
        p.psall = ctx.enter_context(nc.psum_tensor("psall", [P, 8 * 512], F32))
        p.ps = [p.psall[:, 512 * i:512 * i + 512] for i in range(8)]
        p.score2 = lambda s, nk: p.psall[:, 512 * s:512 * s + nk]
        sb = p.sb
        p.x = sb(ctx, "x", [P, NT, D])
        p.cons = sb(ctx, "cons", [P, CONS])
        p.rope = sb(ctx, "rope", [P, 2, 4, 32])
        p.sc = sb(ctx, "sc", [P, KT, 2])
        p.vec = sb(ctx, "vec", [P, V_END])
        p.row = sb(ctx, "row", [P, R_END])
        p.mod = sb(ctx, "mod", [P, 48, 2])
        p.A1 = sb(ctx, "A1", [P, KT, 2])
        p.A2 = sb(ctx, "A2", [P, KT, 2])
        p.ss1 = sb(ctx, "ss1", [P, 8])
        p.rt1 = sb(ctx, "rt1", [P, 8])
        p.junk = sb(ctx, "junk", [P, D])
        p.ident = p.cons[:, 0:P]
        p.ones = p.cons[:, P:2 * P]
        p.imask = p.cons[:, 2 * P:4 * P].rearrange("p (d n) -> p d n", d=2)
        p.lmask = p.cons[:, 4 * P:18 * P].rearrange("p (d l n) -> p d l n", d=2, l=7)
        p.io16 = p.cons[:, 18 * P:18 * P + 16]
        p.eps = p.cons[:, 18 * P + 16:18 * P + 17]
        p.one = p.cons[:, 18 * P + 17:18 * P + 18]
        start(p)
        outer = set(p.sems)
        with nc.Fori(0, LAYERS) as lay:
            layer(p, lay, stop, dumps)
            for name, s in p.sems.items():
                if name not in outer and not name.startswith("row_in"):
                    nc.sync.sem_clear(s)
            nc.all_engine_barrier()
        if stop is None:
            p.tmp = sb(ctx, "tmp", [P, D])
            finish(p)


def layer(p, lay, stop, dumps):
    nc, sb = p.nc, p.sb

    def at(name):
        if stop != name:
            return False
        for n, ap in dumps(p).items():
            nc.sync.dma_start(p.d[n], ap).then_inc(p.sem("dump"), 16)
            nc.sync.wait_ge(p.sem("dump"), 16 * (1 + list(dumps(p)).index(n)))
        return True

    with ExitStack() as whole:
        p.mixed = sb(whole, "mixed", [P, NT, D])
        with ExitStack() as c1:
            p.proj = sb(c1, "proj", [P, NT, TM])
            with ExitStack() as c2:
                p.qkv = sb(c2, "qkv", [P, NT, 768])
                with ExitStack() as c3:
                    p.qkvT = sb(c3, "qkvT", [P, 6, LINE])
                    with ExitStack() as c4:
                        p.hT = sb(c4, "hT", [P, KT, TOK])
                        p.xn = sb(c4, "xn", [P, 2, D])
                        p.wring = sb(c4, "wring", [P, 3, KT, WCH])
                        mod_and_project(p, lay)
                        if at("project"):
                            return
                    with ExitStack() as c4:
                        p.convd = sb(c4, "convd", [P, 6, LINE - 2])
                        conv(p)
                        if at("conv"):
                            return
                with ExitStack() as c3:
                    p.ssd = sb(c3, "ssd", [P, NT, 8])
                    p.rd = sb(c3, "rd", [P, NT, 8])
                    p.zz = sb(c3, "zz", [P, NT, 8])
                    p.zab = sb(c3, "zab", [P, NT, 8])
                    p.sp1 = sb(c3, "sp1", [P, NT, 8])
                    p.bet = sb(c3, "bet", [P, NT, 8])
                    p.eal = sb(c3, "eal", [P, 8])
                    p.g = sb(c3, "g", [P, NT, 8])
                    p.gcol = sb(c3, "gcol", [P, NT, 8])
                    p.egc = sb(c3, "egc", [P, NT, 8])
                    p.begc = sb(c3, "begc", [P, NT, 8])
                    p.sso = sb(c3, "sso", [P, NT, 4])
                    p.oC = sb(c3, "oC", [P, NT, 256])
                    p.dif = sb(c3, "dif", [P, 2, HC, P])
                    p.dec = sb(c3, "dec", [P, 2, HC, P])
                    p.lt = sb(c3, "lt", [P, 2, HC, P])
                    p.mlt = sb(c3, "mlt", [P, 2, 2, HC, P])
                    p.X = sb(c3, "X", [P, 2, HC, P])
                    p.XT = sb(c3, "XT", [P, 2, HC, P])
                    p.t1s = sb(c3, "t1s", [P, 2, HC * P])
                    p.qk = sb(c3, "qk", [P, 2, HC, P])
                    p.rv = sb(c3, "rv", [P, 2, HC, 64])
                    p.rk = sb(c3, "rk", [P, 2, HC, 64])
                    p.kd = sb(c3, "kd", [P, 2, HC, 64])
                    p.w = sb(c3, "w", [P, 2, HC, 64])
                    p.kT = sb(c3, "kT", [64, 2, HC * P])
                    p.qT = sb(c3, "qT", [64, 2, HC * P])
                    p.egr = sb(c3, "egr", [64, 2, HC, P])
                    p.qd = sb(c3, "qd", [64, 2, HC, P])
                    p.nwk = sb(c3, "nwk", [64, 2, HC * P])
                    p.state = sb(c3, "state", [64, 2, HC, 64])
                    delta(p, lay)
                    if at("delta"):
                        return
            with ExitStack() as c2:
                p.qTa = sb(c2, "qTa", [P, 2, TOK])
                p.kTa = sb(c2, "kTa", [P, 2, KEYS])
                p.cav = sb(c2, "cav", [P, 256])
                p.lam = sb(c2, "lam", [P, 8])
                p.vb = sb(c2, "vb", [P, 6, 512])
                p.qTb = sb(c2, "qTb", [96, HB, TOK])
                p.kTb = sb(c2, "kTb", [96, HB, KEYS])
                with ExitStack() as c3:
                    p.cak = sb(c3, "cak", [P, 256])
                    p.cckv = sb(c3, "cckv", [P, 128])
                    p.ckr = sb(c3, "ckr", [P, 96])
                    p.krp = sb(c3, "krp", [P, NT, 96])
                    p.ssl = sb(c3, "ssl", [P, 2, NT])
                    p.rl = sb(c3, "rl", [P, 2, NT])
                    p.qcT = sb(c3, "qcT", [P, 2, TOK])
                    p.ckvT = sb(c3, "ckvT", [P, KEYS])
                    p.wuq = sb(c3, "wuq", [P, 2, 768])
                    p.wukn = sb(c3, "wukn", [P, 512])
                    p.wukv = sb(c3, "wukv", [P, 512])
                    p.qb = sb(c3, "qb", [P, 2, 768])
                    p.ru = sb(c3, "ru", [P, 512])
                    p.rv2 = sb(c3, "rv2", [P, 512])
                    prepare_attention(p, lay)
                with ExitStack() as c3:
                    p.prob = sb(c3, "prob", [P, 4, 640])
                    p.probT = sb(c3, "probT", [P, 2, 640])
                    p.mx = sb(c3, "mx", [P, 4])
                    p.nmax = sb(c3, "nmax", [P, 4])
                    p.esum = sb(c3, "esum", [P, 4])
                    p.rs = sb(c3, "rs", [P, 8])
                    p.r01 = sb(c3, "r01", [P, 2])
                    p.ssa = sb(c3, "ssa", [P, NT, 4])
                    p.gsub = sb(c3, "gsub", [P, 64])
                    attend(p)
                    if at("attend"):
                        return
        p.gt2 = sb(whole, "gt2", [P, 2, D])
        p.gat = sb(whole, "gat", [P, NT, SLOTS])
        p.eidx = sb(whole, "eidx", [P, NT, SLOTS], U32)
        with ExitStack() as c1:
            p.h2T = sb(c1, "h2T", [P, KT, TOK])
            p.wring2 = sb(c1, "wring2", [P, 2, KT, WCH])
            with ExitStack() as c2:
                p.mixedT = sb(c2, "mixedT", [P, KT, TOK])
                p.rows = sb(c2, "rows", [P, 3, 2, D])
                p.diag4 = sb(c2, "diag4", [P, 2, 512])
                p.gated = sb(c2, "gated", [P, D])
                project_out(p, lay)
                if at("out"):
                    return
            with ExitStack() as c2:
                p.qpT = sb(c2, "qpT", [P, 2, 4, TOK])
                p.keysT = sb(c2, "keysT", [P, 16 * P])
                p.sub = sb(c2, "sub", [P, NT, 2048])
                p.tv = sb(c2, "tv", [P, 16, TOPK])
                p.tf = sb(c2, "tf", [P, 16, TOPK])
                p.bv = sb(c2, "bv", [P, NH, TOPK])
                p.bf = sb(c2, "bf", [P, 2, NH, TOPK])
                p.ex = sb(c2, "ex", [P, 2, NH, TOPK])
                p.gs = sb(c2, "gs", [P, NH])
                p.ti = sb(c2, "ti", [P, 16, TOPK], U32)
                p.bi = sb(c2, "bi", [P, NH, TOPK], U32)
                p.bij = sb(c2, "bij", [P, 2, NH, TOPK], U32)
                route(p, lay)
                if at("route"):
                    return
        with ExitStack() as c1:
            p.uv = sb(c1, "uv", [P, RING, 2 * D])
            p.hcur = sb(c1, "hcur", [P, D])
            p.y = sb(c1, "y", [P, D])
            p.dot = sb(c1, "dot", [P, 2, RING])
            p.act8 = sb(c1, "act8", [P, 2, RING])
            p.wgt = sb(c1, "wgt", [P, 2, RING])
            p.diag = sb(c1, "diag", [P, RING, P])
            p.stage = sb(c1, "stage", [P, 2, RING], U32)
            experts(p, lay)
            if at("experts"):
                return


CONS = 18 * P + 18


def constants():
    i = np.arange(P)
    c = np.zeros((P, CONS), np.float32)
    c[:, 0:P] = np.eye(P)
    c[:, P:2 * P] = 1.0
    upper = (i[:, None] <= i[None, :]).astype(np.float32)
    c[:, 2 * P:3 * P] = upper
    c[:, 3 * P:4 * P] = upper.T
    for lvl in range(7):
        b = 2 ** lvl
        join = ((i[:, None] // (2 * b) == i[None, :] // (2 * b)) & (i[:, None] // b % 2 == 0) & (i[None, :] // b % 2 == 1))
        c[:, (4 + lvl) * P:(5 + lvl) * P] = join
        c[:, (11 + lvl) * P:(12 + lvl) * P] = join.T
    c[:, 18 * P:18 * P + 16] = np.arange(16)
    c[:, 18 * P + 16] = EPS
    c[:, 18 * P + 17] = 1.0
    t = np.arange(512)
    n_freq = 8
    freqs = (np.float32(10000.0) ** (-np.arange(n_freq, dtype=np.float32) / n_freq)).astype(np.float32)
    ar = (t // 64).astype(np.float32)[:, None] * freqs
    ac = (t % 64).astype(np.float32)[:, None] * freqs
    ang = np.concatenate([ar, ar, ac, ac], axis=-1)
    sign = np.repeat([-1.0, 1.0, -1.0, 1.0], 8).astype(np.float32)
    tables = np.stack([np.cos(ang), np.sin(ang) * sign]).astype(np.float32)
    rope = tables.reshape(2, 4, P, 32).transpose(2, 0, 1, 3)
    return c, np.ascontiguousarray(rope)


def lay_out(i):
    f = {n: np.asarray(a) for n, a in i.items()}

    def kmajor(w):
        l, k, n = w.shape
        return w.reshape(l, k // P, P, n).transpose(0, 2, 1, 3)

    def fm(v):
        return v.reshape(L, -1, P).transpose(0, 2, 1)

    c_qkv, c_g = 1184, 1952
    w = f["w_in"]
    tm = np.concatenate([w[:, :, :c_qkv], w[:, :, c_g:]], axis=2)
    ukv = f["w_ukv"].reshape(L, P, HB, 2, 64)
    lam = [f[n] for n in ("lam_q1", "lam_k1", "lam_q2", "lam_k2")]
    li = [0.8 - 0.6 * math.exp(-0.3 * l) for l in range(L)]
    layer_consts = np.array([[v, 1.0 - v, l * NK * NK] for l, v in enumerate(li)], np.float32)
    rows = np.concatenate([f["g_subln"], f["g_qc"], f["g_kvc"], f["g_onorm"]] + lam
                          + [f["a_log_f"], f["a_log_b"], f["dt_bias_f"], f["dt_bias_b"], layer_consts], axis=1)
    conv_w = f["conv_c"].reshape(L, 3, 6, P).transpose(0, 3, 2, 1).reshape(L, P, 18)
    vecs = np.concatenate([fm(f["b_mod"]), fm(f["g_norm1"]), fm(f["g_norm2"]), conv_w], axis=2)
    cons, rope = constants()
    out = {
        "consts": cons, "rope": rope,
        "cond": np.stack([f["c_ctx"].reshape(KT, P).T, f["c"].reshape(KT, P).T], axis=2),
        "xp": f["x_prompt"].reshape(P, D),
        "xs": f["x_sample"].reshape(4, P, D).transpose(1, 0, 2),
        "vecs": vecs, "rows": rows,
        "w_mod": kmajor(f["w_mod"]), "w_in_tm": kmajor(tm), "w_in_fm": kmajor(w[:, :, c_qkv:c_g]),
        "cache_a_k": f["cache_a_k"].reshape(L, P, 256), "cache_a_v": f["cache_a_v"].reshape(L, P, 256),
        "cache_ckv": f["cache_b_ckv"].reshape(L, P, 128), "cache_kr": f["cache_b_krope"].reshape(L, P, 32),
        "in_sf": f["state_c_fwd"].reshape(L, HC, 64, 64), "in_sb": f["state_c_bwd"].reshape(L, HC, 64, 64),
        "w_uq": kmajor(f["w_uq"]), "w_ukn": ukv[:, :, :, 0].reshape(L, P, 512), "w_ukv": ukv[:, :, :, 1].reshape(L, P, 512),
        "w_out": kmajor(f["w_out"]), "w_pq": kmajor(f["w_pq"]),
        "keysT": f["peer_keys"].reshape(L, 16, NK, P).transpose(0, 3, 1, 2).reshape(L, P, 16 * NK),
        "peer_uv": np.concatenate([f["peer_u"], f["peer_v"]], axis=2).reshape(L * NK * NK, 2 * D),
        "g_final": f["g_final"].reshape(1, D),
    }
    return {n: np.ascontiguousarray(a, dtype=np.float32) for n, a in out.items()}


OUTS = {"yp": (P, D), "ys": (P, 4, D), "out_ak": (L, P, 256), "out_av": (L, P, 256), "out_ckv": (L, P, 128),
        "out_kr": (L, P, 32), "out_sf": (L, HC, 64, 64), "out_sb": (L, HC, 64, 64)}


def kernel(**inputs):
    import concourse.bacc as bacc
    from concourse.bass_utils import run_bass_kernel_spmd

    nc = bacc.Bacc("TRN2", target_bir_lowering=False, num_devices=1)
    arrays = lay_out(inputs)
    dram = {n: nc.dram_tensor("in_" + n, a.shape, F32, kind="ExternalInput").ap() for n, a in arrays.items()}
    dram.update({n: nc.dram_tensor("res_" + n, s, F32, kind="ExternalOutput").ap() for n, s in OUTS.items()})
    build(nc, dram)
    got = run_bass_kernel_spmd(nc, [{"in_" + n: a for n, a in arrays.items()}], core_ids=[0]).results[0]
    r = {n: got["res_" + n] for n in OUTS}
    return (r["yp"].reshape(1, P, D), r["ys"].transpose(1, 0, 2).reshape(1, 4 * P, D),
            r["out_ak"].reshape(1, L, P, HA, 2, 32), r["out_av"].reshape(1, L, P, HA, 64),
            r["out_ckv"].reshape(1, L, P, 128), r["out_kr"].reshape(1, L, P, 32),
            r["out_sf"].reshape(1, L, HC, 64, 64), r["out_sb"].reshape(1, L, HC, 64, 64))
```

```python
import math
from contextlib import ExitStack

import numpy as np

import concourse.bass as bass
from concourse import mybir

F32 = mybir.dt.float32
U32 = mybir.dt.uint32
ALU = mybir.AluOpType
ACT = mybir.ActivationFunctionType
AX = mybir.AxisListType

P = 128
D, L = 1024, 2
LAYERS = L
KT = D // P
NT = 5
TOK = NT * P
EPS = 1e-6
QA, KA, VA, QC, KVC, KR, GATE, BF, TM = 0, 256, 512, 768, 1024, 1152, 1184, 1440, 1456
TM_CHUNKS = [(0, 512), (512, 1024), (1024, TM)]
FM_CHUNKS = [(0, 512), (512, 768)]
MOD_CHUNKS = 12
WCH = 512
LINE = 644
HA, HB, HC = 4, 8, 4
KEYS = 6 * P
NH, NK, TOPK = 8, 128, 16
LEVELS = 7
X_STEPS = 2 * (LEVELS - 1)
KS_LEVEL = 2
AHEAD = 2
PIECES = TOPK
STEPS = 19
SLOTS = NH * TOPK
RING = 8
R_SUB, R_QC, R_KVC, R_ON, R_LAM, R_ALOG, R_DT, R_LI, R_OFF, R_END = 0, 64, 320, 448, 512, 640, 648, 656, 658, 659
V_BMOD, V_G1, V_G2, V_CONV, V_END = 0, 48, 56, 64, 82
NEG = -3.0e38


def kcol(t):
    return 0 if t == 0 else P * (t + 1)


class Chain:

    def __init__(self, eng, sem):
        self.eng, self.sem, self.n = eng, sem, 0

    def mark(self, ins):
        self.n += 1
        ins.then_inc(self.sem, 1)
        return self.n

    def wait(self, n):
        self.eng.wait_ge(self.sem, n)

    def link(self, ins):
        self.wait(self.mark(ins))


class Prog:

    def __init__(self, nc, dram):
        self.nc, self.d = nc, dram
        self.sems = {}
        self.first = None

    def sem(self, name):
        if name not in self.sems:
            self.sems[name] = self.nc.alloc_semaphore(name)
        return self.sems[name]

    def sb(self, ctx, name, shape, dt=F32):
        return ctx.enter_context(self.nc.sbuf_tensor(name, shape, dt))


def bc(ap, axis, n):
    a = ap.unsqueeze(axis)
    shape = list(a.shape)
    shape[axis] = n
    return a.to_broadcast(shape)


def start(p):
    nc, d, sem = p.nc, p.d, p.sem
    with nc.Block() as block:
        @block.sync
        def _(sp):
            sp.dma_start(p.cons[:, :], d["consts"]).then_inc(sem("load_const"), 16)
            sp.dma_start(p.rope[:, :, :, :], d["rope"]).then_inc(sem("load_const"), 16)
            sp.dma_start(p.sc[:, :, :], d["cond"]).then_inc(sem("load_cond"), 16)
            sp.dma_start(p.x[:, 0, :], d["xp"]).then_inc(sem("load_const"), 16)
            sp.dma_start(p.x[:, 1:NT, :], d["xs"]).then_inc(sem("load_const"), 16)
            sp.wait_ge(sem("load_const"), 64)

        @block.scalar
        def _(act):
            act.wait_ge(sem("load_cond"), 16)
            nc.scalar.activation(p.sc[:, :, :], p.sc[:, :, :], ACT.Silu).then_inc(sem("silu_c"), 1)
            act.wait_ge(sem("silu_c"), 1)


def mod_and_project(p, lay):
    nc, d, sem = p.nc, p.d, p.sem
    ps = p.ps
    wsem = [sem(f"load_w{i}") for i in range(3)]
    n_chunks = MOD_CHUNKS + len(TM_CHUNKS) + len(FM_CHUNKS)

    jobs = []
    for c, (a, b) in enumerate(TM_CHUNKS):
        for t in range(NT):
            jobs.append(("tm", MOD_CHUNKS + c, t, a, b))
    for c, (a, b) in enumerate(FM_CHUNKS):
        for blk in range(a // P, b // P):
            for g in range(2):
                jobs.append(("fm", MOD_CHUNKS + len(TM_CHUNKS) + c, g, blk, blk - a // P))

    jobs_until = {job[1]: j + 1 for j, job in enumerate(jobs)}

    def w_arrived(pe, c):
        pe.wait_ge(wsem[c % 3], 16 * (c // 3 + 1))

    with nc.Block() as block:
        @block.sync
        def _(sp):
            sp.dma_start(p.vec[:, :], d["vecs"][bass.ds(lay, 1)].rearrange("a p n -> p (a n)")).then_inc(sem("load_vec"), 16)
            sp.dma_start(p.row[:, :], d["rows"][bass.ds(lay, 1)].to_broadcast([P, R_END])).then_inc(sem("load_row"), 16)
            for c in range(n_chunks):
                if c >= MOD_CHUNKS + 3:
                    sp.wait_ge(sem("proj"), jobs_until[c - 3])
                elif c >= 3:
                    sp.wait_ge(sem("w_used"), c - 2)
                if c < MOD_CHUNKS:
                    src = d["w_mod"][bass.ds(lay, 1), :, :, c * WCH:(c + 1) * WCH]
                    w = WCH
                elif c < MOD_CHUNKS + len(TM_CHUNKS):
                    a, b = TM_CHUNKS[c - MOD_CHUNKS]
                    src = d["w_in_tm"][bass.ds(lay, 1), :, :, a:b]
                    w = b - a
                else:
                    a, b = FM_CHUNKS[c - MOD_CHUNKS - len(TM_CHUNKS)]
                    src = d["w_in_fm"][bass.ds(lay, 1), :, :, a:b]
                    w = b - a
                sp.dma_start(p.wring[:, c % 3, :, 0:w], src.rearrange("a p k n -> p (a k) n")).then_inc(wsem[c % 3], 16)

        @block.scalar
        def _(act):
            for t in range(NT):
                if t >= 1:
                    act.wait_ge(sem("square1"), t)
                nc.scalar.activation(p.junk[:, :], p.x[:, t, :], ACT.Square,
                                     accum_out=p.ss1[:, t:t + 1]).then_inc(sem("square1"), 1)
            act.wait_ge(sem("square1"), NT)
            nc.scalar.activation(p.rt1[:, 0:NT], p.ss1[:, 0:NT], ACT.Sqrt, bias=p.eps[:, 0:1],
                                 scale=1.0 / D).then_inc(sem("root1"), 1)
            for j, (kind, c, i, a, b) in enumerate(jobs):
                if j % 2 == 0:
                    act.wait_ge(sem("proj"), j + 1)
                    dst, src = proj_evac(p, j, kind, i, a, b)
                    nc.scalar.activation(dst, src, ACT.Copy).then_inc(sem("proj_out_act"), 1)

        @block.vector
        def _(dve):
            own = Chain(dve, sem("dve_mod"))
            nc.vector.memset(p.qkvT[:, :, 0:1], 0.0)
            nc.vector.memset(p.qkvT[:, :, 129:131], 0.0)
            nc.vector.memset(p.qkvT[:, :, LINE - 1:LINE], 0.0)
            for c in range(MOD_CHUNKS):
                dve.wait_ge(sem("w_used"), c + 1)
                if c >= 2:
                    dve.wait_ge(sem("mod_turned"), c - 1)
                nc.vector.tensor_copy(p.mrow[0:2, c % 2, :], ps[5 + c % 2][0:2, :]).then_inc(sem("mod_row"), 1)
            dve.wait_ge(sem("root1"), 1)
            own.link(nc.vector.reciprocal(p.rt1[:, 0:NT], p.rt1[:, 0:NT]))
            dve.wait_ge(sem("load_vec"), 16)
            dve.wait_ge(sem("mod_turned"), MOD_CHUNKS)
            own.link(nc.vector.tensor_tensor(p.mod[:, :, :], ps[0][:, 0:96].rearrange("p (n g) -> p n g", g=2),
                                             bc(p.vec[:, V_BMOD:V_BMOD + 48], 2, 2), ALU.add))
            own.mark(nc.vector.scalar_tensor_tensor(out=p.A1[:, :, :], in0=p.mod[:, 8:16, :], scalar=1.0,
                                                    in1=bc(p.vec[:, V_G1:V_G1 + 8], 2, 2), op0=ALU.add, op1=ALU.mult))
            own.link(nc.vector.scalar_tensor_tensor(out=p.A2[:, :, :], in0=p.mod[:, 32:40, :], scalar=1.0,
                                                    in1=bc(p.vec[:, V_G2:V_G2 + 8], 2, 2), op0=ALU.add, op1=ALU.mult))

            def scaled(t):
                if t >= 2:
                    dve.wait_ge(sem("turned1"), t - 1)
                nc.vector.tensor_scalar(p.xn[:, t % 2, :], p.x[:, t, :], p.rt1[:, t:t + 1], None,
                                        ALU.mult).then_inc(sem("scaled1"), 1)

            scaled(0)
            for t in range(NT):
                if t + 1 < NT:
                    scaled(t + 1)
                dve.wait_ge(sem("turned1"), t + 1)
                g = 0 if t == 0 else 1
                for k in range(KT):
                    nc.vector.tensor_scalar(p.hT[:, k, t * P:(t + 1) * P],
                                            ps[1 + 2 * (t % 2) + k // 4][:, (k % 4) * P:(k % 4 + 1) * P],
                                            p.A1[:, k, g:g + 1], p.mod[:, k, g:g + 1],
                                            ALU.mult, ALU.add).then_inc(sem("h_ready"), 1)
            for j, (kind, c, i, a, b) in enumerate(jobs):
                if j % 2 == 1:
                    dve.wait_ge(sem("proj"), j + 1)
                    dst, src = proj_evac(p, j, kind, i, a, b)
                    nc.vector.tensor_copy(dst, src).then_inc(sem("proj_out_dve"), 1)

        @block.tensor
        def _(pe):
            for c in range(MOD_CHUNKS + 1):
                if c < MOD_CHUNKS:
                    w_arrived(pe, c)
                    if c >= 2:
                        pe.wait_ge(sem("mod_row"), c - 1)
                    for k in range(KT):
                        last = nc.tensor.matmul(ps[5 + c % 2][0:2, :], p.sc[:, k, :], p.wring[:, c % 3, k, :],
                                                start=(k == 0), stop=(k == KT - 1))
                    last.then_inc(sem("w_used"), 1)
                if c >= 1:
                    pe.wait_ge(sem("mod_row"), c)
                    for b in range(4):
                        col = 2 * (4 * (c - 1) + b)
                        last = nc.tensor.transpose(ps[0][:, col:col + 2], p.mrow[0:2, (c - 1) % 2, b * P:(b + 1) * P],
                                                   p.ident[0:2, 0:2])
                    last.then_inc(sem("mod_turned"), 1)
            for t in range(NT):
                pe.wait_ge(sem("scaled1"), t + 1)
                if t >= 2:
                    pe.wait_ge(sem("h_ready"), KT * (t - 1))
                for k in range(KT):
                    last = nc.tensor.transpose(ps[1 + 2 * (t % 2) + k // 4][:, (k % 4) * P:(k % 4 + 1) * P],
                                               p.xn[:, t % 2, k * P:(k + 1) * P], p.ident)
                last.then_inc(sem("turned1"), 1)
            chunk = -1
            for j, (kind, c, i, a, b) in enumerate(jobs):
                if c != chunk:
                    w_arrived(pe, c)
                    chunk = c
                if j == 0:
                    pe.wait_ge(sem("h_ready"), KT * NT)
                if j >= 8:
                    pe.wait_ge(sem("proj_out_act" if j % 2 == 0 else "proj_out_dve"), (j - 8) // 2 + 1)
                bank = ps[j % 8]
                for k in range(KT):
                    if kind == "tm":
                        last = nc.tensor.matmul(bank[:, 0:b - a], p.hT[:, k, i * P:(i + 1) * P],
                                                p.wring[:, c % 3, k, 0:b - a], start=(k == 0), stop=(k == KT - 1))
                    else:
                        lo, hi = (0, P) if i == 0 else (P, TOK)
                        last = nc.tensor.matmul(bank[:, 0:hi - lo], p.wring[:, c % 3, k, b * P:(b + 1) * P],
                                                p.hT[:, k, lo:hi], start=(k == 0), stop=(k == KT - 1))
                last.then_inc(sem("proj"), 1)


def proj_evac(p, j, kind, i, a, b):
    bank = p.ps[j % 8]
    if kind == "tm":
        return p.proj[:, i, a:b], bank[:, 0:b - a]
    if i == 0:
        return p.qkvT[:, a, 1:1 + P], bank[:, 0:P]
    return p.qkvT[:, a, 131:131 + 4 * P], bank[:, :]


def conv(p):
    nc, sem, ps = p.nc, p.sem, p.ps
    with nc.Block() as block:
        @block.vector
        def _(dve):
            own = Chain(dve, sem("dve_conv"))
            for pair in range(3):
                for tap in range(3):
                    for b in (2 * pair, 2 * pair + 1):
                        w = p.vec[:, V_CONV + 3 * b + tap:V_CONV + 3 * b + tap + 1]
                        x = p.qkvT[:, b, tap:tap + LINE - 2]
                        if tap == 0:
                            n = own.mark(nc.vector.tensor_scalar(p.convd[:, b, :], x, w, None, ALU.mult))
                        else:
                            own.wait(6 * pair + 2 * tap - 1 + b % 2)
                            n = own.mark(nc.vector.scalar_tensor_tensor(
                                out=p.convd[:, b, :], in0=x, scalar=w, in1=p.convd[:, b, :],
                                op0=ALU.mult, op1=ALU.add))

        @block.scalar
        def _(act):
            for b in range(6):
                act.wait_ge(sem("dve_conv"), 6 * (b // 2) + 5 + b % 2)
                nc.scalar.activation(p.convd[:, b, :], p.convd[:, b, :], ACT.Silu).then_inc(sem("conv_silu"), 1)
            nc.scalar.activation(p.proj[:, :, GATE:BF], p.proj[:, :, GATE:BF], ACT.Silu).then_inc(sem("gate_silu"), 1)
            act.wait_ge(sem("gate_silu"), 1)
            for t in range(NT):
                for h, (a, b) in enumerate(((0, 512), (512, 768))):
                    act.wait_ge(sem("conv_turned"), 2 * t + h + 1)
                    nc.scalar.activation(p.qkv[:, t, a:b], ps[(2 * t + h) % 8][:, 0:b - a],
                                         ACT.Copy).then_inc(sem("qkv_out"), 1)

        @block.tensor
        def _(pe):
            for t in range(NT):
                lo = 0 if t == 0 else 130 + P * (t - 1)
                for h, (a, b) in enumerate(((0, 4), (4, 6))):
                    j = 2 * t + h
                    pe.wait_ge(sem("conv_silu"), b)
                    if j >= 8:
                        pe.wait_ge(sem("qkv_out"), j - 7)
                    for k in range(a, b):
                        last = nc.tensor.transpose(ps[j % 8][:, (k - a) * P:(k - a + 1) * P],
                                                   p.convd[:, k, lo:lo + P], p.ident)
                    last.then_inc(sem("conv_turned"), 1)


def delta(p, lay):
    nc, sem, ps = p.nc, p.sem, p.ps
    steps = [(0, 0)] + [(t, NT - t) for t in range(1, NT)]

    def tile_of(s, d):
        return steps[s][d]

    def heads(ap, n=HC):
        return ap.rearrange("p (h n) -> p h n", h=n)

    with nc.Block() as block:
        @block.sync
        def _(sp):
            sp.wait_ge(sem("states_zero"), 1)
            sp.wait_ge(sem("step0"), 1)
            sp.wait_ge(sem("step1"), 1)
            for d, name in enumerate(("sf", "sb")):
                sp.dma_start(p.d["out_" + name][bass.ds(lay, 1)].rearrange("l h d v -> d (l h) v"),
                             p.state[:, d, :, :]).then_inc(sem("store"), 16)
            sp.wait_ge(sem("store"), 32)
            for d, name in enumerate(("sf", "sb")):
                sp.dma_start(p.state[:, d, :, :],
                             p.d["in_" + name][bass.ds(lay, 1)].rearrange("l h d v -> d (l h) v")).then_inc(sem("load_state"), 16)

        @block.gpsimd
        def _(pool):
            nc.gpsimd.memset(p.state[:, :, :, :], 0.0).then_inc(sem("states_zero"), 1)
            for s in range(NT):
                for lvl in range(1, LEVELS):
                    for d in range(2):
                        pool.wait_ge(sem(f"lt_ready{d}"), s + 1)
                        n = doubling(s, lvl)
                        if n >= 2:
                            pool.wait_ge(sem(f"t1{d}"), n - 1)
                        nc.gpsimd.tensor_tensor(p.mlt[:, d, lvl_buf(n), :, :], p.lt[:, d, :, :],
                                                bc(p.lmask[:, d, lvl, :], 1, HC), ALU.mult).then_inc(sem(f"mlt{d}"), 1)

        @block.scalar
        def _(act):
            act.wait_ge(sem("squares_d"), NT)
            nc.scalar.activation(p.rd[:, :, :], p.ssd[:, :, :], ACT.Sqrt, bias=p.eps[:, 0:1]).then_inc(sem("root_d"), 1)
            act.wait_ge(sem("zabs"), 1)
            nc.scalar.activation(p.sp1[:, :, :], p.zab[:, :, :], ACT.Exp, scale=-1.0).then_inc(sem("exp_small"), 1)
            nc.scalar.activation(p.bet[:, :, :], p.proj[:, :, BF:BF + 8], ACT.Exp, scale=-1.0).then_inc(sem("exp_small"), 1)
            nc.scalar.activation(p.eal[:, :], p.row[:, R_ALOG:R_ALOG + 8], ACT.Exp).then_inc(sem("exp_small"), 1)
            act.wait_ge(sem("exp_small"), 3)
            nc.scalar.activation(p.sp1[:, :, :], p.sp1[:, :, :], ACT.Ln, bias=p.one[:, 0:1]).then_inc(sem("ln_small"), 1)
            act.wait_ge(sem("gcol_out"), 1)
            nc.scalar.activation(p.egc[:, :, :], p.gcol[:, :, :], ACT.Exp).then_inc(sem("egc"), 1)
            for s in range(NT):
                for d in range(2):
                    act.wait_ge(sem(f"kq_turned{d}"), s + 1)
                    if s >= 1:
                        act.wait_ge(sem(f"kk{d}"), s)
                    nc.scalar.activation(p.kT[:, d, :], ps[4 * d + 2][0:64, :], ACT.Copy).then_inc(sem(f"kqT{d}"), 1)
                    nc.scalar.activation(p.qT[:, d, :], ps[4 * d + 3][0:64, :], ACT.Copy).then_inc(sem(f"kqT{d}"), 1)
                for d in range(2):
                    act.wait_ge(sem(f"diff{d}"), s + 1)
                    if s >= 1:
                        act.wait_ge(sem(f"prep{d}"), 4 * s)
                    nc.scalar.activation(p.dec[:, d, :, :], p.dif[:, d, :, :], ACT.Exp).then_inc(sem(f"dec{d}"), 1)
                    if s >= 1:
                        act.wait_ge(sem(f"step{d}"), s)
                    nc.scalar.activation(p.egr[:, d, :, :], heads(ps[4 * d][0:64, :]), ACT.Exp).then_inc(sem(f"egr{d}"), 1)
                for d in range(2):
                    act.wait_ge(sem(f"x_turned{d}"), s + 1)
                    nc.scalar.activation(p.X[:, d, :, :], heads(ps[4 * d][:, :]), ACT.Copy).then_inc(sem(f"first_x{d}"), 1)
                for lvl in range(1, LEVELS):
                    for d in range(2):
                        n = doubling(s, lvl)
                        act.wait_ge(sem(f"t1{d}"), n + 1)
                        if n >= 1:
                            act.wait_ge(sem(f"t2{d}"), n)
                        nc.scalar.activation(p.t1s[:, d, :], ps[4 * d][:, :], ACT.Copy).then_inc(sem(f"t1s{d}"), 1)
            act.wait_ge(sem("squares_o"), NT)
            nc.scalar.activation(p.sso[:, :, :], p.sso[:, :, :], ACT.Sqrt, bias=p.eps[:, 0:1],
                                 scale=1.0 / 64).then_inc(sem("root_o"), 1)

        @block.vector
        def _(dve):
            own = Chain(dve, sem("dve_delta"))
            nc.vector.memset(p.oC[:, :, :], 0.0)
            for t in range(NT):
                if t >= 1:
                    dve.wait_ge(sem("squares_d"), t)
                own.link(nc.vector.tensor_tensor(p.junk[:, 0:512], p.qkv[:, t, 0:512], p.qkv[:, t, 0:512], ALU.mult))
                nc.vector.tensor_reduce(p.ssd[:, t, :], heads(p.junk[:, 0:512], 8), AX.X, ALU.add).then_inc(sem("squares_d"), 1)
            own.link(nc.vector.tensor_tensor(p.zz[:, :, :], p.proj[:, :, BF + 8:BF + 16],
                                             bc(p.row[:, R_DT:R_DT + 8], 1, NT), ALU.add))
            nc.vector.scalar_tensor_tensor(out=p.zab[:, :, :], in0=p.zz[:, :, :], scalar=-1.0, in1=p.zz[:, :, :],
                                           op0=ALU.mult, op1=ALU.max).then_inc(sem("zabs"), 1)
            dve.wait_ge(sem("root_d"), 1)
            own.link(nc.vector.reciprocal(p.rd[:, :, :], p.rd[:, :, :]))
            own.link(nc.vector.tensor_scalar(p.rd[:, :, 0:4], p.rd[:, :, 0:4], 0.125, None, ALU.mult))
            for t in range(NT):
                nc.vector.tensor_tensor(heads(p.qkv[:, t, 0:512], 8), heads(p.qkv[:, t, 0:512], 8),
                                        bc(p.rd[:, t, :], 2, 64), ALU.mult).then_inc(sem("qk_unit"), 1)
            dve.wait_ge(sem("exp_small"), 3)
            own.link(nc.vector.tensor_scalar(p.bet[:, :, :], p.bet[:, :, :], 1.0, None, ALU.add))
            own.link(nc.vector.reciprocal(p.bet[:, :, :], p.bet[:, :, :]))
            dve.wait_ge(sem("ln_small"), 1)
            own.link(nc.vector.scalar_tensor_tensor(out=p.g[:, :, :], in0=p.zz[:, :, :], scalar=0.0, in1=p.sp1[:, :, :],
                                                    op0=ALU.max, op1=ALU.add))
            nc.vector.scalar_tensor_tensor(out=p.g[:, :, :], in0=p.g[:, :, :], scalar=-1.0, in1=bc(p.eal[:, :], 1, NT),
                                           op0=ALU.mult, op1=ALU.mult).then_inc(sem("g_ready"), 1)
            dve.wait_ge(sem("gcol"), 1)
            nc.vector.tensor_copy(p.gcol[:, :, :], ps[0][:, 0:NT * 8].rearrange("p (t c) -> p t c", t=NT)).then_inc(sem("gcol_out"), 1)
            dve.wait_ge(sem("egc"), 1)
            for s in range(NT):
                for d in range(2):
                    t, c = tile_of(s, d), 4 * d
                    dve.wait_ge(sem(f"rows{d}"), s + 1)
                    own.link(nc.vector.tensor_tensor(p.dif[:, d, :, :], heads(ps[4 * d][:, :]),
                                                     bc(p.gcol[:, t, c:c + 4], 2, P), ALU.subtract))
                    nc.vector.tensor_scalar(p.dif[:, d, :, :], p.dif[:, d, :, :], 0.0, None, ALU.min).then_inc(sem(f"diff{d}"), 1)
                for d in range(2):
                    t, c = tile_of(s, d), 4 * d
                    dve.wait_ge(sem(f"dec{d}"), s + 1)
                    own.link(nc.vector.tensor_tensor(p.lt[:, d, :, :], p.dec[:, d, :, :], bc(p.bet[:, t, c:c + 4], 2, P), ALU.mult))
                    dve.wait_ge(sem(f"kk{d}"), s + 1)
                    nc.vector.tensor_tensor(p.lt[:, d, :, :], heads(ps[4 * d + 2][:, :]), p.lt[:, d, :, :], ALU.mult).then_inc(sem(f"lt_ready{d}"), 1)
                    dve.wait_ge(sem(f"lt_ready{d}"), s + 1)
                    own.link(nc.vector.tensor_tensor(p.XT[:, d, :, :], p.lt[:, d, :, :], bc(p.lmask[:, d, 0, :], 1, HC), ALU.mult))
                    nc.vector.tensor_tensor(p.XT[:, d, :, :], bc(p.ident, 1, HC), p.XT[:, d, :, :], ALU.subtract).then_inc(sem(f"x{d}"), 1)
                for d in range(2):
                    t = tile_of(s, d)
                    last = P - 1 if d == 0 else 0
                    kh = heads(p.qkv[:, t, 256:512])
                    nc.vector.tensor_tensor(p.kd[:, d, :, :], kh, p.dec[:, d, :, last:last + 1].to_broadcast([P, HC, 64]),
                                            ALU.mult).then_inc(sem(f"prep{d}"), 1)
                    own.link(nc.vector.tensor_tensor(p.qk[:, d, :, :], heads(ps[4 * d + 3][:, :]), p.dec[:, d, :, :], ALU.mult))
                    nc.vector.tensor_tensor(p.qk[:, d, :, :], p.qk[:, d, :, :], bc(p.imask[:, d, :], 1, HC), ALU.mult).then_inc(sem(f"prep{d}"), 1)
                    dve.wait_ge(sem(f"egr{d}"), s + 1)
                    dve.wait_ge(sem(f"kqT{d}"), 2 * s + 2)
                    nc.vector.tensor_tensor(p.qd[:, d, :, :], heads(p.qT[:, d, :]), p.egr[:, d, :, :], ALU.mult).then_inc(sem(f"prep{d}"), 1)
                for lvl in range(1, LEVELS):
                    for d in range(2):
                        n = doubling(s, lvl)
                        if lvl == KS_LEVEL + 1:
                            t, c = tile_of(s, d), 4 * d
                            dve.wait_ge(sem(f"ks{d}"), s + 1)
                            own.link(nc.vector.tensor_tensor(p.rv[:, d, :, :], heads(ps[4 * d + 2][:, 0:256]),
                                                             bc(p.egc[:, t, c:c + 4], 2, 64), ALU.mult))
                            nc.vector.tensor_tensor(p.rv[:, d, :, :], heads(p.qkv[:, t, 512:768]), p.rv[:, d, :, :],
                                                    ALU.subtract).then_inc(sem(f"prep{d}"), 1)
                        dve.wait_ge(sem(f"t2{d}"), n + 1)
                        if lvl < LEVELS - 1:
                            nc.vector.tensor_tensor(p.X[:, d, :, :], p.X[:, d, :, :], heads(ps[4 * d][:, :]), ALU.subtract).then_inc(sem(f"x{d}"), 1)
                        nc.vector.tensor_tensor(p.XT[:, d, :, :], p.XT[:, d, :, :], heads(ps[4 * d + 1][:, :]), ALU.subtract).then_inc(sem(f"x{d}"), 1)
                for d in range(2):
                    t, c = tile_of(s, d), 4 * d
                    dve.wait_ge(sem(f"w{d}"), s + 1)
                    nc.vector.tensor_tensor(p.w[:, d, :, :], heads(ps[4 * d + 1][:, 0:256]),
                                            bc(p.bet[:, t, c:c + 4], 2, 64), ALU.mult).then_inc(sem(f"w_out{d}"), 1)
                if s == 1:
                    dve.wait_ge(sem("load_state"), 32)
                for d in range(2):
                    t = tile_of(s, d)
                    last = P - 1 if d == 0 else 0
                    dve.wait_ge(sem(f"od{d}"), s + 1)
                    own.link(nc.vector.tensor_tensor(p.oC[:, t, :], p.oC[:, t, :], ps[4 * d + 1][:, 256:512], ALU.add))
                    own.link(nc.vector.tensor_tensor(p.state[:, d, :, :], p.state[:, d, :, :],
                                                     p.egr[:, d, :, last:last + 1].to_broadcast([64, HC, 64]), ALU.mult))
                    nc.vector.tensor_tensor(p.state[:, d, :, :], p.state[:, d, :, :], heads(ps[4 * d + 2][0:64, 0:256]),
                                            ALU.add).then_inc(sem(f"step{d}"), 1)
            own.wait(own.n)
            sq = p.junk[:, 0:256].rearrange("p (h n) -> p h n", h=4)
            for t in range(NT):
                if t >= 1:
                    dve.wait_ge(sem("squares_o"), t)
                own.link(nc.vector.tensor_tensor(p.junk[:, 0:256], p.oC[:, t, :], p.oC[:, t, :], ALU.mult))
                nc.vector.tensor_reduce(p.sso[:, t, :], sq, AX.X, ALU.add).then_inc(sem("squares_o"), 1)
            dve.wait_ge(sem("root_o"), 1)
            own.link(nc.vector.reciprocal(p.sso[:, :, :], p.sso[:, :, :]))
            for t in range(NT):
                o = heads(p.oC[:, t, :])
                own.link(nc.vector.tensor_tensor(o, o, bc(p.sso[:, t, :], 2, 64), ALU.mult))
                own.link(nc.vector.tensor_tensor(o, o, bc(p.row[:, R_ON:R_ON + 64], 1, HC), ALU.mult))
                own.mark(nc.vector.tensor_tensor(p.mixed[:, t, 768:1024], p.oC[:, t, :], p.proj[:, t, GATE:BF], ALU.mult))

        @block.tensor
        def _(pe):
            pe.wait_ge(sem("g_ready"), 1)
            for t in range(NT):
                for d in range(2):
                    last = nc.tensor.matmul(ps[0][:, 8 * t + 4 * d:8 * t + 4 * d + 4], p.imask[:, d, :],
                                            p.g[:, t, 4 * d:4 * d + 4], start=True, stop=True)
            last.then_inc(sem("gcol"), 1)
            pe.wait_ge(sem("gcol_out"), 1)
            pe.wait_ge(sem("qk_unit"), NT)
            for s in range(NT):
                for d in range(2):
                    t = tile_of(s, d)
                    B = ps[4 * d:4 * d + 4]
                    if s >= 1:
                        pe.wait_ge(sem(f"step{d}"), s)
                    for h in range(HC):
                        nc.tensor.transpose(B[2][0:64, h * P:(h + 1) * P], p.qkv[:, t, 256 + 64 * h:320 + 64 * h], p.ident)
                    for h in range(HC):
                        mm = nc.tensor.transpose(B[3][0:64, h * P:(h + 1) * P], p.qkv[:, t, 64 * h:64 * h + 64], p.ident)
                    mm.then_inc(sem(f"kq_turned{d}"), 1)
                    for h in range(HC):
                        mm = nc.tensor.matmul(B[0][:, h * P:(h + 1) * P], p.g[:, t, 4 * d + h:4 * d + h + 1].to_broadcast([P, P]),
                                              p.imask[:, d, :], start=True, stop=True)
                    mm.then_inc(sem(f"rows{d}"), 1)
                for d in range(2):
                    B = ps[4 * d:4 * d + 4]
                    pe.wait_ge(sem(f"kqT{d}"), 2 * s + 2)
                    for h in range(HC):
                        k = p.kT[:, d, h * P:(h + 1) * P]
                        nc.tensor.matmul(B[2][:, h * P:(h + 1) * P], k, k, start=True, stop=True)
                    for h in range(HC):
                        mm = nc.tensor.matmul(B[3][:, h * P:(h + 1) * P], p.kT[:, d, h * P:(h + 1) * P],
                                              p.qT[:, d, h * P:(h + 1) * P], start=True, stop=True)
                    mm.then_inc(sem(f"kk{d}"), 1)
                for d in range(2):
                    pe.wait_ge(sem(f"x{d}"), X_STEPS * s + 1)
                    pe.wait_ge(sem(f"egr{d}"), s + 1)
                    for h in range(HC):
                        mm = nc.tensor.transpose(ps[4 * d][:, h * P:(h + 1) * P], p.XT[:, d, h, :], p.ident)
                    mm.then_inc(sem(f"x_turned{d}"), 1)
                for lvl in range(1, LEVELS):
                    for d in range(2):
                        B = ps[4 * d:4 * d + 4]
                        n = doubling(s, lvl)
                        pe.wait_ge(sem(f"mlt{d}"), n + 1)
                        if lvl == 1:
                            pe.wait_ge(sem(f"first_x{d}"), s + 1)
                        else:
                            pe.wait_ge(sem(f"x{d}"), X_STEPS * s + 1 + 2 * (lvl - 1))
                        for h in range(HC):
                            mm = nc.tensor.matmul(B[0][:, h * P:(h + 1) * P], p.mlt[:, d, lvl_buf(n), h, :],
                                                  p.X[:, d, h, :], start=True, stop=True)
                        mm.then_inc(sem(f"t1{d}"), 1)
                        if lvl == KS_LEVEL:
                            if s == 0:
                                pe.wait_ge(sem("states_zero"), 1)
                            if s == 1:
                                pe.wait_ge(sem("load_state"), 32)
                            for h in range(HC):
                                mm = nc.tensor.matmul(B[2][:, h * 64:h * 64 + 64], p.kT[:, d, h * P:(h + 1) * P],
                                                      p.state[:, d, h, :], start=True, stop=True)
                            mm.then_inc(sem(f"ks{d}"), 1)
                    for d in range(2):
                        B = ps[4 * d:4 * d + 4]
                        n = doubling(s, lvl)
                        pe.wait_ge(sem(f"t1s{d}"), n + 1)
                        if lvl < LEVELS - 1:
                            for h in range(HC):
                                nc.tensor.matmul(B[0][:, h * P:(h + 1) * P], p.XT[:, d, h, :],
                                                 p.t1s[:, d, h * P:(h + 1) * P], start=True, stop=True)
                        for h in range(HC):
                            mm = nc.tensor.matmul(B[1][:, h * P:(h + 1) * P], p.t1s[:, d, h * P:(h + 1) * P],
                                                  p.XT[:, d, h, :], start=True, stop=True)
                        mm.then_inc(sem(f"t2{d}"), 1)
                for d in range(2):
                    B = ps[4 * d:4 * d + 4]
                    pe.wait_ge(sem(f"prep{d}"), 4 * (s + 1))
                    pe.wait_ge(sem(f"x{d}"), X_STEPS * (s + 1))
                    for h in range(HC):
                        mm = nc.tensor.matmul(B[1][:, h * 64:h * 64 + 64], p.XT[:, d, h, :], p.rv[:, d, h, :], start=True, stop=True)
                    mm.then_inc(sem(f"w{d}"), 1)
                for d in range(2):
                    B = ps[4 * d:4 * d + 4]
                    pe.wait_ge(sem(f"w_out{d}"), s + 1)
                    for h in range(HC):
                        o = B[1][:, 256 + h * 64:320 + h * 64]
                        nc.tensor.matmul(o, p.qd[:, d, h, :], p.state[:, d, h, :], start=True, stop=False)
                        nc.tensor.matmul(o, p.qk[:, d, h, :], p.w[:, d, h, :], start=False, stop=True)
                    for h in range(HC):
                        mm = nc.tensor.matmul(B[2][0:64, h * 64:h * 64 + 64], p.kd[:, d, h, :], p.w[:, d, h, :],
                                              start=True, stop=True)
                    mm.then_inc(sem(f"od{d}"), 1)


def doubling(s, lvl):
    return (LEVELS - 1) * s + lvl - 1


def lvl_buf(n):
    return n % 2


def prepare_attention(p, lay):
    nc, d, sem, ps = p.nc, p.d, p.sem, p.ps

    def rope(own, dve, x, n, t):
        cos, sin = p.rope[:, 0, t - 1, :], p.rope[:, 1, t - 1, :]
        u = p.ru[:, 0:n * 32].rearrange("p (n c) -> p n c", c=32)
        v = p.rv2[:, 0:n * 32].rearrange("p (n c) -> p n c", c=32)
        for half in range(2):
            for q in range(2):
                a, b = 16 * half + 8 * q, 16 * half + 8 * (1 - q)
                own.mark(nc.vector.tensor_tensor(u[:, :, a:a + 8], x[:, :, b:b + 8], bc(sin[:, a:a + 8], 1, n), ALU.mult))
        own.link(nc.vector.tensor_tensor(v, x, bc(cos, 1, n), ALU.mult))
        return nc.vector.tensor_tensor(x, u, v, ALU.add)

    jobs = []
    for t in range(NT):
        jobs += [("qk", t, 0), ("low", t, 0)]
    jobs += [("qk", NT, 0), ("low", NT, 0)]
    for h in range(HB):
        jobs += [("kn", h, 0), ("kn", h, 1)]
    jobs += [("v", t, 0) for t in range(6)]
    for t in range(NT):
        jobs += [("uq", t, 0), ("uq", t, 1), ]
        if t >= 1:
            jobs += [("qt", t - 1, 0), ("qt", t - 1, 1)]
    jobs += [("qt", NT - 1, 0), ("qt", NT - 1, 1)]
    at = {job: j for j, job in enumerate(jobs)}

    with nc.Block() as block:
        @block.sync
        def _(sp):
            one = bass.ds(lay, 1)
            sp.dma_start(p.cak[:, :], d["cache_a_k"][one].rearrange("l p n -> p (l n)")).then_inc(sem("load_cache"), 16)
            sp.dma_start(p.cav[:, :], d["cache_a_v"][one].rearrange("l p n -> p (l n)")).then_inc(sem("load_cache"), 16)
            sp.dma_start(p.cckv[:, :], d["cache_ckv"][one].rearrange("l p n -> p (l n)")).then_inc(sem("load_cache"), 16)
            sp.dma_start(p.ckr[:, 64:96], d["cache_kr"][one].rearrange("l p n -> p (l n)")).then_inc(sem("load_cache"), 16)
            sp.dma_start(p.wuq[:, :, :], d["w_uq"][one].rearrange("l p k n -> p (l k) n")).then_inc(sem("load_wuq"), 16)
            sp.dma_start(p.wukn[:, :], d["w_ukn"][one].rearrange("l p n -> p (l n)")).then_inc(sem("load_wuk"), 16)
            sp.dma_start(p.wukv[:, :], d["w_ukv"][one].rearrange("l p n -> p (l n)")).then_inc(sem("load_wuk"), 16)
            sp.dma_start(d["out_ak"][one].rearrange("l p n -> p (l n)"), p.proj[:, 0, KA:VA]).then_inc(sem("store_ctx"), 16)
            sp.dma_start(d["out_av"][one].rearrange("l p n -> p (l n)"), p.proj[:, 0, VA:QC]).then_inc(sem("store_ctx"), 16)
            sp.wait_ge(sem("low_norm"), 1)
            sp.dma_start(d["out_ckv"][one].rearrange("l p n -> p (l n)"), p.proj[:, 0, KVC:KR]).then_inc(sem("store_ctx"), 16)
            sp.dma_start(d["out_kr"][one].rearrange("l p n -> p (l n)"), p.proj[:, 0, KR:GATE]).then_inc(sem("store_ctx"), 16)
            sp.wait_ge(sem("store_ctx"), 64)

        @block.gpsimd
        def _(pool):
            nc.gpsimd.memset(p.krp[:, :, 0:64], 0.0).then_inc(sem("pads"), 1)
            nc.gpsimd.memset(p.ckr[:, 0:64], 0.0).then_inc(sem("pads"), 1)

        @block.scalar
        def _(act):
            act.wait_ge(sem("squares_l"), 2 * NT)
            nc.scalar.activation(p.rl[:, 0, :], p.ssl[:, 0, :], ACT.Sqrt, bias=p.eps[:, 0:1], scale=1.0 / 256).then_inc(sem("root_l"), 1)
            nc.scalar.activation(p.rl[:, 1, :], p.ssl[:, 1, :], ACT.Sqrt, bias=p.eps[:, 0:1], scale=1.0 / 128).then_inc(sem("root_l"), 1)
            for j, (kind, t, half) in enumerate(jobs):
                b = ps[j % 8]
                act.wait_ge(sem("p_mm"), j + 1)
                tc, kc = (t * P, kcol(t) if t < NT else P)
                if kind == "qk":
                    if t < NT:
                        nc.scalar.activation(p.qTa[:, :, tc:tc + P], b[:, 0:256].rearrange("p (b n) -> p b n", b=2), ACT.Copy)
                    last = nc.scalar.activation(p.kTa[:, :, kc:kc + P], b[:, 256:512].rearrange("p (b n) -> p b n", b=2), ACT.Copy)
                elif kind == "low":
                    if t < NT:
                        nc.scalar.activation(p.qcT[:, :, tc:tc + P], b[:, 0:256].rearrange("p (b n) -> p b n", b=2), ACT.Copy)
                    nc.scalar.activation(p.ckvT[:, kc:kc + P], b[:, 256:384], ACT.Copy)
                    last = nc.scalar.activation(p.kTb[64:96, :, kc:kc + P], bc(b[64:96, 384:512], 1, HB), ACT.Copy)
                elif kind == "kn":
                    lo, hi = (0, 512) if half == 0 else (512, KEYS)
                    last = nc.scalar.activation(p.kTb[0:64, t, lo:hi], b[0:64, 0:hi - lo], ACT.Copy)
                elif kind == "v":
                    last = nc.scalar.activation(p.vb[:, t, :], b[:, :], ACT.Copy)
                elif kind == "uq":
                    if t >= 2:
                        act.wait_ge(sem("p_mm"), at[("qt", t - 2, 1)] + 1)
                    last = nc.scalar.activation(p.qb[:, t % 2, half * 384:half * 384 + 384], b[:, 0:384], ACT.Copy)
                else:
                    last = nc.scalar.activation(p.qTb[:, 4 * half:4 * half + 4, tc:tc + P],
                                                b[0:96, :].rearrange("p (h n) -> p h n", h=4), ACT.Copy)
                last.then_inc(sem("p_ev"), 1)

        @block.vector
        def _(dve):
            own = Chain(dve, sem("dve_prep"))
            for t in range(NT):
                if t >= 1:
                    dve.wait_ge(sem("squares_l"), 2 * t)
                for i, (a, b) in enumerate(((QC, KVC), (KVC, KR))):
                    nc.vector.tensor_tensor_reduce(out=p.junk[:, 256 * i:256 * i + b - a], in0=p.proj[:, t, a:b], in1=p.proj[:, t, a:b],
                                                   scale=1.0, scalar=0.0, op0=ALU.mult, op1=ALU.add,
                                                   accum_out=p.ssl[:, i, t:t + 1]).then_inc(sem("squares_l"), 1)
            for i in range(2):
                q1 = R_LAM + 64 * i
                nc.vector.tensor_tensor_reduce(out=p.junk[:, 512 + 32 * i:544 + 32 * i], in0=p.row[:, q1:q1 + 32], in1=p.row[:, q1 + 32:q1 + 64],
                                               scale=1.0, scalar=0.0, op0=ALU.mult, op1=ALU.add,
                                               accum_out=p.lam[:, i:i + 1]).then_inc(sem("lam_dot"), 1)
            dve.wait_ge(sem("root_l"), 2)
            own.link(nc.vector.reciprocal(p.rl[:, :, :], p.rl[:, :, :]))
            for t in range(NT):
                nc.vector.scalar_tensor_tensor(out=p.proj[:, t, KVC:KR], in0=p.proj[:, t, KVC:KR], scalar=p.rl[:, 1, t:t + 1],
                                               in1=p.row[:, R_KVC:R_KVC + 128], op0=ALU.mult, op1=ALU.mult).then_inc(sem("low_norm"), 1)
                nc.vector.scalar_tensor_tensor(out=p.proj[:, t, QC:KVC], in0=p.proj[:, t, QC:KVC], scalar=p.rl[:, 0, t:t + 1],
                                               in1=p.row[:, R_QC:R_QC + 256], op0=ALU.mult, op1=ALU.mult).then_inc(sem("low_norm"), 1)
                if t == 0:
                    dve.wait_ge(sem("pads"), 2)
                else:
                    own.wait(own.n)
                    own.link(rope(own, dve, p.proj[:, t, QA:VA].rearrange("p (n c) -> p n c", c=32), 16, t))
                    own.link(rope(own, dve, p.proj[:, t, KR:GATE].rearrange("p (n c) -> p n c", c=32), 1, t))
                nc.vector.tensor_copy(p.krp[:, t, 64:96], p.proj[:, t, KR:GATE]).then_inc(sem("tile_prep"), 1)
            for t in range(1, NT):
                dve.wait_ge(sem("p_ev"), at[("uq", t, 1)] + 1)
                x = p.qb[:, t % 2, :].rearrange("p (h c) -> p h c", c=96)[:, :, 64:96]
                own.wait(own.n)
                rope(own, dve, x, HB, t).then_inc(sem("q_roped"), 1)
                dve.wait_ge(sem("q_roped"), t)

        @block.tensor
        def _(pe):
            for j, (kind, t, half) in enumerate(jobs):
                b = ps[j % 8]
                if j >= 8:
                    pe.wait_ge(sem("p_ev"), j - 7)
                if kind in ("qk", "low"):
                    if t < NT:
                        pe.wait_ge(sem("tile_prep"), t + 1)
                        pe.wait_ge(sem("low_norm"), 2 * t + 2)
                    else:
                        pe.wait_ge(sem("load_cache"), 64)
                        pe.wait_ge(sem("pads"), 2)
                if kind == "qk":
                    cols = ([p.proj[:, t, QA + P * i:QA + P * (i + 1)] for i in range(4)] if t < NT
                            else [None, None, p.cak[:, 0:128], p.cak[:, 128:256]])
                    for i, c in enumerate(cols):
                        if c is not None:
                            last = nc.tensor.transpose(b[:, i * P:(i + 1) * P], c, p.ident)
                elif kind == "low":
                    cols = ([p.proj[:, t, QC:QC + P], p.proj[:, t, QC + P:KVC], p.proj[:, t, KVC:KR], p.krp[:, t, :]] if t < NT
                            else [None, None, p.cckv[:, :], p.ckr[:, :]])
                    for i, c in enumerate(cols):
                        if c is not None:
                            last = nc.tensor.transpose(b[0:c.shape[1], i * P:(i + 1) * P], c, p.ident)
                elif kind == "kn":
                    if (t, half) == (0, 0):
                        pe.wait_ge(sem("load_wuk"), 32)
                        pe.wait_ge(sem("p_ev"), at[("low", NT, 0)] + 1)
                    lo, hi = (0, 512) if half == 0 else (512, KEYS)
                    last = nc.tensor.matmul(b[0:64, 0:hi - lo], p.wukn[:, t * 64:t * 64 + 64], p.ckvT[:, lo:hi], start=True, stop=True)
                elif kind == "v":
                    last = nc.tensor.matmul(b[:, :], p.ckvT[:, t * P:(t + 1) * P], p.wukv[:, :], start=True, stop=True)
                elif kind == "uq":
                    if (t, half) == (0, 0):
                        pe.wait_ge(sem("load_wuq"), 16)
                    for k in range(2):
                        last = nc.tensor.matmul(b[:, 0:384], p.qcT[:, k, t * P:(t + 1) * P], p.wuq[:, k, half * 384:half * 384 + 384],
                                                start=(k == 0), stop=(k == 1))
                else:
                    pe.wait_ge(sem("p_ev"), at[("uq", t, 1)] + 1)
                    if t >= 1:
                        pe.wait_ge(sem("q_roped"), t)
                    for h in range(4):
                        hh = 4 * half + h
                        last = nc.tensor.transpose(b[0:96, h * P:(h + 1) * P], p.qb[:, t % 2, hh * 96:hh * 96 + 96], p.ident)
                last.then_inc(sem("p_mm"), 1)


def attend(p):
    nc, sem, ps = p.nc, p.sem, p.ps
    maps, outs = [], []
    for t in range(NT):
        for h in range(HA):
            maps += [(t, h, 0), (t, h, 1)]
            outs.append(("a", t, h, len(maps)))
        for h in range(HB):
            maps.append((t, h, None))
            outs.append(("b", t, h, len(maps)))
    out_after = {n: (o, kind, t, h) for o, (kind, t, h, n) in enumerate(outs)}

    def keys(t):
        return (0, P) if t == 0 else (P, KEYS)

    def value(kind, t, kt, h):
        if kind == "b":
            return p.vb[:, kt, h * 64:h * 64 + 64]
        if kt == 1:
            return p.cav[:, h * 64:h * 64 + 64]
        return p.proj[:, 0 if kt == 0 else kt - 1, VA + h * 64:VA + h * 64 + 64]

    A, B = 32.0 ** -0.5, 96.0 ** -0.5
    with nc.Block() as block:
        @block.tensor
        def _(pe):
            def scores(m):
                t, h, i = maps[m]
                lo, hi = keys(t)
                s = 2 * (m % 2)
                if m >= 2:
                    pe.wait_ge(sem("a_exp"), m - 1)
                if i is None:
                    q = p.qTb[:, h, t * P:(t + 1) * P]
                    k = p.kTb[:, h, lo:hi]
                else:
                    c = 2 * h + i
                    r = 32 * (c % 4)
                    q = p.qTa[r:r + 32, c // 4, t * P:(t + 1) * P]
                    k = p.kTa[r:r + 32, c // 4, lo:hi]
                n = min(hi - lo, 512)
                last = nc.tensor.matmul(ps[s][:, 0:n], q, k[:, 0:n], start=True, stop=True)
                if hi - lo > 512:
                    last = nc.tensor.matmul(ps[s + 1][:, 0:P], q, k[:, 512:640], start=True, stop=True)
                last.then_inc(sem("a_scores"), 1)

            def turn(o):
                kind, t, h, n = outs[o]
                pe.wait_ge(sem("a_diff") if kind == "a" else sem("a_exp"),
                           t * HA + h + 1 if kind == "a" else n)
                if o >= 1:
                    pe.wait_ge(sem("a_turned_out"), o)
                src = p.prob[:, (n - 1) % 4, :]
                for j in range((keys(t)[1] - keys(t)[0]) // P):
                    last = nc.tensor.transpose(ps[4 + j // 4][:, (j % 4) * P:(j % 4 + 1) * P], src[:, j * P:(j + 1) * P], p.ident)
                last.then_inc(sem("a_turned"), 1)

            def sums(o):
                kind, t, h, n = outs[o]
                pe.wait_ge(sem("a_turned_out"), o + 1)
                if o >= 2:
                    pe.wait_ge(sem("a_out"), o - 1)
                nk = (keys(t)[1] - keys(t)[0]) // P
                for j in range(nk):
                    last = nc.tensor.matmul(ps[6 + o % 2][:, 0:64], p.probT[:, o % 2, j * P:(j + 1) * P],
                                            value(kind, t, j if t == 0 else j + 1, h), start=(j == 0), stop=(j == nk - 1))
                last.then_inc(sem("a_sums"), 1)

            o = 0
            for m in range(len(maps) + 4):
                if m < len(maps):
                    scores(m)
                if m - 1 in out_after:
                    turn(out_after[m - 1][0])
                if m - 2 in out_after:
                    sums(out_after[m - 2][0])

        @block.scalar
        def _(act):
            act.wait_ge(sem("lam_dot"), 2)
            nc.scalar.activation(p.lam[:, 2:4], p.lam[:, 0:2], ACT.Exp).then_inc(sem("lam_exp"), 1)

            def turned_out(o):
                kind, t, h, n = outs[o]
                act.wait_ge(sem("a_turned"), o + 1)
                if o >= 2:
                    act.wait_ge(sem("a_sums"), o - 1)
                nk = (keys(t)[1] - keys(t)[0])
                last = nc.scalar.activation(p.probT[:, o % 2, 0:min(nk, 512)], ps[4][:, 0:min(nk, 512)], ACT.Copy)
                if nk > 512:
                    last = nc.scalar.activation(p.probT[:, o % 2, 512:nk], ps[5][:, 0:P], ACT.Copy)
                last.then_inc(sem("a_turned_out"), 1)

            for m in range(len(maps) + 4):
                if m < len(maps):
                    t, h, i = maps[m]
                    nk = keys(t)[1] - keys(t)[0]
                    act.wait_ge(sem("a_max"), m + 1)
                    if m >= 4:
                        done = [o for o, x in enumerate(outs) if x[3] > m - 4]
                        act.wait_ge(sem("a_turned"), done[0] + 1)
                    s = 2 * (m % 2)
                    sc = p.score2(s, nk)
                    nc.scalar.activation(p.prob[:, m % 4, 0:nk], sc, ACT.Exp, bias=p.nmax[:, m % 4:m % 4 + 1],
                                         scale=B if i is None else A, accum_out=p.esum[:, m % 4:m % 4 + 1]).then_inc(sem("a_exp"), 1)
                if m - 1 in out_after:
                    turned_out(out_after[m - 1][0])
            act.wait_ge(sem("squares_a"), NT)
            nc.scalar.activation(p.ssa[:, :, :], p.ssa[:, :, :], ACT.Sqrt, bias=p.eps[:, 0:1],
                                 scale=1.0 / 64).then_inc(sem("root_a"), 1)

        @block.vector
        def _(dve):
            own = Chain(dve, sem("dve_attend"))
            dve.wait_ge(sem("lam_exp"), 1)
            own.link(nc.vector.tensor_tensor(p.lam[:, 4:5], p.lam[:, 3:4], p.lam[:, 2:3], ALU.subtract))
            own.link(nc.vector.tensor_tensor(p.lam[:, 5:6], p.lam[:, 4:5], p.row[:, R_LI:R_LI + 1], ALU.subtract))

            def max_of(m):
                t, h, i = maps[m]
                nk = keys(t)[1] - keys(t)[0]
                dve.wait_ge(sem("a_scores"), m + 1)
                if m >= 4:
                    dve.wait_ge(sem("a_exp"), m - 3)
                own.link(nc.vector.tensor_reduce(p.mx[:, m % 4:m % 4 + 1], p.score2(2 * (m % 2), nk), AX.X, ALU.max))
                nc.vector.tensor_scalar(p.nmax[:, m % 4:m % 4 + 1], p.mx[:, m % 4:m % 4 + 1], -(B if i is None else A), None,
                                        ALU.mult).then_inc(sem("a_max"), 1)

            def weigh(o):
                kind, t, h, n = outs[o]
                dve.wait_ge(sem("a_exp"), n)
                m = n - 1
                if kind == "b":
                    if o >= 8:
                        dve.wait_ge(sem("a_out"), o - 7)
                    own.mark(nc.vector.reciprocal(p.rs[:, o % 8:o % 8 + 1], p.esum[:, m % 4:m % 4 + 1]))
                    return
                nk = keys(t)[1] - keys(t)[0]
                own.mark(nc.vector.reciprocal(p.r01[:, 0:1], p.esum[:, (m - 1) % 4:(m - 1) % 4 + 1]))
                own.link(nc.vector.reciprocal(p.r01[:, 1:2], p.esum[:, m % 4:m % 4 + 1]))
                own.link(nc.vector.tensor_tensor(p.r01[:, 1:2], p.r01[:, 1:2], p.lam[:, 5:6], ALU.mult))
                own.link(nc.vector.tensor_scalar(p.prob[:, (m - 1) % 4, 0:nk], p.prob[:, (m - 1) % 4, 0:nk], p.r01[:, 0:1], None, ALU.mult))
                nc.vector.scalar_tensor_tensor(out=p.prob[:, m % 4, 0:nk], in0=p.prob[:, m % 4, 0:nk], scalar=p.r01[:, 1:2],
                                               in1=p.prob[:, (m - 1) % 4, 0:nk], op0=ALU.mult, op1=ALU.add).then_inc(sem("a_diff"), 1)

            def out(o):
                kind, t, h, n = outs[o]
                dve.wait_ge(sem("a_sums"), o + 1)
                if kind == "a":
                    nc.vector.tensor_copy(p.mixed[:, t, h * 64:h * 64 + 64], ps[6 + o % 2][:, 0:64]).then_inc(sem("a_out"), 1)
                else:
                    own.wait(own.n)
                    nc.vector.tensor_scalar(p.mixed[:, t, 256 + h * 64:320 + h * 64], ps[6 + o % 2][:, 0:64],
                                            p.rs[:, o % 8:o % 8 + 1], None, ALU.mult).then_inc(sem("a_out"), 1)

            for m in range(len(maps) + 5):
                if m < len(maps):
                    max_of(m)
                if m in out_after:
                    weigh(out_after[m][0])
                if m - 3 in out_after:
                    out(out_after[m - 3][0])
            dve.wait_ge(sem("a_out"), len(outs))
            for t in range(NT):
                x = p.mixed[:, t, 0:256]
                if t >= 1:
                    dve.wait_ge(sem("squares_a"), t)
                own.link(nc.vector.tensor_tensor(p.junk[:, 0:256], x, x, ALU.mult))
                nc.vector.tensor_reduce(p.ssa[:, t, :], p.junk[:, 0:256].rearrange("p (h n) -> p h n", h=4), AX.X,
                                        ALU.add).then_inc(sem("squares_a"), 1)
            own.link(nc.vector.tensor_scalar(p.gsub[:, :], p.row[:, R_SUB:R_SUB + 64], p.row[:, R_LI + 1:R_LI + 2], None, ALU.mult))
            dve.wait_ge(sem("root_a"), 1)
            own.link(nc.vector.reciprocal(p.ssa[:, :, :], p.ssa[:, :, :]))
            for t in range(NT):
                x = p.mixed[:, t, 0:256].rearrange("p (h n) -> p h n", h=4)
                own.link(nc.vector.tensor_tensor(x, x, bc(p.ssa[:, t, :], 2, 64), ALU.mult))
                own.mark(nc.vector.tensor_tensor(x, x, bc(p.gsub[:, :], 1, 4), ALU.mult))


def project_out(p, lay):
    nc, d, sem, ps = p.nc, p.d, p.sem, p.ps
    vecs = [p.mod[:, 16:24, :], p.A2[:, :, :], p.mod[:, 24:32, :], p.mod[:, 40:48, :]]
    units = [(v, g, half) for v in range(4) for g in range(2) for half in range(2)]

    def row_of(v, g):
        return p.gt2[:, g, :] if v == 3 else p.rows[:, v, g, :]

    with nc.Block() as block:
        @block.sync
        def _(sp):
            load_weights_out(p, sp, lay, range(0, 2))

        @block.tensor
        def _(pe):
            for t in range(NT):
                if t >= 1:
                    pe.wait_ge(sem("m_out"), 2 * t)
                for k in range(KT):
                    last = nc.tensor.transpose(ps[k // 4][:, (k % 4) * P:(k % 4 + 1) * P], p.mixed[:, t, k * P:(k + 1) * P], p.ident)
                last.then_inc(sem("m_turned"), 1)
            for u in range(len(units)):
                pe.wait_ge(sem("diag2"), u + 1)
                if u >= 2:
                    pe.wait_ge(sem("row_out"), u - 1)
                nc.tensor.matmul(ps[2 + u % 2][:, :], p.ones, p.diag4[:, u % 2, :], start=True, stop=True).then_inc(sem("row_mm"), 1)
            pe.wait_ge(sem("m_out"), 2 * NT)
            for t in range(NT):
                for c in range(2):
                    j = 2 * t + c
                    if t == 0:
                        pe.wait_ge(sem(f"load_v{c}"), 16)
                    if j >= 4:
                        pe.wait_ge(sem("res1"), j - 3)
                    for k in range(KT):
                        last = nc.tensor.matmul(ps[4 + j % 4][:, :], p.mixedT[:, k, t * P:(t + 1) * P], p.wring2[:, c, k, :],
                                                start=(k == 0), stop=(k == KT - 1))
                    last.then_inc(sem("wout_mm"), 1)
            for t in range(NT):
                pe.wait_ge(sem("h2_ready"), t + 1)
                if t >= 1:
                    pe.wait_ge(sem("h2T_out"), 2 * t)
                for k in range(KT):
                    last = nc.tensor.transpose(ps[k // 4][:, (k % 4) * P:(k % 4 + 1) * P], p.mixed[:, t, k * P:(k + 1) * P], p.ident)
                last.then_inc(sem("h2_turned"), 1)

        @block.scalar
        def _(act):
            for t in range(NT):
                act.wait_ge(sem("m_turned"), t + 1)
                for h in range(2):
                    nc.scalar.activation(p.mixedT[:, 4 * h:4 * h + 4, t * P:(t + 1) * P],
                                         ps[h].rearrange("p (k n) -> p k n", k=4), ACT.Copy).then_inc(sem("m_out"), 1)
            for u, (v, g, half) in enumerate(units):
                act.wait_ge(sem("row_mm"), u + 1)
                nc.scalar.activation(row_of(v, g)[:, half * 512:half * 512 + 512], ps[2 + u % 2], ACT.Copy).then_inc(sem("row_out"), 1)
            for t in range(NT):
                act.wait_ge(sem("res1"), 2 * t + 2)
                nc.scalar.activation(p.junk[:, :], p.x[:, t, :], ACT.Square, accum_out=p.ss1[:, t:t + 1]).then_inc(sem("square2"), 1)
                act.wait_ge(sem("square2"), t + 1)
                nc.scalar.activation(p.rt1[:, t:t + 1], p.ss1[:, t:t + 1], ACT.Sqrt, bias=p.eps[:, 0:1], scale=1.0 / D).then_inc(sem("root2"), 1)
            for t in range(NT):
                act.wait_ge(sem("h2_turned"), t + 1)
                for h in range(2):
                    nc.scalar.activation(p.h2T[:, 4 * h:4 * h + 4, t * P:(t + 1) * P],
                                         ps[h].rearrange("p (k n) -> p k n", k=4), ACT.Copy).then_inc(sem("h2T_out"), 1)

        @block.vector
        def _(dve):
            own = Chain(dve, sem("dve_out"))
            for u, (v, g, half) in enumerate(units):
                if u >= 2:
                    dve.wait_ge(sem("row_mm"), u - 1)
                nc.vector.tensor_tensor(p.diag4[:, u % 2, :].rearrange("p (k n) -> p k n", k=4), bc(p.ident, 1, 4),
                                        bc(vecs[v][:, 4 * half:4 * half + 4, g], 2, P), ALU.mult).then_inc(sem("diag2"), 1)
            dve.wait_ge(sem("row_out"), len(units))

            def norm(t):
                g = 0 if t == 0 else 1
                dve.wait_ge(sem("root2"), t + 1)
                own.link(nc.vector.reciprocal(p.rt1[:, t:t + 1], p.rt1[:, t:t + 1]))
                own.link(nc.vector.scalar_tensor_tensor(out=p.mixed[:, t, :], in0=p.x[:, t, :], scalar=p.rt1[:, t:t + 1],
                                                        in1=p.rows[:, 1, g, :], op0=ALU.mult, op1=ALU.mult))
                nc.vector.tensor_tensor(p.mixed[:, t, :], p.mixed[:, t, :], p.rows[:, 2, g, :], ALU.add).then_inc(sem("h2_ready"), 1)

            for t in range(NT):
                g = 0 if t == 0 else 1
                for c in range(2):
                    j = 2 * t + c
                    cols = slice(c * 512, c * 512 + 512)
                    dve.wait_ge(sem("wout_mm"), j + 1)
                    own.link(nc.vector.tensor_tensor(p.gated[:, cols], ps[4 + j % 4], p.rows[:, 0, g, cols], ALU.mult))
                    nc.vector.tensor_tensor(p.x[:, t, cols], p.x[:, t, cols], p.gated[:, cols], ALU.add).then_inc(sem("res1"), 1)
                if t >= 1:
                    norm(t - 1)
            norm(NT - 1)


def load_weights_out(p, sp, lay, chunks):
    for c in chunks:
        if c >= 2:
            if c < 4:
                sp.wait_ge(p.sem("wout_mm"), 2 * NT)
            else:
                sp.wait_ge(p.sem("pq_mm"), 8 * (c - 3))
        src = p.d["w_out"] if c < 2 else p.d["w_pq"]
        a = WCH * (c if c < 2 else c - 2)
        sp.dma_start(p.wring2[:, c % 2, :, :], src[bass.ds(lay, 1), :, :, a:a + WCH].rearrange("l p k n -> p (l k) n")).then_inc(p.sem(f"load_v{c % 2}"), 16)


def flat(ap):
    return ap.rearrange("p t n -> p (t n)")


def route_piece(p, dve, steps, i, n):
    nc, sem, v = p.nc, p.sem, p.nc.vector
    a, b = (0, 1)
    row = [p.r_sub[:, 0:NK], p.r_sub[:, NK:2 * NK]]

    def step():
        dve.wait_ge(sem("piece"), steps)
        dve.reg_add(steps, steps, 1)

    def mark(ins):
        ins.then_inc(sem("piece"), 1)

    step()
    if i == 0:
        mark(v.tensor_copy(p.r_sub[:, :], flat(p.sub)[:, bass.ds(n * (2 * NK), 2 * NK)]))
    elif i in (1, 3):
        c = slice(0, 8) if i == 1 else slice(8, 16)
        v.max(p.r_top[:, a, c], row[a])
        mark(v.max(p.r_top[:, b, c], row[b]))
    elif i in (2, 4):
        c = slice(0, 8) if i == 2 else slice(8, 16)
        v.max_index(p.r_ix[:, a, c], p.r_top[:, a, c], row[a])
        mark(v.max_index(p.r_ix[:, b, c], p.r_top[:, b, c], row[b]))
        if i == 2:
            step()
            v.match_replace(row[a], p.r_top[:, a, c], row[a], NEG)
            mark(v.match_replace(row[b], p.r_top[:, b, c], row[b], NEG))
    elif i == 5:
        v.tensor_tensor(p.r_cand[:, :].rearrange("p (i j) -> p i j", i=TOPK), bc(p.r_top[:, a, :], 2, TOPK),
                        bc(p.r_top[:, b, :], 1, TOPK), ALU.add)
        mark(v.tensor_copy(p.r_ixf[:, :, :], p.r_ix[:, :, :]))
    elif i in (6, 9):
        c = slice(0, 8) if i == 6 else slice(8, 16)
        mark(v.max(p.r_best[:, c], p.r_cand[:, :]))
    elif i in (7, 10):
        c = slice(0, 8) if i == 7 else slice(8, 16)
        mark(v.max_index(p.r_pos[:, c], p.r_best[:, c], p.r_cand[:, :]))
    elif i == 8:
        mark(v.match_replace(p.r_cand[:, :], p.r_best[:, 0:8], p.r_cand[:, :], NEG))
    elif i == 11:
        v.tensor_scalar(p.r_ij[:, a, :], p.r_pos[:, :], 4, None, ALU.logical_shift_right)
        mark(v.tensor_scalar(p.r_ij[:, b, :], p.r_pos[:, :], 15, None, ALU.bitwise_and))
    elif i == 12:
        v.tensor_tensor(p.r_gate[:, :], p.r_best[:, :], p.r_best[:, 0:1].to_broadcast([P, TOPK]),
                        ALU.subtract).then_inc(sem("centred"), 1)
        mark(v.tensor_copy(p.r_ijf[:, :, :], p.r_ij[:, :, :]))
    elif i == 13:
        v.tensor_tensor(p.r_pick[:, a, :, :], bc(p.r_ijf[:, a, :], 2, TOPK), bc(p.io16, 1, TOPK), ALU.is_equal)
        mark(v.tensor_tensor(p.r_pick[:, b, :, :], bc(p.r_ijf[:, b, :], 2, TOPK), bc(p.io16, 1, TOPK), ALU.is_equal))
    elif i == 14:
        mark(v.tensor_tensor(p.r_pick[:, :, :, :], p.r_pick[:, :, :, :], bc(p.r_ixf[:, :, :], 2, TOPK), ALU.mult))
    else:
        mark(v.tensor_reduce(p.r_ex[:, :, :], p.r_pick[:, :, :, :], AX.X, ALU.add))
        dve.wait_ge(sem("gate_exp"), n + 1)
        step()
        v.reciprocal(p.r_gs[:, 0:1], p.r_gs[:, 1:2])
        mark(v.scalar_tensor_tensor(out=p.r_e[:, :], in0=p.r_ex[:, a, :], scalar=float(NK), in1=p.r_ex[:, b, :],
                                    op0=ALU.mult, op1=ALU.add))
        step()
        cols = bass.ds(n * TOPK, TOPK)
        v.tensor_scalar(flat(p.eidx)[:, cols], p.r_e[:, :], p.row[:, R_OFF:R_OFF + 1], None,
                        ALU.add).then_inc(sem("routed"), 1)
        mark(v.tensor_scalar(flat(p.gat)[:, cols], p.r_gate[:, :], p.r_gs[:, 0:1], None, ALU.mult))


def route_gates(p, act, n):
    act.wait_ge(p.sem("centred"), n + 1)
    p.nc.scalar.activation(p.r_gate[:, :], p.r_gate[:, :], ACT.Exp, accum_out=p.r_gs[:, 1:2]).then_inc(p.sem("gate_exp"), 1)


def route(p, lay):
    nc, d, sem, ps = p.nc, p.d, p.sem, p.ps
    C = 4
    jobs = []
    for c in range(C + 1):
        if c < C:
            jobs += [("q", c, b, g) for b in range(4) for g in range(2)]
        if c >= 1:
            jobs += [("s", c - 1, t, 0) for t in range(NT)]
    at = {job: j for j, job in enumerate(jobs)}
    gates_after = [at[("q", 2 + n, 3, 1)] for n in range(AHEAD)]
    items_here = at[("s", 0, 0, 0)] + 1

    with nc.Block() as block:
        @block.vector
        def _(dve):
            steps = dve.alloc_register("first_route_steps")
            dve.reg_mov(steps, 1)
            dve.wait_ge(sem("r_out"), items_here)
            nc.vector.memset(p.r_gs[:, :], 0.0).then_inc(sem("piece"), 1)
            with dve.Fori(0, AHEAD) as n:
                for i in range(PIECES):
                    route_piece(p, dve, steps, i, n)

        @block.sync
        def _(sp):
            sp.dma_start(p.keysT[:, :], d["keysT"][bass.ds(lay, 1)].rearrange("l p n -> p (l n)")).then_inc(sem("load_keys"), 16)
            load_weights_out(p, sp, lay, range(2, 6))

        @block.tensor
        def _(pe):
            for j, (kind, c, i, g) in enumerate(jobs):
                if j >= 8:
                    pe.wait_ge(sem("r_out"), j - 7)
                b = ps[j % 8]
                if kind == "q":
                    if (i, g) == (0, 0):
                        pe.wait_ge(sem(f"load_v{c % 2}"), 16 * (2 + c // 2))
                    lo, hi = (0, P) if g == 0 else (P, TOK)
                    for k in range(KT):
                        last = nc.tensor.matmul(b[:, 0:hi - lo], p.wring2[:, c % 2, k, i * P:(i + 1) * P], p.h2T[:, k, lo:hi],
                                                start=(k == 0), stop=(k == KT - 1))
                    last.then_inc(sem("pq_mm"), 1)
                else:
                    if i == 0:
                        pe.wait_ge(sem("load_keys"), 16)
                        pe.wait_ge(sem("r_out"), at[("q", c, 3, 1)] + 1)
                    for q in range(4):
                        last = nc.tensor.matmul(b[:, q * P:(q + 1) * P], p.qpT[:, c % 2, q, i * P:(i + 1) * P],
                                                p.keysT[:, (4 * c + q) * P:(4 * c + q + 1) * P], start=True, stop=True)
                    last.then_inc(sem("sc_mm"), 1)

        @block.scalar
        def _(act):
            for j, (kind, c, i, g) in enumerate(jobs):
                b = ps[j % 8]
                if kind == "q":
                    act.wait_ge(sem("pq_mm"), 8 * c + 2 * i + g + 1)
                    if c >= 2 and (i, g) == (0, 0):
                        act.wait_ge(sem("sc_mm"), NT * (c - 1))
                    lo, hi = (0, P) if g == 0 else (P, TOK)
                    nc.scalar.activation(p.qpT[:, c % 2, i, lo:hi], b[:, 0:hi - lo], ACT.Copy).then_inc(sem("r_out"), 1)
                else:
                    act.wait_ge(sem("sc_mm"), NT * c + i + 1)
                    nc.scalar.activation(p.sub[:, i, 512 * c:512 * c + 512], b, ACT.Copy).then_inc(sem("r_out"), 1)
                if j in gates_after:
                    route_gates(p, act, gates_after.index(j))


def experts(p, lay):
    nc, d, sem, ps = p.nc, p.d, p.sem, p.ps
    H = RING

    def tile(ap, t):
        return ap[:, t, :] if type(t) is int else ap[:, bass.ds(t, 1), :].rearrange("p a n -> p (a n)")

    with nc.Block() as block:
        @block.gpsimd
        def _(pool):
            free = pool.alloc_register("rows_free")
            pool.reg_mov(free, 1)
            staged = pool.alloc_register("halves_staged")
            pool.reg_mov(staged, 1)

            def row_is_free():
                pool.wait_ge(sem("row_free"), free)
                pool.reg_add(free, free, 1)

            def head(t, h, n):
                for half in range(2):
                    row_is_free()
                    if half == 0:
                        pool.wait_ge(sem("routed"), n + 1)
                    nc.gpsimd.tensor_copy(p.stage[:, half, :], tile(p.eidx, t)[:, bass.ds(h * TOPK + half * H, H)]).then_inc(sem("staged"), 1)
                    pool.wait_ge(sem("staged"), staged)
                    pool.reg_add(staged, staged, 1)
                    for s in range(H):
                        if s > 0:
                            row_is_free()
                        nc.gpsimd.indirect_dma_start(out=p.uv[:, s, :], out_offset=None, in_=d["peer_uv"],
                                                     in_offset=bass.IndirectOffsetOnAxis(ap=p.stage[:, half, s:s + 1], axis=0)
                                                     ).then_inc(sem(f"row_in{s}"), 16)

            with pool.Fori(0, NT) as t:
                with pool.Fori(0, NH) as h:
                    head(t, h, t * NH + h)

        @block.vector
        def _(dve):
            steps = dve.alloc_register("route_steps")
            dve.reg_mov(steps, 1 + AHEAD * STEPS)

            def tile_pass(t, heads):
                g = 0 if type(t) is int and t == 0 else 1
                nc.vector.tensor_copy(p.hcur[:, :], tile(p.mixed, t)).then_inc(sem("h_here"), 1)
                for lo, hi, more in heads:
                    with dve.Fori(lo, hi) as h:
                        head_pass(t, h, more)
                for c in range(2):
                    cols = slice(c * 512, c * 512 + 512)
                    dve.wait_ge(sem("tile_sum"), t + 1)
                    nc.vector.tensor_tensor(p.y[:, cols], ps[c], p.gt2[:, g, cols], ALU.mult).then_inc(sem("y_read"), 1)
                dve.wait_ge(sem("y_read"), 2 * t + 2)
                nc.vector.tensor_tensor(tile(p.x, t), tile(p.x, t), p.y[:, :], ALU.add).then_inc(sem("residual"), 1)
                dve.wait_ge(sem("residual"), t + 1)

            def head_pass(t, h, more):
                n = t * NH + h
                rows = dve.snap((lay * NT * NH + n) * 32)
                dve.wait_ge(sem("h_here"), t + 1)
                for s in range(TOPK):
                    dve.wait_ge(sem(f"row_in{s % H}"), rows + (s // H + 1) * 16)
                    nc.vector.tensor_tensor_reduce(out=p.uv[:, s % H, 0:D], in0=p.uv[:, s % H, 0:D], in1=p.hcur[:, :], scale=1.0,
                                                   scalar=0.0, op0=ALU.mult, op1=ALU.add, accum_out=p.dot[:, s:s + 1]).then_inc(sem("dots"), 1)
                    if more:
                        route_piece(p, dve, steps, s, n + AHEAD)
                    if s % 2 == 1 and s >= 3:
                        weigh(t, h, n, s // 2 - 1)
                weigh(t, h, n, NH - 1)

            def weigh(t, h, n, q):
                dve.wait_ge(sem("gelus"), n * NH + q + 1)
                nc.vector.tensor_tensor(p.wgt[:, 2 * q:2 * q + 2], p.act16[:, 2 * q:2 * q + 2],
                                        tile(p.gat, t)[:, bass.ds(h * TOPK + 2 * q, 2)], ALU.mult).then_inc(sem("weights"), 1)

            tile_pass(0, [(0, NH, True)])
            with dve.Fori(1, NT - 1) as t:
                tile_pass(t, [(0, NH, True)])
            tile_pass(NT - 1, [(0, NH - AHEAD, True), (NH - AHEAD, NH, False)])

        @block.scalar
        def _(act):
            nc.scalar.activation(p.zero[:, :], p.ident, ACT.Copy, scale=0.0).then_inc(sem("zeros"), 1)

            def head(n, more):
                for q in range(NH + 1):
                    if q < NH:
                        act.wait_ge(sem("dots"), n * TOPK + 2 * q + 2)
                        nc.scalar.activation(p.act16[:, 2 * q:2 * q + 2], p.dot[:, 2 * q:2 * q + 2], ACT.Gelu_apprx_tanh).then_inc(sem("gelus"), 1)
                    if more and q == 7:
                        route_gates(p, act, n + AHEAD)
                    if q >= 1:
                        act.wait_ge(sem("weights"), n * NH + q)
                        for s in (2 * q - 2, 2 * q - 1):
                            act.wait_ge(sem("row_free"), n * TOPK + s + 1)
                            nc.scalar.activation(p.diag[:, s % H, :], p.ident, ACT.Copy, scale=p.wgt[:, s:s + 1]).then_inc(sem("diags"), 1)

            with act.Fori(0, NT * NH - AHEAD) as n:
                head(n, True)
            with act.Fori(NT * NH - AHEAD, NT * NH) as n:
                head(n, False)

        @block.tensor
        def _(pe):
            def mark(inc):
                nc.tensor.matmul(ps[2][:, 0:8], p.ident, p.ident[:, 0:8], start=True, stop=True).then_inc(sem("row_free"), inc)

            mark(H)
            with pe.Fori(0, NT) as t:
                for c in range(2):
                    pe.wait_ge(sem("zeros"), 1)
                    nc.tensor.matmul(ps[c], p.zero[:, :], p.cons[:, 0:512], start=True, stop=False, skip_group_check=True)
                with pe.Fori(0, NH) as h:
                    for s in range(TOPK):
                        pe.wait_ge(sem("diags"), (t * NH + h) * TOPK + s + 1)
                        for c in range(2):
                            mm = nc.tensor.matmul(ps[c], p.diag[:, s % H, :], p.uv[:, s % H, D + 512 * c:D + 512 * c + 512],
                                                  start=False, stop=False, skip_group_check=True)
                        mm.then_inc(sem("row_free"), 1)
                for c in range(2):
                    mm = nc.tensor.matmul(ps[c], p.zero[:, :], p.cons[:, 0:512], start=False, stop=True, skip_group_check=True)
                mm.then_inc(sem("tile_sum"), 1)
                pe.wait_ge(sem("y_read"), 2 * t + 2)
                nc.tensor.matmul(ps[2][:, 0:8], p.ident, p.ident[:, 0:8], start=True, stop=True)


def finish(p):
    nc, d, sem = p.nc, p.d, p.sem
    with nc.Block() as block:
        @block.scalar
        def _(act):
            for t in range(NT):
                if t >= 1:
                    act.wait_ge(sem("square_f"), t)
                nc.scalar.activation(p.junk[:, :], p.x[:, t, :], ACT.Square, accum_out=p.ss1[:, t:t + 1]).then_inc(sem("square_f"), 1)
            act.wait_ge(sem("square_f"), NT)
            nc.scalar.activation(p.rt1[:, 0:NT], p.ss1[:, 0:NT], ACT.Sqrt, bias=p.eps[:, 0:1], scale=1.0 / D).then_inc(sem("root_f"), 1)

        @block.vector
        def _(dve):
            dve.wait_ge(sem("root_f"), 1)
            nc.vector.reciprocal(p.rt1[:, 0:NT], p.rt1[:, 0:NT]).then_inc(sem("recip_f"), 1)
            dve.wait_ge(sem("recip_f"), 1)
            dve.wait_ge(sem("load_gf"), 16)
            for t in range(NT):
                nc.vector.scalar_tensor_tensor(out=p.x[:, t, :], in0=p.x[:, t, :], scalar=p.rt1[:, t:t + 1], in1=p.tmp[:, :],
                                               op0=ALU.mult, op1=ALU.mult).then_inc(sem("y_ready"), 1)

        @block.sync
        def _(sp):
            sp.dma_start(p.tmp[:, :], d["g_final"].to_broadcast([P, D])).then_inc(sem("load_gf"), 16)
            sp.wait_ge(sem("y_ready"), 1)
            sp.dma_start(d["yp"], p.x[:, 0, :]).then_inc(sem("store_y"), 16)
            sp.wait_ge(sem("y_ready"), NT)
            sp.dma_start(d["ys"], p.x[:, 1:NT, :]).then_inc(sem("store_y"), 16)
            sp.wait_ge(sem("store_y"), 32)


def build(nc, dram, stop=None, dumps=None):
    p = Prog(nc, dram)
    with ExitStack() as ctx:
        p.psall = ctx.enter_context(nc.psum_tensor("psall", [P, 8 * 512], F32))
        p.ps = [p.psall[:, 512 * i:512 * i + 512] for i in range(8)]
        p.score2 = lambda s, nk: p.psall[:, 512 * s:512 * s + nk]
        sb = p.sb
        p.x = sb(ctx, "x", [P, NT, D])
        p.cons = sb(ctx, "cons", [P, CONS])
        p.rope = sb(ctx, "rope", [P, 2, 4, 32])
        p.sc = sb(ctx, "sc", [P, KT, 2])
        p.vec = sb(ctx, "vec", [P, V_END])
        p.row = sb(ctx, "row", [P, R_END])
        p.mod = sb(ctx, "mod", [P, 48, 2])
        p.A1 = sb(ctx, "A1", [P, KT, 2])
        p.A2 = sb(ctx, "A2", [P, KT, 2])
        p.ss1 = sb(ctx, "ss1", [P, 8])
        p.rt1 = sb(ctx, "rt1", [P, 8])
        p.junk = sb(ctx, "junk", [P, D])
        p.ident = p.cons[:, 0:P]
        p.ones = p.cons[:, P:2 * P]
        p.imask = p.cons[:, 2 * P:4 * P].rearrange("p (d n) -> p d n", d=2)
        p.lmask = p.cons[:, 4 * P:18 * P].rearrange("p (d l n) -> p d l n", d=2, l=7)
        p.io16 = p.cons[:, 18 * P:18 * P + 16]
        p.eps = p.cons[:, 18 * P + 16:18 * P + 17]
        p.one = p.cons[:, 18 * P + 17:18 * P + 18]
        start(p)
        outer = set(p.sems)
        with nc.Fori(0, LAYERS) as lay:
            layer(p, lay, stop, dumps)
            for name, s in p.sems.items():
                if name not in outer and not name.startswith("row_in"):
                    nc.sync.sem_clear(s)
            nc.all_engine_barrier()
        if stop is None:
            p.tmp = sb(ctx, "tmp", [P, D])
            finish(p)


def layer(p, lay, stop, dumps):
    nc, sb = p.nc, p.sb

    def at(name):
        if stop != name:
            return False
        for n, ap in dumps(p).items():
            nc.sync.dma_start(p.d[n], ap).then_inc(p.sem("dump"), 16)
            nc.sync.wait_ge(p.sem("dump"), 16 * (1 + list(dumps(p)).index(n)))
        return True

    with ExitStack() as whole:
        p.mixed = sb(whole, "mixed", [P, NT, D])
        with ExitStack() as c1:
            p.proj = sb(c1, "proj", [P, NT, TM])
            with ExitStack() as c2:
                p.qkv = sb(c2, "qkv", [P, NT, 768])
                with ExitStack() as c3:
                    p.qkvT = sb(c3, "qkvT", [P, 6, LINE])
                    with ExitStack() as c4:
                        p.hT = sb(c4, "hT", [P, KT, TOK])
                        p.xn = sb(c4, "xn", [P, 2, D])
                        p.mrow = sb(c4, "mrow", [2, 2, WCH])
                        p.wring = sb(c4, "wring", [P, 3, KT, WCH])
                        mod_and_project(p, lay)
                        if at("project"):
                            return
                    with ExitStack() as c4:
                        p.convd = sb(c4, "convd", [P, 6, LINE - 2])
                        conv(p)
                        if at("conv"):
                            return
                with ExitStack() as c3:
                    p.ssd = sb(c3, "ssd", [P, NT, 8])
                    p.rd = sb(c3, "rd", [P, NT, 8])
                    p.zz = sb(c3, "zz", [P, NT, 8])
                    p.zab = sb(c3, "zab", [P, NT, 8])
                    p.sp1 = sb(c3, "sp1", [P, NT, 8])
                    p.bet = sb(c3, "bet", [P, NT, 8])
                    p.eal = sb(c3, "eal", [P, 8])
                    p.g = sb(c3, "g", [P, NT, 8])
                    p.gcol = sb(c3, "gcol", [P, NT, 8])
                    p.egc = sb(c3, "egc", [P, NT, 8])
                    p.sso = sb(c3, "sso", [P, NT, 4])
                    p.oC = sb(c3, "oC", [P, NT, 256])
                    p.dif = sb(c3, "dif", [P, 2, HC, P])
                    p.dec = sb(c3, "dec", [P, 2, HC, P])
                    p.lt = sb(c3, "lt", [P, 2, HC, P])
                    p.mlt = sb(c3, "mlt", [P, 2, 2, HC, P])
                    p.X = sb(c3, "X", [P, 2, HC, P])
                    p.XT = sb(c3, "XT", [P, 2, HC, P])
                    p.t1s = sb(c3, "t1s", [P, 2, HC * P])
                    p.qk = sb(c3, "qk", [P, 2, HC, P])
                    p.rv = sb(c3, "rv", [P, 2, HC, 64])
                    p.kd = sb(c3, "kd", [P, 2, HC, 64])
                    p.w = sb(c3, "w", [P, 2, HC, 64])
                    p.kT = sb(c3, "kT", [64, 2, HC * P])
                    p.qT = sb(c3, "qT", [64, 2, HC * P])
                    p.egr = sb(c3, "egr", [64, 2, HC, P])
                    p.qd = sb(c3, "qd", [64, 2, HC, P])
                    p.state = sb(c3, "state", [64, 2, HC, 64])
                    delta(p, lay)
                    if at("delta"):
                        return
            with ExitStack() as c2:
                p.qTa = sb(c2, "qTa", [P, 2, TOK])
                p.kTa = sb(c2, "kTa", [P, 2, KEYS])
                p.cav = sb(c2, "cav", [P, 256])
                p.lam = sb(c2, "lam", [P, 8])
                p.vb = sb(c2, "vb", [P, 6, 512])
                p.qTb = sb(c2, "qTb", [96, HB, TOK])
                p.kTb = sb(c2, "kTb", [96, HB, KEYS])
                with ExitStack() as c3:
                    p.cak = sb(c3, "cak", [P, 256])
                    p.cckv = sb(c3, "cckv", [P, 128])
                    p.ckr = sb(c3, "ckr", [P, 96])
                    p.krp = sb(c3, "krp", [P, NT, 96])
                    p.ssl = sb(c3, "ssl", [P, 2, NT])
                    p.rl = sb(c3, "rl", [P, 2, NT])
                    p.qcT = sb(c3, "qcT", [P, 2, TOK])
                    p.ckvT = sb(c3, "ckvT", [P, KEYS])
                    p.wuq = sb(c3, "wuq", [P, 2, 768])
                    p.wukn = sb(c3, "wukn", [P, 512])
                    p.wukv = sb(c3, "wukv", [P, 512])
                    p.qb = sb(c3, "qb", [P, 2, 768])
                    p.ru = sb(c3, "ru", [P, 512])
                    p.rv2 = sb(c3, "rv2", [P, 512])
                    prepare_attention(p, lay)
                with ExitStack() as c3:
                    p.prob = sb(c3, "prob", [P, 4, 640])
                    p.probT = sb(c3, "probT", [P, 2, 640])
                    p.mx = sb(c3, "mx", [P, 4])
                    p.nmax = sb(c3, "nmax", [P, 4])
                    p.esum = sb(c3, "esum", [P, 4])
                    p.rs = sb(c3, "rs", [P, 8])
                    p.r01 = sb(c3, "r01", [P, 2])
                    p.ssa = sb(c3, "ssa", [P, NT, 4])
                    p.gsub = sb(c3, "gsub", [P, 64])
                    attend(p)
                    if at("attend"):
                        return
        p.gt2 = sb(whole, "gt2", [P, 2, D])
        p.gat = sb(whole, "gat", [P, NT, SLOTS])
        p.eidx = sb(whole, "eidx", [P, NT, SLOTS], U32)
        with ExitStack() as c1:
            region = sb(c1, "region", [P, RING * 2 * D])
            p.h2T = region[:, 0:KT * TOK].rearrange("p (k n) -> p k n", k=KT)
            p.wring2 = region[:, KT * TOK:KT * TOK + 2 * KT * WCH].rearrange("p (b k n) -> p b k n", b=2, k=KT)
            p.uv = region[:, :].rearrange("p (s n) -> p s n", s=RING)
            with ExitStack() as c2:
                p.mixedT = sb(c2, "mixedT", [P, KT, TOK])
                p.rows = sb(c2, "rows", [P, 3, 2, D])
                p.diag4 = sb(c2, "diag4", [P, 2, 512])
                p.gated = sb(c2, "gated", [P, D])
                project_out(p, lay)
                if at("out"):
                    return
            p.sub = sb(c1, "sub", [P, NT, 2048])
            p.r_sub = sb(c1, "r_sub", [P, 2 * NK])
            p.r_top = sb(c1, "r_top", [P, 2, TOPK])
            p.r_ix = sb(c1, "r_ix", [P, 2, TOPK], U32)
            p.r_ixf = sb(c1, "r_ixf", [P, 2, TOPK])
            p.r_cand = sb(c1, "r_cand", [P, TOPK * TOPK])
            p.r_best = sb(c1, "r_best", [P, TOPK])
            p.r_pos = sb(c1, "r_pos", [P, TOPK], U32)
            p.r_ij = sb(c1, "r_ij", [P, 2, TOPK], U32)
            p.r_ijf = sb(c1, "r_ijf", [P, 2, TOPK])
            p.r_gate = sb(c1, "r_gate", [P, TOPK])
            p.r_gs = sb(c1, "r_gs", [P, 2])
            p.r_pick = sb(c1, "r_pick", [P, 2, TOPK, TOPK])
            p.r_ex = sb(c1, "r_ex", [P, 2, TOPK])
            p.r_e = sb(c1, "r_e", [P, TOPK])
            with ExitStack() as c2:
                p.qpT = sb(c2, "qpT", [P, 2, 4, TOK])
                p.keysT = sb(c2, "keysT", [P, 16 * P])
                route(p, lay)
            p.hcur = sb(c1, "hcur", [P, D])
            p.y = sb(c1, "y", [P, D])
            p.diag = sb(c1, "diag", [P, RING, P])
            p.zero = sb(c1, "zero", [P, P])
            p.dot = sb(c1, "dot", [P, TOPK])
            p.act16 = sb(c1, "act16", [P, TOPK])
            p.wgt = sb(c1, "wgt", [P, TOPK])
            p.stage = sb(c1, "stage", [P, 2, RING], U32)
            experts(p, lay)
            if at("route") or at("experts"):
                return


CONS = 18 * P + 18


def constants():
    i = np.arange(P)
    c = np.zeros((P, CONS), np.float32)
    c[:, 0:P] = np.eye(P)
    c[:, P:2 * P] = 1.0
    upper = (i[:, None] <= i[None, :]).astype(np.float32)
    c[:, 2 * P:3 * P] = upper
    c[:, 3 * P:4 * P] = upper.T
    for lvl in range(7):
        b = 2 ** lvl
        join = ((i[:, None] // (2 * b) == i[None, :] // (2 * b)) & (i[:, None] // b % 2 == 0) & (i[None, :] // b % 2 == 1))
        c[:, (4 + lvl) * P:(5 + lvl) * P] = join
        c[:, (11 + lvl) * P:(12 + lvl) * P] = join.T
    c[:, 18 * P:18 * P + 16] = np.arange(16)
    c[:, 18 * P + 16] = EPS
    c[:, 18 * P + 17] = 1.0
    t = np.arange(512)
    n_freq = 8
    freqs = (np.float32(10000.0) ** (-np.arange(n_freq, dtype=np.float32) / n_freq)).astype(np.float32)
    ar = (t // 64).astype(np.float32)[:, None] * freqs
    ac = (t % 64).astype(np.float32)[:, None] * freqs
    ang = np.concatenate([ar, ar, ac, ac], axis=-1)
    sign = np.repeat([-1.0, 1.0, -1.0, 1.0], 8).astype(np.float32)
    tables = np.stack([np.cos(ang), np.sin(ang) * sign]).astype(np.float32)
    rope = tables.reshape(2, 4, P, 32).transpose(2, 0, 1, 3)
    return c, np.ascontiguousarray(rope)


def lay_out(i):
    f = {n: np.asarray(a) for n, a in i.items()}

    def kmajor(w):
        l, k, n = w.shape
        return w.reshape(l, k // P, P, n).transpose(0, 2, 1, 3)

    def fm(v):
        return v.reshape(L, -1, P).transpose(0, 2, 1)

    c_qkv, c_g = 1184, 1952
    w = f["w_in"]
    tm = np.concatenate([w[:, :, :c_qkv], w[:, :, c_g:]], axis=2)
    ukv = f["w_ukv"].reshape(L, P, HB, 2, 64)
    lam = [f[n] for n in ("lam_q1", "lam_k1", "lam_q2", "lam_k2")]
    li = [0.8 - 0.6 * math.exp(-0.3 * l) for l in range(L)]
    layer_consts = np.array([[v, 1.0 - v, l * NK * NK] for l, v in enumerate(li)], np.float32)
    rows = np.concatenate([f["g_subln"], f["g_qc"], f["g_kvc"], f["g_onorm"]] + lam
                          + [f["a_log_f"], f["a_log_b"], f["dt_bias_f"], f["dt_bias_b"], layer_consts], axis=1)
    conv_w = f["conv_c"].reshape(L, 3, 6, P).transpose(0, 3, 2, 1).reshape(L, P, 18)
    vecs = np.concatenate([fm(f["b_mod"]), fm(f["g_norm1"]), fm(f["g_norm2"]), conv_w], axis=2)
    cons, rope = constants()
    out = {
        "consts": cons, "rope": rope,
        "cond": np.stack([f["c_ctx"].reshape(KT, P).T, f["c"].reshape(KT, P).T], axis=2),
        "xp": f["x_prompt"].reshape(P, D),
        "xs": f["x_sample"].reshape(4, P, D).transpose(1, 0, 2),
        "vecs": vecs, "rows": rows,
        "w_mod": kmajor(f["w_mod"]), "w_in_tm": kmajor(tm), "w_in_fm": kmajor(w[:, :, c_qkv:c_g]),
        "cache_a_k": f["cache_a_k"].reshape(L, P, 256), "cache_a_v": f["cache_a_v"].reshape(L, P, 256),
        "cache_ckv": f["cache_b_ckv"].reshape(L, P, 128), "cache_kr": f["cache_b_krope"].reshape(L, P, 32),
        "in_sf": f["state_c_fwd"].reshape(L, HC, 64, 64), "in_sb": f["state_c_bwd"].reshape(L, HC, 64, 64),
        "w_uq": kmajor(f["w_uq"]), "w_ukn": ukv[:, :, :, 0].reshape(L, P, 512), "w_ukv": ukv[:, :, :, 1].reshape(L, P, 512),
        "w_out": kmajor(f["w_out"]), "w_pq": kmajor(f["w_pq"]),
        "keysT": f["peer_keys"].reshape(L, 16, NK, P).transpose(0, 3, 1, 2).reshape(L, P, 16 * NK),
        "peer_uv": np.concatenate([f["peer_u"], f["peer_v"]], axis=2).reshape(L * NK * NK, 2 * D),
        "g_final": f["g_final"].reshape(1, D),
    }
    return {n: np.ascontiguousarray(a, dtype=np.float32) for n, a in out.items()}


OUTS = {"yp": (P, D), "ys": (P, 4, D), "out_ak": (L, P, 256), "out_av": (L, P, 256), "out_ckv": (L, P, 128),
        "out_kr": (L, P, 32), "out_sf": (L, HC, 64, 64), "out_sb": (L, HC, 64, 64)}


def kernel(**inputs):
    import concourse.bacc as bacc
    from concourse.bass_utils import run_bass_kernel_spmd

    nc = bacc.Bacc("TRN2", target_bir_lowering=False, num_devices=1)
    arrays = lay_out(inputs)
    dram = {n: nc.dram_tensor("in_" + n, a.shape, F32, kind="ExternalInput").ap() for n, a in arrays.items()}
    dram.update({n: nc.dram_tensor("res_" + n, s, F32, kind="ExternalOutput").ap() for n, s in OUTS.items()})
    build(nc, dram)
    got = run_bass_kernel_spmd(nc, [{"in_" + n: a for n, a in arrays.items()}], core_ids=[0]).results[0]
    r = {n: got["res_" + n] for n in OUTS}
    return (r["yp"].reshape(1, P, D), r["ys"].transpose(1, 0, 2).reshape(1, 4 * P, D),
            r["out_ak"].reshape(1, L, P, HA, 2, 32), r["out_av"].reshape(1, L, P, HA, 64),
            r["out_ckv"].reshape(1, L, P, 128), r["out_kr"].reshape(1, L, P, 32),
            r["out_sf"].reshape(1, L, HC, 64, 64), r["out_sb"].reshape(1, L, HC, 64, 64))
```

```python
import math
from contextlib import ExitStack

import numpy as np

import concourse.bass as bass
from concourse import mybir

F32 = mybir.dt.float32
U32 = mybir.dt.uint32
ALU = mybir.AluOpType
ACT = mybir.ActivationFunctionType
AX = mybir.AxisListType

P = 128
D, L = 1024, 2
KT = D // P
NT = 5
TOK = NT * P
EPS = 1e-6
QA, KA, VA, QC, KVC, KR, GATE, BF, TM = 0, 256, 512, 768, 1024, 1152, 1184, 1440, 1456
TM_CHUNKS = [(0, 512), (512, 1024), (1024, TM)]
FM_CHUNKS = [(0, 512), (512, 768)]
WCH = 512
EARLY = 4
LATE = 8
LATE_STEPS = 2 * KT
LINE = 644
HA, HB, HC = 4, 8, 4
KEYS = 6 * P
NH, NK, TOPK = 8, 128, 16
W_A = 256
UNTURNED = (0, 1, 6, 7)
PROBS = 6
LEVELS = 7
X_STEPS = 2 * (LEVELS - 1)
KS_LEVEL = 2
AHEAD = 2
PIECES = TOPK
STEPS = 19
SLOTS = NH * TOPK
RING = 8
R_SUB, R_QC, R_KVC, R_ON, R_LAM, R_ALOG, R_DT, R_LI, R_OFF, R_END = 0, 64, 320, 448, 512, 640, 648, 656, 658, 659
V_BMOD, V_G1, V_G2, V_CONV, V_END = 0, 48, 56, 64, 82
NEG = -3.0e38


def kcol(t):
    return 0 if t == 0 else P * (t + 1)


class Chain:

    def __init__(self, eng, sem):
        self.eng, self.sem, self.n = eng, sem, 0

    def mark(self, ins):
        self.n += 1
        ins.then_inc(self.sem, 1)
        return self.n

    def wait(self, n):
        self.eng.wait_ge(self.sem, n)

    def link(self, ins):
        self.wait(self.mark(ins))


class Prog:

    def __init__(self, nc, dram):
        self.nc, self.d = nc, dram
        self.sems = {}

    def sem(self, name):
        if name not in self.sems:
            self.sems[name] = self.nc.alloc_semaphore(name)
        return self.sems[name]

    def sb(self, ctx, name, shape, dt=F32):
        return ctx.enter_context(self.nc.sbuf_tensor(name, shape, dt))


def bc(ap, axis, n):
    a = ap.unsqueeze(axis)
    shape = list(a.shape)
    shape[axis] = n
    return a.to_broadcast(shape)


def start(p):
    nc, d, sem = p.nc, p.d, p.sem
    with nc.Block() as block:
        @block.sync
        def _(sp):
            sp.dma_start(p.cons[:, :], d["consts"]).then_inc(sem("load_const"), 16)
            sp.dma_start(p.rope[:, :, :, :], d["rope"]).then_inc(sem("load_const"), 16)
            sp.dma_start(p.sc[:, :, :], d["cond"]).then_inc(sem("load_cond"), 16)
            sp.dma_start(p.x[:, 0, :], d["xp"]).then_inc(sem("load_const"), 16)
            sp.dma_start(p.x[:, 1:NT, :], d["xs"]).then_inc(sem("load_const"), 16)
            sp.wait_ge(sem("load_const"), 64)

        @block.scalar
        def _(act):
            act.wait_ge(sem("load_cond"), 16)
            nc.scalar.activation(p.sc[:, :, :], p.sc[:, :, :], ACT.Silu).then_inc(sem("silu_c"), 1)
            act.wait_ge(sem("silu_c"), 1)


def mod_and_project(p, lay):
    nc, d, sem = p.nc, p.d, p.sem
    ps = p.ps
    wsem = [sem(f"load_w{i}") for i in range(3)]
    first_tm, first_fm = EARLY, EARLY + len(TM_CHUNKS)
    n_chunks = first_fm + len(FM_CHUNKS)
    w_late = p.mixed[:, 0:4, :].rearrange("p t (k n) -> p (t k) n", n=WCH)
    sums_late = p.qkv[:, 0:4, :].rearrange("p t n -> p (t n)").rearrange("p (b g n) -> p b g n", b=3, g=2)

    LATE_AFTER = ((0, 1), (0, 3), (1, 0), (1, 2), (1, 4), (2, 2), (2, 4))
    jobs = []
    for c, (a, b) in enumerate(TM_CHUNKS):
        for t in range(NT):
            jobs.append(("tm", first_tm + c, t, a, b))
            if (c, t) in LATE_AFTER:
                jobs.append(("late", None, LATE_AFTER.index((c, t)), 0, 0))
    for c, (a, b) in enumerate(FM_CHUNKS):
        for blk in range(a // P, b // P):
            for g in range(2):
                jobs.append(("fm", first_fm + c, g, blk, blk - a // P))
        if c == 0:
            jobs.append(("late", None, LATE - 1, 0, 0))

    jobs_until = {job[1]: j + 1 for j, job in enumerate(jobs)}
    tm_until = max(j + 1 for j, job in enumerate(jobs) if job[0] == "tm")
    late_until = {job[2]: j + 1 for j, job in enumerate(jobs) if job[0] == "late"}

    def w_arrived(pe, c):
        pe.wait_ge(wsem[c % 3], 16 * (c // 3 + 1))

    with nc.Block() as block:
        @block.sync
        def _(sp):
            sp.dma_start(p.vec[:, :], d["vecs"][bass.ds(lay, 1)].rearrange("a p n -> p (a n)")).then_inc(sem("load_vec"), 16)
            sp.dma_start(p.row[:, :], d["rows"][bass.ds(lay, 1)].to_broadcast([P, R_END])).then_inc(sem("load_row"), 16)
            order = [0, 1, 2, 3, "late", 4, 5, "late", 6, "late", "late", 7, "late", "late", 8, "late", "late"]
            i = 0
            for c in order:
                if c == "late":
                    for half in range(2):
                        if i >= 1:
                            sp.wait_ge(sem("late_sum"), LATE_STEPS * (i - 1) + KT * (half + 1))
                        a = (EARLY + i) * WCH
                        sp.dma_start(w_late[:, 4 * half:4 * half + 4, :],
                                     d["w_mod"][bass.ds(lay, 1), :, 4 * half:4 * half + 4, a:a + WCH].rearrange("a p k n -> p (a k) n")
                                     ).then_inc(sem(f"load_late{half}"), 16)
                    i += 1
                    continue
                if c >= EARLY + 3:
                    sp.wait_ge(sem("proj"), jobs_until[c - 3])
                elif c >= 3:
                    sp.wait_ge(sem("w_used"), c - 2)
                if c < EARLY:
                    src = d["w_mod"][bass.ds(lay, 1), :, :, c * WCH:(c + 1) * WCH]
                    w = WCH
                elif c < first_fm:
                    a, b = TM_CHUNKS[c - first_tm]
                    src = d["w_in_tm"][bass.ds(lay, 1), :, :, a:b]
                    w = b - a
                else:
                    a, b = FM_CHUNKS[c - first_fm]
                    src = d["w_in_fm"][bass.ds(lay, 1), :, :, a:b]
                    w = b - a
                sp.dma_start(p.wring[:, c % 3, :, 0:w], src.rearrange("a p k n -> p (a k) n")).then_inc(wsem[c % 3], 16)

        @block.scalar
        def _(act):
            for t in range(NT):
                if t >= 1:
                    act.wait_ge(sem("square1"), t)
                nc.scalar.activation(p.junk[:, :], p.x[:, t, :], ACT.Square,
                                     accum_out=p.ss1[:, t:t + 1]).then_inc(sem("square1"), 1)
            act.wait_ge(sem("square1"), NT)
            nc.scalar.activation(p.rt1[:, 0:NT], p.ss1[:, 0:NT], ACT.Sqrt, bias=p.eps[:, 0:1],
                                 scale=1.0 / D).then_inc(sem("root1"), 1)
            for t in range(NT):
                act.wait_ge(sem("turned1"), t + 1)
                for q in range(2):
                    nc.scalar.activation(p.hT[:, 4 * q:4 * q + 4, t * P:(t + 1) * P],
                                         ps[1 + 2 * (t % 2) + q].rearrange("p (k n) -> p k n", k=4), ACT.Copy).then_inc(sem("xn_out"), 1)
            for j, (kind, c, i, a, b) in enumerate(jobs):
                act.wait_ge(sem("proj"), j + 1)
                dst, src = proj_evac(p, j, kind, i, a, b)
                nc.scalar.activation(dst, src, ACT.Copy).then_inc(sem("proj_out"), 1)
                if j == tm_until + 1:
                    act.wait_ge(sem("squares_l"), 2 * NT)
                    nc.scalar.activation(p.rl[:, 0, :], p.ssl[:, 0, :], ACT.Sqrt, bias=p.eps[:, 0:1], scale=1.0 / 256).then_inc(sem("root_l"), 1)
                    nc.scalar.activation(p.rl[:, 1, :], p.ssl[:, 1, :], ACT.Sqrt, bias=p.eps[:, 0:1], scale=1.0 / 128).then_inc(sem("root_l"), 1)

        @block.vector
        def _(dve):
            own = Chain(dve, sem("dve_mod"))
            nc.vector.memset(p.qkvT[:, :, 0:1], 0.0)
            nc.vector.memset(p.qkvT[:, :, 129:131], 0.0)
            nc.vector.memset(p.qkvT[:, :, LINE - 1:LINE], 0.0)
            dve.wait_ge(sem("root1"), 1)
            own.link(nc.vector.reciprocal(p.rt1[:, 0:NT], p.rt1[:, 0:NT]))
            for t in range(NT):
                if t >= 2:
                    dve.wait_ge(sem("turned1"), t - 1)
                nc.vector.tensor_scalar(p.xn[:, t % 2, :], p.x[:, t, :], p.rt1[:, t:t + 1], None,
                                        ALU.mult).then_inc(sem("scaled1"), 1)
            for c in range(EARLY):
                dve.wait_ge(sem("w_used"), c + 1)
                if c >= 2:
                    dve.wait_ge(sem("mod_turned"), c - 1)
                nc.vector.tensor_copy(p.mrow[0:2, c % 2, :], ps[5 + c % 2][0:2, :]).then_inc(sem("mod_row"), 1)
            dve.wait_ge(sem("load_vec"), 16)
            dve.wait_ge(sem("mod_turned"), EARLY)
            own.link(nc.vector.tensor_tensor(p.mod[:, 0:16, :], ps[0][:, 0:32].rearrange("p (n g) -> p n g", g=2),
                                             bc(p.vec[:, V_BMOD:V_BMOD + 16], 2, 2), ALU.add))
            own.link(nc.vector.scalar_tensor_tensor(out=p.A1[:, :, :], in0=p.mod[:, 8:16, :], scalar=1.0,
                                                    in1=bc(p.vec[:, V_G1:V_G1 + 8], 2, 2), op0=ALU.add, op1=ALU.mult))
            dve.wait_ge(sem("xn_out"), 2 * NT)
            for g, cols in enumerate((slice(0, P), slice(P, TOK))):
                for k in range(KT):
                    nc.vector.tensor_scalar(p.hT[:, k, cols], p.hT[:, k, cols], p.A1[:, k, g:g + 1], p.mod[:, k, g:g + 1],
                                            ALU.mult, ALU.add).then_inc(sem("h_ready"), 1)
            late = Chain(dve, sem("late_sum"))
            for i in range(LATE):
                if i >= 3:
                    dve.wait_ge(sem("proj"), late_until[i - 3])
                for k in range(KT):
                    if k % 4 == 0:
                        dve.wait_ge(sem(f"load_late{k // 4}"), 16 * (i + 1))
                    for g in range(2):
                        acc = sums_late[:, i % 3, g, :]
                        if k == 0:
                            late.mark(nc.vector.tensor_scalar(acc, w_late[:, k, :], p.sc[:, k, g:g + 1], None, ALU.mult))
                        else:
                            late.wait(late.n - 1)
                            late.mark(nc.vector.scalar_tensor_tensor(out=acc, in0=w_late[:, k, :], scalar=p.sc[:, k, g:g + 1], in1=acc,
                                                                     op0=ALU.mult, op1=ALU.add))
            dve.wait_ge(sem("proj_out"), tm_until)
            dve.wait_ge(sem("load_row"), 16)
            norm_and_rope(p, dve, own)
            dve.wait_ge(sem("proj_out"), late_until[LATE - 1])
            own.link(nc.vector.tensor_tensor(p.mod[:, 16:48, :], p.mod[:, 16:48, :],
                                             bc(p.vec[:, V_BMOD + 16:V_BMOD + 48], 2, 2), ALU.add))
            own.link(nc.vector.scalar_tensor_tensor(out=p.A2[:, :, :], in0=p.mod[:, 32:40, :], scalar=1.0,
                                                    in1=bc(p.vec[:, V_G2:V_G2 + 8], 2, 2), op0=ALU.add, op1=ALU.mult))

        @block.tensor
        def _(pe):
            for t in range(NT):
                pe.wait_ge(sem("scaled1"), t + 1)
                if t >= 2:
                    pe.wait_ge(sem("xn_out"), 2 * (t - 1))
                for k in range(KT):
                    last = nc.tensor.transpose(ps[1 + 2 * (t % 2) + k // 4][:, (k % 4) * P:(k % 4 + 1) * P],
                                               p.xn[:, t % 2, k * P:(k + 1) * P], p.ident)
                last.then_inc(sem("turned1"), 1)
            for c in range(EARLY + 1):
                if c < EARLY:
                    w_arrived(pe, c)
                    if c >= 2:
                        pe.wait_ge(sem("mod_row"), c - 1)
                    for k in range(KT):
                        last = nc.tensor.matmul(ps[5 + c % 2][0:2, :], p.sc[:, k, :], p.wring[:, c % 3, k, :],
                                                start=(k == 0), stop=(k == KT - 1))
                    last.then_inc(sem("w_used"), 1)
                if c >= 1:
                    pe.wait_ge(sem("mod_row"), c)
                    for b in range(4):
                        col = 2 * (4 * (c - 1) + b)
                        last = nc.tensor.transpose(ps[0][:, col:col + 2], p.mrow[0:2, (c - 1) % 2, b * P:(b + 1) * P],
                                                   p.ident[0:2, 0:2])
                    last.then_inc(sem("mod_turned"), 1)
            chunk = -1
            first_sample = [j for j, job in enumerate(jobs) if job[0] == "tm" and job[2] > 0][0]
            for j, (kind, c, i, a, b) in enumerate(jobs):
                if kind == "late":
                    pe.wait_ge(sem("late_sum"), LATE_STEPS * (i + 1))
                elif c != chunk:
                    w_arrived(pe, c)
                    chunk = c
                if j in (0, first_sample):
                    pe.wait_ge(sem("h_ready"), KT if j == 0 else 2 * KT)
                if j >= 8:
                    pe.wait_ge(sem("proj_out"), j - 7)
                bank = ps[j % 8]
                if kind == "late":
                    for blk in range(4):
                        for g in range(2):
                            last = nc.tensor.matmul(bank[:, 2 * blk + g:2 * blk + g + 1], sums_late[:, i % 3, g, blk * P:(blk + 1) * P],
                                                    p.ones[:, 0:1], start=True, stop=True)
                    last.then_inc(sem("proj"), 1)
                    continue
                for k in range(KT):
                    if kind == "tm":
                        last = nc.tensor.matmul(bank[:, 0:b - a], p.hT[:, k, i * P:(i + 1) * P],
                                                p.wring[:, c % 3, k, 0:b - a], start=(k == 0), stop=(k == KT - 1))
                    else:
                        lo, hi = (0, P) if i == 0 else (P, TOK)
                        last = nc.tensor.matmul(bank[:, 0:hi - lo], p.wring[:, c % 3, k, b * P:(b + 1) * P],
                                                p.hT[:, k, lo:hi], start=(k == 0), stop=(k == KT - 1))
                last.then_inc(sem("proj"), 1)


def proj_evac(p, j, kind, i, a, b):
    bank = p.ps[j % 8]
    if kind == "late":
        return p.mod[:, 4 * (EARLY + i):4 * (EARLY + i + 1), :], bank[:, 0:8].rearrange("p (n g) -> p n g", g=2)
    if kind == "tm":
        return p.proj[:, i, a:b], bank[:, 0:b - a]
    if i == 0:
        return p.qkvT[:, a, 1:1 + P], bank[:, 0:P]
    return p.qkvT[:, a, 131:131 + 4 * P], bank[:, :]


def conv(p):
    nc, sem, ps = p.nc, p.sem, p.ps
    with nc.Block() as block:
        @block.vector
        def _(dve):
            own = Chain(dve, sem("dve_conv"))
            for pair in range(3):
                for tap in range(3):
                    for b in (2 * pair, 2 * pair + 1):
                        w = p.vec[:, V_CONV + 3 * b + tap:V_CONV + 3 * b + tap + 1]
                        x = p.qkvT[:, b, tap:tap + LINE - 2]
                        if tap == 0:
                            n = own.mark(nc.vector.tensor_scalar(p.convd[:, b, :], x, w, None, ALU.mult))
                        else:
                            own.wait(6 * pair + 2 * tap - 1 + b % 2)
                            n = own.mark(nc.vector.scalar_tensor_tensor(
                                out=p.convd[:, b, :], in0=x, scalar=w, in1=p.convd[:, b, :],
                                op0=ALU.mult, op1=ALU.add))

        @block.scalar
        def _(act):
            for b in range(6):
                act.wait_ge(sem("dve_conv"), 6 * (b // 2) + 5 + b % 2)
                nc.scalar.activation(p.convd[:, b, :], p.convd[:, b, :], ACT.Silu).then_inc(sem("conv_silu"), 1)
            nc.scalar.activation(p.proj[:, :, GATE:BF], p.proj[:, :, GATE:BF], ACT.Silu).then_inc(sem("gate_silu"), 1)
            act.wait_ge(sem("gate_silu"), 1)
            for t in range(NT):
                for h, (a, b) in enumerate(((0, 512), (512, 768))):
                    act.wait_ge(sem("conv_turned"), 2 * t + h + 1)
                    nc.scalar.activation(p.qkv[:, t, a:b], ps[(2 * t + h) % 8][:, 0:b - a],
                                         ACT.Copy).then_inc(sem("qkv_out"), 1)

        @block.tensor
        def _(pe):
            for t in range(NT):
                lo = 0 if t == 0 else 130 + P * (t - 1)
                for h, (a, b) in enumerate(((0, 4), (4, 6))):
                    j = 2 * t + h
                    pe.wait_ge(sem("conv_silu"), b)
                    if j >= 8:
                        pe.wait_ge(sem("qkv_out"), j - 7)
                    for k in range(a, b):
                        last = nc.tensor.transpose(ps[j % 8][:, (k - a) * P:(k - a + 1) * P],
                                                   p.convd[:, k, lo:lo + P], p.ident)
                    last.then_inc(sem("conv_turned"), 1)


def delta(p, lay):
    nc, sem, ps = p.nc, p.sem, p.ps
    steps = [(0, 0)] + [(t, NT - t) for t in range(1, NT)]

    def tile_of(s, d):
        return steps[s][d]

    def heads(ap, n=HC):
        return ap.rearrange("p (h n) -> p h n", h=n)

    with nc.Block() as block:
        @block.sync
        def _(sp):
            sp.wait_ge(sem("states_zero"), 1)
            sp.wait_ge(sem("step0"), 1)
            sp.wait_ge(sem("step1"), 1)
            for d, name in enumerate(("sf", "sb")):
                sp.dma_start(p.d["out_" + name][bass.ds(lay, 1)].rearrange("l h d v -> d (l h) v"),
                             p.state[:, d, :, :]).then_inc(sem("store"), 16)
            sp.wait_ge(sem("store"), 32)
            for d, name in enumerate(("sf", "sb")):
                sp.dma_start(p.state[:, d, :, :],
                             p.d["in_" + name][bass.ds(lay, 1)].rearrange("l h d v -> d (l h) v")).then_inc(sem("load_state"), 16)

        @block.gpsimd
        def _(pool):
            nc.gpsimd.memset(p.state[:, :, :, :], 0.0).then_inc(sem("states_zero"), 1)
            for s in range(NT):
                for lvl in range(1, LEVELS):
                    for d in range(2):
                        pool.wait_ge(sem(f"lt_ready{d}"), s + 1)
                        n = doubling(s, lvl)
                        if n >= 2:
                            pool.wait_ge(sem(f"t1{d}"), n - 1)
                        nc.gpsimd.tensor_tensor(p.mlt[:, d, lvl_buf(n), :, :], p.lt[:, d, :, :],
                                                bc(p.lmask[:, d, lvl, :], 1, HC), ALU.mult).then_inc(sem(f"mlt{d}"), 1)

        @block.scalar
        def _(act):
            act.wait_ge(sem("squares_d"), NT)
            nc.scalar.activation(p.rd[:, :, :], p.ssd[:, :, :], ACT.Sqrt, bias=p.eps[:, 0:1]).then_inc(sem("root_d"), 1)
            act.wait_ge(sem("zabs"), 1)
            nc.scalar.activation(p.sp1[:, :, :], p.zab[:, :, :], ACT.Exp, scale=-1.0).then_inc(sem("exp_small"), 1)
            nc.scalar.activation(p.bet[:, :, :], p.proj[:, :, BF:BF + 8], ACT.Exp, scale=-1.0).then_inc(sem("exp_small"), 1)
            nc.scalar.activation(p.eal[:, :], p.row[:, R_ALOG:R_ALOG + 8], ACT.Exp).then_inc(sem("exp_small"), 1)
            act.wait_ge(sem("exp_small"), 3)
            nc.scalar.activation(p.sp1[:, :, :], p.sp1[:, :, :], ACT.Ln, bias=p.one[:, 0:1]).then_inc(sem("ln_small"), 1)
            act.wait_ge(sem("gcol_out"), 1)
            nc.scalar.activation(p.egc[:, :, :], p.gcol[:, :, :], ACT.Exp).then_inc(sem("egc"), 1)
            for s in range(NT):
                for d in range(2):
                    act.wait_ge(sem(f"kq_turned{d}"), s + 1)
                    if s >= 1:
                        act.wait_ge(sem(f"kk{d}"), s)
                    nc.scalar.activation(p.kT[:, d, :], ps[4 * d + 2][0:64, :], ACT.Copy).then_inc(sem(f"kqT{d}"), 1)
                    nc.scalar.activation(p.qT[:, d, :], ps[4 * d + 3][0:64, :], ACT.Copy).then_inc(sem(f"kqT{d}"), 1)
                for d in range(2):
                    act.wait_ge(sem(f"diff{d}"), s + 1)
                    if s >= 1:
                        act.wait_ge(sem(f"prep{d}"), 4 * s)
                    nc.scalar.activation(p.dec[:, d, :, :], p.dif[:, d, :, :], ACT.Exp).then_inc(sem(f"dec{d}"), 1)
                    if s >= 1:
                        act.wait_ge(sem(f"step{d}"), s)
                    nc.scalar.activation(p.egr[:, d, :, :], heads(ps[4 * d][0:64, :]), ACT.Exp).then_inc(sem(f"egr{d}"), 1)
                for d in range(2):
                    act.wait_ge(sem(f"x_turned{d}"), s + 1)
                    nc.scalar.activation(p.X[:, d, :, :], heads(ps[4 * d][:, :]), ACT.Copy).then_inc(sem(f"first_x{d}"), 1)
                for lvl in range(1, LEVELS):
                    for d in range(2):
                        n = doubling(s, lvl)
                        act.wait_ge(sem(f"t1{d}"), n + 1)
                        if n >= 1:
                            act.wait_ge(sem(f"t2{d}"), n)
                        nc.scalar.activation(p.t1s[:, d, :], ps[4 * d][:, :], ACT.Copy).then_inc(sem(f"t1s{d}"), 1)

        @block.vector
        def _(dve):
            own = Chain(dve, sem("dve_delta"))
            nc.vector.memset(p.oC[:, :, :], 0.0)
            for t in range(NT):
                if t >= 1:
                    dve.wait_ge(sem("squares_d"), t)
                own.link(nc.vector.tensor_tensor(p.junk[:, 0:512], p.qkv[:, t, 0:512], p.qkv[:, t, 0:512], ALU.mult))
                nc.vector.tensor_reduce(p.ssd[:, t, :], heads(p.junk[:, 0:512], 8), AX.X, ALU.add).then_inc(sem("squares_d"), 1)
            own.link(nc.vector.tensor_tensor(p.zz[:, :, :], p.proj[:, :, BF + 8:BF + 16],
                                             bc(p.row[:, R_DT:R_DT + 8], 1, NT), ALU.add))
            nc.vector.scalar_tensor_tensor(out=p.zab[:, :, :], in0=p.zz[:, :, :], scalar=-1.0, in1=p.zz[:, :, :],
                                           op0=ALU.mult, op1=ALU.max).then_inc(sem("zabs"), 1)
            dve.wait_ge(sem("root_d"), 1)
            own.link(nc.vector.reciprocal(p.rd[:, :, :], p.rd[:, :, :]))
            own.link(nc.vector.tensor_scalar(p.rd[:, :, 0:4], p.rd[:, :, 0:4], 0.125, None, ALU.mult))
            for t in range(NT):
                nc.vector.tensor_tensor(heads(p.qkv[:, t, 0:512], 8), heads(p.qkv[:, t, 0:512], 8),
                                        bc(p.rd[:, t, :], 2, 64), ALU.mult).then_inc(sem("qk_unit"), 1)
            dve.wait_ge(sem("exp_small"), 3)
            own.link(nc.vector.tensor_scalar(p.bet[:, :, :], p.bet[:, :, :], 1.0, None, ALU.add))
            own.link(nc.vector.reciprocal(p.bet[:, :, :], p.bet[:, :, :]))
            dve.wait_ge(sem("ln_small"), 1)
            own.link(nc.vector.scalar_tensor_tensor(out=p.g[:, :, :], in0=p.zz[:, :, :], scalar=0.0, in1=p.sp1[:, :, :],
                                                    op0=ALU.max, op1=ALU.add))
            nc.vector.scalar_tensor_tensor(out=p.g[:, :, :], in0=p.g[:, :, :], scalar=-1.0, in1=bc(p.eal[:, :], 1, NT),
                                           op0=ALU.mult, op1=ALU.mult).then_inc(sem("g_ready"), 1)
            dve.wait_ge(sem("gcol"), 1)
            nc.vector.tensor_copy(p.gcol[:, :, :], ps[0][:, 0:NT * 8].rearrange("p (t c) -> p t c", t=NT)).then_inc(sem("gcol_out"), 1)
            dve.wait_ge(sem("egc"), 1)
            for s in range(NT):
                for d in range(2):
                    t, c = tile_of(s, d), 4 * d
                    dve.wait_ge(sem(f"rows{d}"), s + 1)
                    own.link(nc.vector.tensor_tensor(p.dif[:, d, :, :], heads(ps[4 * d][:, :]),
                                                     bc(p.gcol[:, t, c:c + 4], 2, P), ALU.subtract))
                    nc.vector.tensor_scalar(p.dif[:, d, :, :], p.dif[:, d, :, :], 0.0, None, ALU.min).then_inc(sem(f"diff{d}"), 1)
                for d in range(2):
                    t, c = tile_of(s, d), 4 * d
                    dve.wait_ge(sem(f"dec{d}"), s + 1)
                    own.link(nc.vector.tensor_tensor(p.lt[:, d, :, :], p.dec[:, d, :, :], bc(p.bet[:, t, c:c + 4], 2, P), ALU.mult))
                    dve.wait_ge(sem(f"kk{d}"), s + 1)
                    nc.vector.tensor_tensor(p.lt[:, d, :, :], heads(ps[4 * d + 2][:, :]), p.lt[:, d, :, :], ALU.mult).then_inc(sem(f"lt_ready{d}"), 1)
                    dve.wait_ge(sem(f"lt_ready{d}"), s + 1)
                    own.link(nc.vector.tensor_tensor(p.XT[:, d, :, :], p.lt[:, d, :, :], bc(p.lmask[:, d, 0, :], 1, HC), ALU.mult))
                    nc.vector.tensor_tensor(p.XT[:, d, :, :], bc(p.ident, 1, HC), p.XT[:, d, :, :], ALU.subtract).then_inc(sem(f"x{d}"), 1)
                for d in range(2):
                    t = tile_of(s, d)
                    last = P - 1 if d == 0 else 0
                    kh = heads(p.qkv[:, t, 256:512])
                    nc.vector.tensor_tensor(p.kd[:, d, :, :], kh, p.dec[:, d, :, last:last + 1].to_broadcast([P, HC, 64]),
                                            ALU.mult).then_inc(sem(f"prep{d}"), 1)
                    own.link(nc.vector.tensor_tensor(p.qk[:, d, :, :], heads(ps[4 * d + 3][:, :]), p.dec[:, d, :, :], ALU.mult))
                    nc.vector.tensor_tensor(p.qk[:, d, :, :], p.qk[:, d, :, :], bc(p.imask[:, d, :], 1, HC), ALU.mult).then_inc(sem(f"prep{d}"), 1)
                    dve.wait_ge(sem(f"egr{d}"), s + 1)
                    dve.wait_ge(sem(f"kqT{d}"), 2 * s + 2)
                    nc.vector.tensor_tensor(p.qd[:, d, :, :], heads(p.qT[:, d, :]), p.egr[:, d, :, :], ALU.mult).then_inc(sem(f"prep{d}"), 1)
                for lvl in range(1, LEVELS):
                    for d in range(2):
                        n = doubling(s, lvl)
                        if lvl == KS_LEVEL + 1:
                            t, c = tile_of(s, d), 4 * d
                            dve.wait_ge(sem(f"ks{d}"), s + 1)
                            own.link(nc.vector.tensor_tensor(p.rv[:, d, :, :], heads(ps[4 * d + 2][:, 0:256]),
                                                             bc(p.egc[:, t, c:c + 4], 2, 64), ALU.mult))
                            nc.vector.tensor_tensor(p.rv[:, d, :, :], heads(p.qkv[:, t, 512:768]), p.rv[:, d, :, :],
                                                    ALU.subtract).then_inc(sem(f"prep{d}"), 1)
                        dve.wait_ge(sem(f"t2{d}"), n + 1)
                        if lvl < LEVELS - 1:
                            nc.vector.tensor_tensor(p.X[:, d, :, :], p.X[:, d, :, :], heads(ps[4 * d][:, :]), ALU.subtract).then_inc(sem(f"x{d}"), 1)
                        nc.vector.tensor_tensor(p.XT[:, d, :, :], p.XT[:, d, :, :], heads(ps[4 * d + 1][:, :]), ALU.subtract).then_inc(sem(f"x{d}"), 1)
                for d in range(2):
                    t, c = tile_of(s, d), 4 * d
                    dve.wait_ge(sem(f"w{d}"), s + 1)
                    nc.vector.tensor_tensor(p.w[:, d, :, :], heads(ps[4 * d + 1][:, 0:256]),
                                            bc(p.bet[:, t, c:c + 4], 2, 64), ALU.mult).then_inc(sem(f"w_out{d}"), 1)
                if s == 1:
                    dve.wait_ge(sem("load_state"), 32)
                for d in range(2):
                    t = tile_of(s, d)
                    last = P - 1 if d == 0 else 0
                    dve.wait_ge(sem(f"od{d}"), s + 1)
                    own.link(nc.vector.tensor_tensor(p.oC[:, t, :], p.oC[:, t, :], ps[4 * d + 1][:, 256:512], ALU.add))
                    own.link(nc.vector.tensor_tensor(p.state[:, d, :, :], p.state[:, d, :, :],
                                                     p.egr[:, d, :, last:last + 1].to_broadcast([64, HC, 64]), ALU.mult))
                    nc.vector.tensor_tensor(p.state[:, d, :, :], p.state[:, d, :, :], heads(ps[4 * d + 2][0:64, 0:256]),
                                            ALU.add).then_inc(sem(f"step{d}"), 1)

        @block.tensor
        def _(pe):
            pe.wait_ge(sem("g_ready"), 1)
            for t in range(NT):
                for d in range(2):
                    last = nc.tensor.matmul(ps[0][:, 8 * t + 4 * d:8 * t + 4 * d + 4], p.imask[:, d, :],
                                            p.g[:, t, 4 * d:4 * d + 4], start=True, stop=True)
            last.then_inc(sem("gcol"), 1)
            pe.wait_ge(sem("gcol_out"), 1)
            pe.wait_ge(sem("qk_unit"), NT)
            for s in range(NT):
                for d in range(2):
                    t = tile_of(s, d)
                    B = ps[4 * d:4 * d + 4]
                    if s >= 1:
                        pe.wait_ge(sem(f"step{d}"), s)
                    for h in range(HC):
                        nc.tensor.transpose(B[2][0:64, h * P:(h + 1) * P], p.qkv[:, t, 256 + 64 * h:320 + 64 * h], p.ident)
                    for h in range(HC):
                        mm = nc.tensor.transpose(B[3][0:64, h * P:(h + 1) * P], p.qkv[:, t, 64 * h:64 * h + 64], p.ident)
                    mm.then_inc(sem(f"kq_turned{d}"), 1)
                    for h in range(HC):
                        mm = nc.tensor.matmul(B[0][:, h * P:(h + 1) * P], p.g[:, t, 4 * d + h:4 * d + h + 1].to_broadcast([P, P]),
                                              p.imask[:, d, :], start=True, stop=True)
                    mm.then_inc(sem(f"rows{d}"), 1)
                for d in range(2):
                    B = ps[4 * d:4 * d + 4]
                    pe.wait_ge(sem(f"kqT{d}"), 2 * s + 2)
                    for h in range(HC):
                        k = p.kT[:, d, h * P:(h + 1) * P]
                        nc.tensor.matmul(B[2][:, h * P:(h + 1) * P], k, k, start=True, stop=True)
                    for h in range(HC):
                        mm = nc.tensor.matmul(B[3][:, h * P:(h + 1) * P], p.kT[:, d, h * P:(h + 1) * P],
                                              p.qT[:, d, h * P:(h + 1) * P], start=True, stop=True)
                    mm.then_inc(sem(f"kk{d}"), 1)
                for d in range(2):
                    pe.wait_ge(sem(f"x{d}"), X_STEPS * s + 1)
                    pe.wait_ge(sem(f"egr{d}"), s + 1)
                    for h in range(HC):
                        mm = nc.tensor.transpose(ps[4 * d][:, h * P:(h + 1) * P], p.XT[:, d, h, :], p.ident)
                    mm.then_inc(sem(f"x_turned{d}"), 1)
                for lvl in range(1, LEVELS):
                    for d in range(2):
                        B = ps[4 * d:4 * d + 4]
                        n = doubling(s, lvl)
                        pe.wait_ge(sem(f"mlt{d}"), n + 1)
                        if lvl == 1:
                            pe.wait_ge(sem(f"first_x{d}"), s + 1)
                        else:
                            pe.wait_ge(sem(f"x{d}"), X_STEPS * s + 1 + 2 * (lvl - 1))
                        for h in range(HC):
                            mm = nc.tensor.matmul(B[0][:, h * P:(h + 1) * P], p.mlt[:, d, lvl_buf(n), h, :],
                                                  p.X[:, d, h, :], start=True, stop=True)
                        mm.then_inc(sem(f"t1{d}"), 1)
                        if lvl == KS_LEVEL:
                            if s == 0:
                                pe.wait_ge(sem("states_zero"), 1)
                            if s == 1:
                                pe.wait_ge(sem("load_state"), 32)
                            for h in range(HC):
                                mm = nc.tensor.matmul(B[2][:, h * 64:h * 64 + 64], p.kT[:, d, h * P:(h + 1) * P],
                                                      p.state[:, d, h, :], start=True, stop=True)
                            mm.then_inc(sem(f"ks{d}"), 1)
                    for d in range(2):
                        B = ps[4 * d:4 * d + 4]
                        n = doubling(s, lvl)
                        pe.wait_ge(sem(f"t1s{d}"), n + 1)
                        if lvl < LEVELS - 1:
                            for h in range(HC):
                                nc.tensor.matmul(B[0][:, h * P:(h + 1) * P], p.XT[:, d, h, :],
                                                 p.t1s[:, d, h * P:(h + 1) * P], start=True, stop=True)
                        for h in range(HC):
                            mm = nc.tensor.matmul(B[1][:, h * P:(h + 1) * P], p.t1s[:, d, h * P:(h + 1) * P],
                                                  p.XT[:, d, h, :], start=True, stop=True)
                        mm.then_inc(sem(f"t2{d}"), 1)
                for d in range(2):
                    B = ps[4 * d:4 * d + 4]
                    pe.wait_ge(sem(f"prep{d}"), 4 * (s + 1))
                    pe.wait_ge(sem(f"x{d}"), X_STEPS * (s + 1))
                    for h in range(HC):
                        mm = nc.tensor.matmul(B[1][:, h * 64:h * 64 + 64], p.XT[:, d, h, :], p.rv[:, d, h, :], start=True, stop=True)
                    mm.then_inc(sem(f"w{d}"), 1)
                for d in range(2):
                    B = ps[4 * d:4 * d + 4]
                    pe.wait_ge(sem(f"w_out{d}"), s + 1)
                    for h in range(HC):
                        o = B[1][:, 256 + h * 64:320 + h * 64]
                        nc.tensor.matmul(o, p.qd[:, d, h, :], p.state[:, d, h, :], start=True, stop=False)
                        nc.tensor.matmul(o, p.qk[:, d, h, :], p.w[:, d, h, :], start=False, stop=True)
                    for h in range(HC):
                        mm = nc.tensor.matmul(B[2][0:64, h * 64:h * 64 + 64], p.kd[:, d, h, :], p.w[:, d, h, :],
                                              start=True, stop=True)
                    mm.then_inc(sem(f"od{d}"), 1)


def doubling(s, lvl):
    return (LEVELS - 1) * s + lvl - 1


def lvl_buf(n):
    return n % 2


def rope(p, own, x, n, t, u, v):
    nc = p.nc
    cos, sin = p.rope[:, 0, t - 1, :], p.rope[:, 1, t - 1, :]
    u = u[:, 0:n * 32].rearrange("p (n c) -> p n c", c=32)
    v = v[:, 0:n * 32].rearrange("p (n c) -> p n c", c=32)
    for half in range(2):
        for q in range(2):
            a, b = 16 * half + 8 * q, 16 * half + 8 * (1 - q)
            own.mark(nc.vector.tensor_tensor(u[:, :, a:a + 8], x[:, :, b:b + 8], bc(sin[:, a:a + 8], 1, n), ALU.mult))
    own.link(nc.vector.tensor_tensor(v, x, bc(cos, 1, n), ALU.mult))
    return nc.vector.tensor_tensor(x, u, v, ALU.add)


def norm_and_rope(p, dve, own):
    nc, sem = p.nc, p.sem
    for t in range(NT):
        if t >= 1:
            dve.wait_ge(sem("squares_l"), 2 * t)
        for i, (a, b) in enumerate(((QC, KVC), (KVC, KR))):
            nc.vector.tensor_tensor_reduce(out=p.junk[:, 256 * i:256 * i + b - a], in0=p.proj[:, t, a:b], in1=p.proj[:, t, a:b],
                                           scale=1.0, scalar=0.0, op0=ALU.mult, op1=ALU.add,
                                           accum_out=p.ssl[:, i, t:t + 1]).then_inc(sem("squares_l"), 1)
    dve.wait_ge(sem("root_l"), 2)
    own.link(nc.vector.reciprocal(p.rl[:, :, :], p.rl[:, :, :]))
    for t in range(NT):
        own.mark(nc.vector.scalar_tensor_tensor(out=p.proj[:, t, KVC:KR], in0=p.proj[:, t, KVC:KR], scalar=p.rl[:, 1, t:t + 1],
                                                in1=p.row[:, R_KVC:R_KVC + 128], op0=ALU.mult, op1=ALU.mult))
        own.link(nc.vector.scalar_tensor_tensor(out=p.proj[:, t, QC:KVC], in0=p.proj[:, t, QC:KVC], scalar=p.rl[:, 0, t:t + 1],
                                                in1=p.row[:, R_QC:R_QC + 256], op0=ALU.mult, op1=ALU.mult))
        if t >= 1:
            own.link(rope(p, own, p.proj[:, t, QA:VA].rearrange("p (n c) -> p n c", c=32), 16, t, p.xn[:, 0, :], p.xn[:, 1, :]))
            own.link(rope(p, own, p.proj[:, t, KR:GATE].rearrange("p (n c) -> p n c", c=32), 1, t, p.xn[:, 0, :], p.xn[:, 1, :]))
        own.mark(nc.vector.tensor_copy(p.krp[:, t, 64:96], p.proj[:, t, KR:GATE]))


def delta_out(p, dve, own):
    nc, sem = p.nc, p.sem
    sq = p.junk[:, 0:256].rearrange("p (h n) -> p h n", h=4)
    for t in range(NT):
        if t >= 1:
            dve.wait_ge(sem("squares_o"), t)
        own.link(nc.vector.tensor_tensor(p.junk[:, 0:256], p.oC[:, t, :], p.oC[:, t, :], ALU.mult))
        nc.vector.tensor_reduce(p.sso[:, t, :], sq, AX.X, ALU.add).then_inc(sem("squares_o"), 1)
    dve.wait_ge(sem("root_o"), 1)
    own.link(nc.vector.reciprocal(p.sso[:, :, :], p.sso[:, :, :]))
    for t in range(NT):
        o = p.oC[:, t, :].rearrange("p (h n) -> p h n", h=HC)
        own.link(nc.vector.tensor_tensor(o, o, bc(p.sso[:, t, :], 2, 64), ALU.mult))
        own.link(nc.vector.tensor_tensor(o, o, bc(p.row[:, R_ON:R_ON + 64], 1, HC), ALU.mult))
        own.mark(nc.vector.tensor_tensor(p.mixed[:, t, 768:1024], p.oC[:, t, :], p.proj[:, t, GATE:BF], ALU.mult))


def prepare_attention(p, lay):
    nc, d, sem, ps = p.nc, p.d, p.sem, p.ps

    jobs = []
    for t in range(NT):
        jobs += [("qk", t, 0), ("low", t, 0)]
    jobs += [("qk", NT, 0), ("low", NT, 0)]
    for h in range(HB):
        jobs += [("kn", h, 0), ("kn", h, 1)]
    jobs += [("v", t, 0) for t in range(6)]
    for t in range(NT):
        jobs += [("uq", t, 0), ("uq", t, 1), ]
        if t >= 1:
            jobs += [("qt", t - 1, 0), ("qt", t - 1, 1)]
    jobs += [("qt", NT - 1, 0), ("qt", NT - 1, 1)]
    at = {job: j for j, job in enumerate(jobs)}

    with nc.Block() as block:
        @block.sync
        def _(sp):
            one = bass.ds(lay, 1)
            sp.dma_start(p.cak[:, :], d["cache_a_k"][one].rearrange("l p n -> p (l n)")).then_inc(sem("load_cache"), 16)
            sp.dma_start(p.cav[:, :], d["cache_a_v"][one].rearrange("l p n -> p (l n)")).then_inc(sem("load_cache"), 16)
            sp.dma_start(p.cckv[:, :], d["cache_ckv"][one].rearrange("l p n -> p (l n)")).then_inc(sem("load_cache"), 16)
            sp.dma_start(p.ckr[:, 64:96], d["cache_kr"][one].rearrange("l p n -> p (l n)")).then_inc(sem("load_cache"), 16)
            sp.dma_start(p.wuq[:, :, :], d["w_uq"][one].rearrange("l p k n -> p (l k) n")).then_inc(sem("load_wuq"), 16)
            sp.dma_start(p.wukn[:, :], d["w_ukn"][one].rearrange("l p n -> p (l n)")).then_inc(sem("load_wuk"), 16)
            sp.dma_start(p.wukv[:, :], d["w_ukv"][one].rearrange("l p n -> p (l n)")).then_inc(sem("load_wuk"), 16)
            sp.dma_start(d["out_ak"][one].rearrange("l p n -> p (l n)"), p.proj[:, 0, KA:VA]).then_inc(sem("store_ctx"), 16)
            sp.dma_start(d["out_av"][one].rearrange("l p n -> p (l n)"), p.proj[:, 0, VA:QC]).then_inc(sem("store_ctx"), 16)
            sp.dma_start(d["out_ckv"][one].rearrange("l p n -> p (l n)"), p.proj[:, 0, KVC:KR]).then_inc(sem("store_ctx"), 16)
            sp.dma_start(d["out_kr"][one].rearrange("l p n -> p (l n)"), p.proj[:, 0, KR:GATE]).then_inc(sem("store_ctx"), 16)
            sp.wait_ge(sem("store_ctx"), 64)

        @block.gpsimd
        def _(pool):
            nc.gpsimd.memset(p.krp[:, :, 0:64], 0.0).then_inc(sem("pads"), 1)
            nc.gpsimd.memset(p.ckr[:, 0:64], 0.0).then_inc(sem("pads"), 1)

        @block.scalar
        def _(act):
            for j, (kind, t, half) in enumerate(jobs):
                if j == 8:
                    act.wait_ge(sem("squares_o"), NT)
                    nc.scalar.activation(p.sso[:, :, :], p.sso[:, :, :], ACT.Sqrt, bias=p.eps[:, 0:1],
                                         scale=1.0 / 64).then_inc(sem("root_o"), 1)
                b = ps[j % 8]
                act.wait_ge(sem("p_mm"), j + 1)
                tc, kc = (t * P, kcol(t) if t < NT else P)
                if kind == "qk":
                    if t < NT:
                        nc.scalar.activation(p.qTa[:, :, tc:tc + P], b[:, 0:256].rearrange("p (b n) -> p b n", b=2), ACT.Copy)
                    last = nc.scalar.activation(p.kTa[:, :, kc:kc + P], b[:, 256:512].rearrange("p (b n) -> p b n", b=2), ACT.Copy)
                elif kind == "low":
                    if t < NT:
                        nc.scalar.activation(p.qcT[:, :, tc:tc + P], b[:, 0:256].rearrange("p (b n) -> p b n", b=2), ACT.Copy)
                    nc.scalar.activation(p.ckvT[:, kc:kc + P], b[:, 256:384], ACT.Copy)
                    last = nc.scalar.activation(p.kTb[64:96, :, kc:kc + P], bc(b[64:96, 384:512], 1, HB), ACT.Copy)
                elif kind == "kn":
                    lo, hi = (0, 512) if half == 0 else (512, KEYS)
                    last = nc.scalar.activation(p.kTb[0:64, t, lo:hi], b[0:64, 0:hi - lo], ACT.Copy)
                elif kind == "v":
                    last = nc.scalar.activation(p.vb[:, t, :], b[:, :], ACT.Copy)
                elif kind == "uq":
                    if t >= 2:
                        act.wait_ge(sem("p_mm"), at[("qt", t - 2, 1)] + 1)
                    last = nc.scalar.activation(p.qb[:, t % 2, half * 384:half * 384 + 384], b[:, 0:384], ACT.Copy)
                else:
                    last = nc.scalar.activation(p.qTb[:, 4 * half:4 * half + 4, tc:tc + P],
                                                b[0:96, :].rearrange("p (h n) -> p h n", h=4), ACT.Copy)
                last.then_inc(sem("p_ev"), 1)

        @block.vector
        def _(dve):
            own = Chain(dve, sem("dve_prep"))
            delta_out(p, dve, own)
            for i in range(2):
                q1 = R_LAM + 64 * i
                nc.vector.tensor_tensor_reduce(out=p.junk[:, 512 + 32 * i:544 + 32 * i], in0=p.row[:, q1:q1 + 32], in1=p.row[:, q1 + 32:q1 + 64],
                                               scale=1.0, scalar=0.0, op0=ALU.mult, op1=ALU.add,
                                               accum_out=p.lam[:, i:i + 1]).then_inc(sem("lam_dot"), 1)
            for t in range(1, NT):
                dve.wait_ge(sem("p_ev"), at[("uq", t, 1)] + 1)
                x = p.qb[:, t % 2, :].rearrange("p (h c) -> p h c", c=96)[:, :, 64:96]
                own.wait(own.n)
                rope(p, own, x, HB, t, p.ru, p.rv2).then_inc(sem("q_roped"), 1)
                dve.wait_ge(sem("q_roped"), t)

        @block.tensor
        def _(pe):
            for j, (kind, t, half) in enumerate(jobs):
                b = ps[j % 8]
                if j >= 8:
                    pe.wait_ge(sem("p_ev"), j - 7)
                if kind in ("qk", "low"):
                    if j == 0:
                        pe.wait_ge(sem("pads"), 2)
                    if t == NT:
                        pe.wait_ge(sem("load_cache"), 64)
                if kind == "qk":
                    cols = ([p.proj[:, t, QA + P * i:QA + P * (i + 1)] for i in range(4)] if t < NT
                            else [None, None, p.cak[:, 0:128], p.cak[:, 128:256]])
                    for i, c in enumerate(cols):
                        if c is not None:
                            last = nc.tensor.transpose(b[:, i * P:(i + 1) * P], c, p.ident)
                elif kind == "low":
                    cols = ([p.proj[:, t, QC:QC + P], p.proj[:, t, QC + P:KVC], p.proj[:, t, KVC:KR], p.krp[:, t, :]] if t < NT
                            else [None, None, p.cckv[:, :], p.ckr[:, :]])
                    for i, c in enumerate(cols):
                        if c is not None:
                            last = nc.tensor.transpose(b[0:c.shape[1], i * P:(i + 1) * P], c, p.ident)
                elif kind == "kn":
                    if (t, half) == (0, 0):
                        pe.wait_ge(sem("load_wuk"), 32)
                        pe.wait_ge(sem("p_ev"), at[("low", NT, 0)] + 1)
                    lo, hi = (0, 512) if half == 0 else (512, KEYS)
                    last = nc.tensor.matmul(b[0:64, 0:hi - lo], p.wukn[:, t * 64:t * 64 + 64], p.ckvT[:, lo:hi], start=True, stop=True)
                elif kind == "v":
                    last = nc.tensor.matmul(b[:, :], p.ckvT[:, t * P:(t + 1) * P], p.wukv[:, :], start=True, stop=True)
                elif kind == "uq":
                    if (t, half) == (0, 0):
                        pe.wait_ge(sem("load_wuq"), 16)
                    for k in range(2):
                        last = nc.tensor.matmul(b[:, 0:384], p.qcT[:, k, t * P:(t + 1) * P], p.wuq[:, k, half * 384:half * 384 + 384],
                                                start=(k == 0), stop=(k == 1))
                else:
                    pe.wait_ge(sem("p_ev"), at[("uq", t, 1)] + 1)
                    if t >= 1:
                        pe.wait_ge(sem("q_roped"), t)
                    for h in range(4):
                        hh = 4 * half + h
                        last = nc.tensor.transpose(b[0:96, h * P:(h + 1) * P], p.qb[:, t % 2, hh * 96:hh * 96 + 96], p.ident)
                last.then_inc(sem("p_mm"), 1)


def attend(p):
    nc, sem, ps = p.nc, p.sem, p.ps
    maps, outs = [], []
    short, long = ([("b", 2 * g, "a", g, "b", 2 * g + 1, t) for t in tiles for g in range(HA)] for tiles in ((0,), range(1, NT)))
    groups = []
    for i, g in enumerate(long):
        groups.append(g)
        if i % (NT - 1) == NT - 2:
            groups.append(short[i // (NT - 1)])
    for *heads, t in groups:
        for kind, h in zip(heads[::2], heads[1::2]):
            maps += [(t, h, 0), (t, h, 1)] if kind == "a" else [(t, h, None)]
            outs.append((kind, t, h, len(maps)))
    out_after = {n: (o, kind, t, h) for o, (kind, t, h, n) in enumerate(outs)}

    def keys(t):
        return (0, P) if t == 0 else (P, KEYS)

    def value(kind, t, kt, h):
        if kind == "b":
            return p.vb[:, kt, h * 64:h * 64 + 64]
        if kt == 1:
            return p.cav[:, h * 64:h * 64 + 64]
        return p.proj[:, 0 if kt == 0 else kt - 1, VA + h * 64:VA + h * 64 + 64]

    A, B = 32.0 ** -0.5, 96.0 ** -0.5
    def score_bank(m):
        return (0, 2, 6)[m % 3]

    def sums_of(kind):
        return ps[5][:, P:P + 64] if kind == "a" else ps[5][0:64, P:2 * P]

    with nc.Block() as block:
        @block.tensor
        def _(pe):
            def scores(m):
                t, h, i = maps[m]
                lo, hi = keys(t)
                s = score_bank(m)
                if m >= 3:
                    pe.wait_ge(sem("a_exp"), m - 2)
                if i is None:
                    q = p.qTb[:, h, t * P:(t + 1) * P]
                    k = p.kTb[:, h, lo:hi]
                else:
                    c = 2 * h + i
                    r = 32 * (c % 4)
                    q = p.qTa[r:r + 32, c // 4, t * P:(t + 1) * P]
                    k = p.kTa[r:r + 32, c // 4, lo:hi]
                n = min(hi - lo, 512)
                last = nc.tensor.matmul(ps[s][:, 0:n], q, k[:, 0:n], start=True, stop=True)
                if hi - lo > 512:
                    last = nc.tensor.matmul(ps[s + 1][:, 0:P], q, k[:, 512:640], start=True, stop=True)
                last.then_inc(sem("a_scores"), 1)

            def turn(o):
                kind, t, h, n = outs[o]
                pe.wait_ge(sem("a_weighed"), o + 1)
                if o >= 1:
                    pe.wait_ge(sem("a_turned_out"), o)
                src = p.prob[:, (n - 1) % PROBS, :]
                for j in range((keys(t)[1] - keys(t)[0]) // P):
                    if j == 4:
                        pe.wait_ge(sem("a_out"), o)
                    last = nc.tensor.transpose(ps[4 + j // 4][:, (j % 4) * P:(j % 4 + 1) * P], src[:, j * P:(j + 1) * P], p.ident)
                last.then_inc(sem("a_turned"), 1)

            def sums(o):
                kind, t, h, n = outs[o]
                pe.wait_ge(sem("a_turned_out"), o + 1)
                if o >= 1:
                    pe.wait_ge(sem("a_out"), o)
                nk = (keys(t)[1] - keys(t)[0]) // P
                for j in range(nk):
                    v, pT = value(kind, t, j if t == 0 else j + 1, h), p.probT[:, o % 2, j * P:(j + 1) * P]
                    flags = dict(start=(j == 0), stop=(j == nk - 1))
                    if kind == "a":
                        last = nc.tensor.matmul(sums_of(kind), pT, v, **flags)
                    else:
                        last = nc.tensor.matmul(sums_of(kind), v, pT, **flags)
                last.then_inc(sem("a_sums"), 1)

            o = 0
            for m in range(len(maps) + 4):
                if m < len(maps):
                    scores(m)
                if m - 3 in out_after:
                    sums(out_after[m - 3][0])
                if m - 2 in out_after:
                    turn(out_after[m - 2][0])

        @block.scalar
        def _(act):
            act.wait_ge(sem("lam_dot"), 2)
            nc.scalar.activation(p.lam[:, 2:4], p.lam[:, 0:2], ACT.Exp).then_inc(sem("lam_exp"), 1)

            def turned_out(o):
                kind, t, h, n = outs[o]
                act.wait_ge(sem("a_turned"), o + 1)
                if o >= 2:
                    act.wait_ge(sem("a_sums"), o - 1)
                nk = (keys(t)[1] - keys(t)[0])
                last = nc.scalar.activation(p.probT[:, o % 2, 0:min(nk, 512)], ps[4][:, 0:min(nk, 512)], ACT.Copy)
                if nk > 512:
                    last = nc.scalar.activation(p.probT[:, o % 2, 512:nk], ps[5][:, 0:P], ACT.Copy)
                last.then_inc(sem("a_turned_out"), 1)

            for m in range(len(maps) + 4):
                o, kind = out_after.get(m - 2, (None, None))[0:2]
                if kind == "a":
                    turned_out(o)
                if m < len(maps):
                    t, h, i = maps[m]
                    nk = keys(t)[1] - keys(t)[0]
                    act.wait_ge(sem("a_max"), m + 1)
                    if m >= PROBS:
                        done = [o for o, x in enumerate(outs) if x[3] > m - PROBS]
                        act.wait_ge(sem("a_turned"), done[0] + 1)
                    sc = p.score2(score_bank(m), nk)
                    nc.scalar.activation(p.prob[:, m % PROBS, 0:nk], sc, ACT.Exp, bias=p.nmax[:, m % 4:m % 4 + 1],
                                         scale=B if i is None else A, accum_out=p.esum[:, m % 4:m % 4 + 1]).then_inc(sem("a_exp"), 1)
                if kind == "b":
                    turned_out(o)
            act.wait_ge(sem("squares_a"), NT)
            nc.scalar.activation(p.ssa[:, :, :], p.ssa[:, :, :], ACT.Sqrt, bias=p.eps[:, 0:1],
                                 scale=1.0 / 64).then_inc(sem("root_a"), 1)

        @block.vector
        def _(dve):
            own = Chain(dve, sem("dve_attend"))
            dve.wait_ge(sem("lam_exp"), 1)
            own.link(nc.vector.tensor_tensor(p.lam[:, 4:5], p.lam[:, 3:4], p.lam[:, 2:3], ALU.subtract))
            own.link(nc.vector.tensor_tensor(p.lam[:, 5:6], p.lam[:, 4:5], p.row[:, R_LI:R_LI + 1], ALU.subtract))

            def max_of(m):
                t, h, i = maps[m]
                nk = keys(t)[1] - keys(t)[0]
                dve.wait_ge(sem("a_scores"), m + 1)
                if m >= 4:
                    dve.wait_ge(sem("a_exp"), m - 3)
                own.link(nc.vector.tensor_reduce(p.mx[:, m % 4:m % 4 + 1], p.score2(score_bank(m), nk), AX.X, ALU.max))
                nc.vector.tensor_scalar(p.nmax[:, m % 4:m % 4 + 1], p.mx[:, m % 4:m % 4 + 1], -(B if i is None else A), None,
                                        ALU.mult).then_inc(sem("a_max"), 1)

            def weigh(o):
                kind, t, h, n = outs[o]
                dve.wait_ge(sem("a_exp"), n)
                m = n - 1
                nk = keys(t)[1] - keys(t)[0]
                r0, r1 = (p.r01[:, o % 2, i:i + 1] for i in range(2))
                if kind == "b":
                    own.link(nc.vector.reciprocal(r0, p.esum[:, m % 4:m % 4 + 1]))
                    nc.vector.tensor_scalar(p.prob[:, m % PROBS, 0:nk], p.prob[:, m % PROBS, 0:nk], r0, None,
                                            ALU.mult).then_inc(sem("a_weighed"), 1)
                    return
                own.mark(nc.vector.reciprocal(r0, p.esum[:, (m - 1) % 4:(m - 1) % 4 + 1]))
                own.link(nc.vector.reciprocal(r1, p.esum[:, m % 4:m % 4 + 1]))
                own.link(nc.vector.tensor_tensor(r1, r1, p.lam[:, 5:6], ALU.mult))
                own.link(nc.vector.tensor_scalar(p.prob[:, (m - 1) % PROBS, 0:nk], p.prob[:, (m - 1) % PROBS, 0:nk], r0, None, ALU.mult))
                nc.vector.scalar_tensor_tensor(out=p.prob[:, m % PROBS, 0:nk], in0=p.prob[:, m % PROBS, 0:nk], scalar=r1,
                                               in1=p.prob[:, (m - 1) % PROBS, 0:nk], op0=ALU.mult, op1=ALU.add).then_inc(sem("a_weighed"), 1)

            def out(o):
                kind, t, h, n = outs[o]
                dve.wait_ge(sem("a_sums"), o + 1)
                if kind == "a":
                    nc.vector.tensor_copy(p.mixed[:, t, h * 64:h * 64 + 64], sums_of(kind)).then_inc(sem("a_out"), 1)
                else:
                    r, c = 64 * (h % 2), W_A + P * (h // 2)
                    nc.vector.tensor_copy(p.mixed[r:r + 64, t, c:c + P], sums_of(kind)).then_inc(sem("a_out"), 1)

            for m in range(len(maps) + 5):
                if m < len(maps):
                    max_of(m)
                if m - 3 in out_after:
                    out(out_after[m - 3][0])
                if m in out_after:
                    weigh(out_after[m][0])
            dve.wait_ge(sem("a_out"), len(outs))
            for t in range(NT):
                x = p.mixed[:, t, 0:256]
                if t >= 1:
                    dve.wait_ge(sem("squares_a"), t)
                own.link(nc.vector.tensor_tensor(p.junk[:, 0:256], x, x, ALU.mult))
                nc.vector.tensor_reduce(p.ssa[:, t, :], p.junk[:, 0:256].rearrange("p (h n) -> p h n", h=4), AX.X,
                                        ALU.add).then_inc(sem("squares_a"), 1)
            own.link(nc.vector.tensor_scalar(p.gsub[:, :], p.row[:, R_SUB:R_SUB + 64], p.row[:, R_LI + 1:R_LI + 2], None, ALU.mult))
            dve.wait_ge(sem("root_a"), 1)
            own.link(nc.vector.reciprocal(p.ssa[:, :, :], p.ssa[:, :, :]))
            for t in range(NT):
                x = p.mixed[:, t, 0:256].rearrange("p (h n) -> p h n", h=4)
                own.link(nc.vector.tensor_tensor(x, x, bc(p.ssa[:, t, :], 2, 64), ALU.mult))
                own.mark(nc.vector.tensor_tensor(x, x, bc(p.gsub[:, :], 1, 4), ALU.mult))


def project_out(p, lay):
    nc, d, sem, ps = p.nc, p.d, p.sem, p.ps
    vecs = [p.mod[:, 16:24, :], p.A2[:, :, :], p.mod[:, 24:32, :], p.mod[:, 40:48, :]]
    units = [(v, g, half) for v in range(4) for g in range(2) for half in range(2)]

    def row_of(v, g):
        return p.gt2[:, g, :] if v == 3 else p.rows[:, v, g, :]

    with nc.Block() as block:
        @block.sync
        def _(sp):
            load_weights_out(p, sp, lay, range(0, 2))

        @block.tensor
        def _(pe):
            for t in range(NT):
                if t >= 2:
                    pe.wait_ge(sem("m_out"), t - 1)
                for i, k in enumerate(UNTURNED):
                    last = nc.tensor.transpose(ps[t % 2][:, i * P:(i + 1) * P], p.mixed[:, t, k * P:(k + 1) * P], p.ident)
                last.then_inc(sem("m_turned"), 1)
            for u in range(len(units)):
                pe.wait_ge(sem("diag2"), u + 1)
                if u >= 2:
                    pe.wait_ge(sem("row_out"), u - 1)
                nc.tensor.matmul(ps[2 + u % 2][:, :], p.ones, p.diag4[:, u % 2, :], start=True, stop=True).then_inc(sem("row_mm"), 1)
            pe.wait_ge(sem("m_out"), NT)
            for t in range(NT):
                for c in range(2):
                    j = 2 * t + c
                    if t == 0:
                        pe.wait_ge(sem(f"load_v{c}"), 16)
                    if j >= 4:
                        pe.wait_ge(sem("res1"), j - 3)
                    for k in range(KT):
                        turned = (p.mixedT[:, UNTURNED.index(k), t * P:(t + 1) * P] if k in UNTURNED
                                  else p.mixed[:, t, k * P:(k + 1) * P])
                        last = nc.tensor.matmul(ps[4 + j % 4][:, :], turned, p.wring2[:, c, k, :],
                                                start=(k == 0), stop=(k == KT - 1))
                    last.then_inc(sem("wout_mm"), 1)
            for t in range(NT):
                pe.wait_ge(sem("h2_ready"), t + 1)
                if t >= 1:
                    pe.wait_ge(sem("h2T_out"), 2 * t)
                for k in range(KT):
                    last = nc.tensor.transpose(ps[k // 4][:, (k % 4) * P:(k % 4 + 1) * P], p.mixed[:, t, k * P:(k + 1) * P], p.ident)
                last.then_inc(sem("h2_turned"), 1)

        @block.scalar
        def _(act):
            for t in range(NT):
                act.wait_ge(sem("m_turned"), t + 1)
                nc.scalar.activation(p.mixedT[:, :, t * P:(t + 1) * P],
                                     ps[t % 2].rearrange("p (k n) -> p k n", k=4), ACT.Copy).then_inc(sem("m_out"), 1)
            for u, (v, g, half) in enumerate(units):
                act.wait_ge(sem("row_mm"), u + 1)
                nc.scalar.activation(row_of(v, g)[:, half * 512:half * 512 + 512], ps[2 + u % 2], ACT.Copy).then_inc(sem("row_out"), 1)
            for t in range(NT):
                act.wait_ge(sem("res1"), 2 * t + 2)
                nc.scalar.activation(p.junk[:, :], p.x[:, t, :], ACT.Square, accum_out=p.ss1[:, t:t + 1]).then_inc(sem("square2"), 1)
                act.wait_ge(sem("square2"), t + 1)
                nc.scalar.activation(p.rt1[:, t:t + 1], p.ss1[:, t:t + 1], ACT.Sqrt, bias=p.eps[:, 0:1], scale=1.0 / D).then_inc(sem("root2"), 1)
            for t in range(NT):
                act.wait_ge(sem("h2_turned"), t + 1)
                for h in range(2):
                    nc.scalar.activation(p.h2T[:, 4 * h:4 * h + 4, t * P:(t + 1) * P],
                                         ps[h].rearrange("p (k n) -> p k n", k=4), ACT.Copy).then_inc(sem("h2T_out"), 1)

        @block.vector
        def _(dve):
            own = Chain(dve, sem("dve_out"))
            for u, (v, g, half) in enumerate(units):
                if u >= 2:
                    dve.wait_ge(sem("row_mm"), u - 1)
                nc.vector.tensor_tensor(p.diag4[:, u % 2, :].rearrange("p (k n) -> p k n", k=4), bc(p.ident, 1, 4),
                                        bc(vecs[v][:, 4 * half:4 * half + 4, g], 2, P), ALU.mult).then_inc(sem("diag2"), 1)
            dve.wait_ge(sem("row_out"), len(units))

            def norm(t):
                g = 0 if t == 0 else 1
                dve.wait_ge(sem("root2"), t + 1)
                own.link(nc.vector.reciprocal(p.rt1[:, t:t + 1], p.rt1[:, t:t + 1]))
                own.link(nc.vector.scalar_tensor_tensor(out=p.mixed[:, t, :], in0=p.x[:, t, :], scalar=p.rt1[:, t:t + 1],
                                                        in1=p.rows[:, 1, g, :], op0=ALU.mult, op1=ALU.mult))
                nc.vector.tensor_tensor(p.mixed[:, t, :], p.mixed[:, t, :], p.rows[:, 2, g, :], ALU.add).then_inc(sem("h2_ready"), 1)

            for t in range(NT):
                g = 0 if t == 0 else 1
                for c in range(2):
                    j = 2 * t + c
                    cols = slice(c * 512, c * 512 + 512)
                    dve.wait_ge(sem("wout_mm"), j + 1)
                    own.link(nc.vector.tensor_tensor(p.gated[:, cols], ps[4 + j % 4], p.rows[:, 0, g, cols], ALU.mult))
                    nc.vector.tensor_tensor(p.x[:, t, cols], p.x[:, t, cols], p.gated[:, cols], ALU.add).then_inc(sem("res1"), 1)
                if t >= 1:
                    norm(t - 1)
            norm(NT - 1)


def load_weights_out(p, sp, lay, chunks):
    for c in chunks:
        if c >= 2:
            if c < 4:
                sp.wait_ge(p.sem("wout_mm"), 2 * NT)
            else:
                sp.wait_ge(p.sem("pq_mm"), 8 * (c - 3))
        src = p.d["w_out"] if c < 2 else p.d["w_pq"]
        a = WCH * (c if c < 2 else c - 2)
        sp.dma_start(p.wring2[:, c % 2, :, :], src[bass.ds(lay, 1), :, :, a:a + WCH].rearrange("l p k n -> p (l k) n")).then_inc(p.sem(f"load_v{c % 2}"), 16)


def flat(ap):
    return ap.rearrange("p t n -> p (t n)")


def route_piece(p, dve, steps, i, n):
    nc, sem, v = p.nc, p.sem, p.nc.vector
    a, b = (0, 1)
    row = [p.r_sub[:, 0:NK], p.r_sub[:, NK:2 * NK]]

    def step():
        dve.wait_ge(sem("piece"), steps)
        dve.reg_add(steps, steps, 1)

    def mark(ins):
        ins.then_inc(sem("piece"), 1)

    step()
    if i == 0:
        mark(v.tensor_copy(p.r_sub[:, :], flat(p.sub)[:, bass.ds(n * (2 * NK), 2 * NK)]))
    elif i in (1, 3):
        c = slice(0, 8) if i == 1 else slice(8, 16)
        v.max(p.r_top[:, a, c], row[a])
        mark(v.max(p.r_top[:, b, c], row[b]))
    elif i in (2, 4):
        c = slice(0, 8) if i == 2 else slice(8, 16)
        v.max_index(p.r_ix[:, a, c], p.r_top[:, a, c], row[a])
        mark(v.max_index(p.r_ix[:, b, c], p.r_top[:, b, c], row[b]))
        if i == 2:
            step()
            v.match_replace(row[a], p.r_top[:, a, c], row[a], NEG)
            mark(v.match_replace(row[b], p.r_top[:, b, c], row[b], NEG))
    elif i == 5:
        v.tensor_tensor(p.r_cand[:, :].rearrange("p (i j) -> p i j", i=TOPK), bc(p.r_top[:, a, :], 2, TOPK),
                        bc(p.r_top[:, b, :], 1, TOPK), ALU.add)
        mark(v.tensor_copy(p.r_ixf[:, :, :], p.r_ix[:, :, :]))
    elif i in (6, 9):
        c = slice(0, 8) if i == 6 else slice(8, 16)
        mark(v.max(p.r_best[:, c], p.r_cand[:, :]))
    elif i in (7, 10):
        c = slice(0, 8) if i == 7 else slice(8, 16)
        mark(v.max_index(p.r_pos[:, c], p.r_best[:, c], p.r_cand[:, :]))
    elif i == 8:
        mark(v.match_replace(p.r_cand[:, :], p.r_best[:, 0:8], p.r_cand[:, :], NEG))
    elif i == 11:
        v.tensor_scalar(p.r_ij[:, a, :], p.r_pos[:, :], 4, None, ALU.logical_shift_right)
        mark(v.tensor_scalar(p.r_ij[:, b, :], p.r_pos[:, :], 15, None, ALU.bitwise_and))
    elif i == 12:
        v.tensor_tensor(p.r_gate[:, :], p.r_best[:, :], p.r_best[:, 0:1].to_broadcast([P, TOPK]),
                        ALU.subtract).then_inc(sem("centred"), 1)
        mark(v.tensor_copy(p.r_ijf[:, :, :], p.r_ij[:, :, :]))
    elif i == 13:
        v.tensor_tensor(p.r_pick[:, a, :, :], bc(p.r_ijf[:, a, :], 2, TOPK), bc(p.io16, 1, TOPK), ALU.is_equal)
        mark(v.tensor_tensor(p.r_pick[:, b, :, :], bc(p.r_ijf[:, b, :], 2, TOPK), bc(p.io16, 1, TOPK), ALU.is_equal))
    elif i == 14:
        mark(v.tensor_tensor(p.r_pick[:, :, :, :], p.r_pick[:, :, :, :], bc(p.r_ixf[:, :, :], 2, TOPK), ALU.mult))
    else:
        mark(v.tensor_reduce(p.r_ex[:, :, :], p.r_pick[:, :, :, :], AX.X, ALU.add))
        dve.wait_ge(sem("gate_exp"), n + 1)
        step()
        v.reciprocal(p.r_gs[:, 0:1], p.r_gs[:, 1:2])
        mark(v.scalar_tensor_tensor(out=p.r_e[:, :], in0=p.r_ex[:, a, :], scalar=float(NK), in1=p.r_ex[:, b, :],
                                    op0=ALU.mult, op1=ALU.add))
        step()
        cols = bass.ds(n * TOPK, TOPK)
        v.tensor_scalar(flat(p.eidx)[:, cols], p.r_e[:, :], p.row[:, R_OFF:R_OFF + 1], None,
                        ALU.add).then_inc(sem("routed"), 1)
        mark(v.tensor_scalar(flat(p.gat)[:, cols], p.r_gate[:, :], p.r_gs[:, 0:1], None, ALU.mult))


def route_gates(p, act, n):
    act.wait_ge(p.sem("centred"), n + 1)
    p.nc.scalar.activation(p.r_gate[:, :], p.r_gate[:, :], ACT.Exp, accum_out=p.r_gs[:, 1:2]).then_inc(p.sem("gate_exp"), 1)


def route(p, lay):
    nc, d, sem, ps = p.nc, p.d, p.sem, p.ps
    C = 4
    jobs = []
    for c in range(C + 1):
        if c < C:
            jobs += [("q", c, b, g) for b in range(4) for g in range(2)]
        if c >= 1:
            jobs += [("s", c - 1, t, 0) for t in range(NT)]
    at = {job: j for j, job in enumerate(jobs)}
    gates_after = [at[("q", 2 + n, 3, 1)] for n in range(AHEAD)]
    items_here = at[("s", 0, 0, 0)] + 1

    with nc.Block() as block:
        @block.vector
        def _(dve):
            steps = dve.alloc_register("first_route_steps")
            dve.reg_mov(steps, 1)
            dve.wait_ge(sem("r_out"), items_here)
            nc.vector.memset(p.r_gs[:, :], 0.0).then_inc(sem("piece"), 1)
            with dve.Fori(0, AHEAD) as n:
                for i in range(PIECES):
                    route_piece(p, dve, steps, i, n)

        @block.sync
        def _(sp):
            sp.dma_start(p.keysT[:, :], d["keysT"][bass.ds(lay, 1)].rearrange("l p n -> p (l n)")).then_inc(sem("load_keys"), 16)
            load_weights_out(p, sp, lay, range(2, 6))

        @block.tensor
        def _(pe):
            for j, (kind, c, i, g) in enumerate(jobs):
                if j >= 8:
                    pe.wait_ge(sem("r_out"), j - 7)
                b = ps[j % 8]
                if kind == "q":
                    if (i, g) == (0, 0):
                        pe.wait_ge(sem(f"load_v{c % 2}"), 16 * (2 + c // 2))
                    lo, hi = (0, P) if g == 0 else (P, TOK)
                    for k in range(KT):
                        last = nc.tensor.matmul(b[:, 0:hi - lo], p.wring2[:, c % 2, k, i * P:(i + 1) * P], p.h2T[:, k, lo:hi],
                                                start=(k == 0), stop=(k == KT - 1))
                    last.then_inc(sem("pq_mm"), 1)
                else:
                    if i == 0:
                        pe.wait_ge(sem("load_keys"), 16)
                        pe.wait_ge(sem("r_out"), at[("q", c, 3, 1)] + 1)
                    for q in range(4):
                        last = nc.tensor.matmul(b[:, q * P:(q + 1) * P], p.qpT[:, c % 2, q, i * P:(i + 1) * P],
                                                p.keysT[:, (4 * c + q) * P:(4 * c + q + 1) * P], start=True, stop=True)
                    last.then_inc(sem("sc_mm"), 1)

        @block.scalar
        def _(act):
            for j, (kind, c, i, g) in enumerate(jobs):
                b = ps[j % 8]
                if kind == "q":
                    act.wait_ge(sem("pq_mm"), 8 * c + 2 * i + g + 1)
                    if c >= 2 and (i, g) == (0, 0):
                        act.wait_ge(sem("sc_mm"), NT * (c - 1))
                    lo, hi = (0, P) if g == 0 else (P, TOK)
                    nc.scalar.activation(p.qpT[:, c % 2, i, lo:hi], b[:, 0:hi - lo], ACT.Copy).then_inc(sem("r_out"), 1)
                else:
                    act.wait_ge(sem("sc_mm"), NT * c + i + 1)
                    nc.scalar.activation(p.sub[:, i, 512 * c:512 * c + 512], b, ACT.Copy).then_inc(sem("r_out"), 1)
                if j in gates_after:
                    route_gates(p, act, gates_after.index(j))


def experts(p, lay):
    nc, d, sem, ps = p.nc, p.d, p.sem, p.ps
    H = RING

    def tile(ap, t):
        return ap[:, t, :] if type(t) is int else ap[:, bass.ds(t, 1), :].rearrange("p a n -> p (a n)")

    with nc.Block() as block:
        @block.gpsimd
        def _(pool):
            free = pool.alloc_register("rows_free")
            pool.reg_mov(free, 1)
            staged = pool.alloc_register("halves_staged")
            pool.reg_mov(staged, 1)

            def row_is_free():
                pool.wait_ge(sem("row_free"), free)
                pool.reg_add(free, free, 1)

            def head(t, h, n):
                for half in range(2):
                    row_is_free()
                    if half == 0:
                        pool.wait_ge(sem("routed"), n + 1)
                    nc.gpsimd.tensor_copy(p.stage[:, half, :], tile(p.eidx, t)[:, bass.ds(h * TOPK + half * H, H)]).then_inc(sem("staged"), 1)
                    pool.wait_ge(sem("staged"), staged)
                    pool.reg_add(staged, staged, 1)
                    for s in range(H):
                        if s > 0:
                            row_is_free()
                        nc.gpsimd.indirect_dma_start(out=p.uv[:, s, :], out_offset=None, in_=d["peer_uv"],
                                                     in_offset=bass.IndirectOffsetOnAxis(ap=p.stage[:, half, s:s + 1], axis=0)
                                                     ).then_inc(sem(f"row_in{s}"), 16)

            with pool.Fori(0, NT) as t:
                with pool.Fori(0, NH) as h:
                    head(t, h, t * NH + h)

        @block.vector
        def _(dve):
            steps = dve.alloc_register("route_steps")
            dve.reg_mov(steps, 1 + AHEAD * STEPS)

            def tile_pass(t, heads):
                g = 0 if type(t) is int and t == 0 else 1
                nc.vector.tensor_copy(p.hcur[:, :], tile(p.mixed, t)).then_inc(sem("h_here"), 1)
                for lo, hi, more in heads:
                    with dve.Fori(lo, hi) as h:
                        head_pass(t, h, more)
                for c in range(2):
                    cols = slice(c * 512, c * 512 + 512)
                    dve.wait_ge(sem("tile_sum"), t + 1)
                    nc.vector.tensor_tensor(p.y[:, cols], ps[c], p.gt2[:, g, cols], ALU.mult).then_inc(sem("y_read"), 1)
                dve.wait_ge(sem("y_read"), 2 * t + 2)
                nc.vector.tensor_tensor(tile(p.x, t), tile(p.x, t), p.y[:, :], ALU.add).then_inc(sem("residual"), 1)
                dve.wait_ge(sem("residual"), t + 1)

            def head_pass(t, h, more):
                n = t * NH + h
                rows = dve.snap((lay * NT * NH + n) * 32)
                dve.wait_ge(sem("h_here"), t + 1)
                for s in range(TOPK):
                    dve.wait_ge(sem(f"row_in{s % H}"), rows + (s // H + 1) * 16)
                    nc.vector.tensor_tensor_reduce(out=p.uv[:, s % H, 0:D], in0=p.uv[:, s % H, 0:D], in1=p.hcur[:, :], scale=1.0,
                                                   scalar=0.0, op0=ALU.mult, op1=ALU.add, accum_out=p.dot[:, s:s + 1]).then_inc(sem("dots"), 1)
                    if more:
                        route_piece(p, dve, steps, s, n + AHEAD)
                    if s % 2 == 1 and s >= 3:
                        weigh(t, h, n, s // 2 - 1)
                weigh(t, h, n, NH - 1)

            def weigh(t, h, n, q):
                dve.wait_ge(sem("gelus"), n * NH + q + 1)
                nc.vector.tensor_tensor(p.wgt[:, 2 * q:2 * q + 2], p.act16[:, 2 * q:2 * q + 2],
                                        tile(p.gat, t)[:, bass.ds(h * TOPK + 2 * q, 2)], ALU.mult).then_inc(sem("weights"), 1)

            tile_pass(0, [(0, NH, True)])
            with dve.Fori(1, NT - 1) as t:
                tile_pass(t, [(0, NH, True)])
            tile_pass(NT - 1, [(0, NH - AHEAD, True), (NH - AHEAD, NH, False)])

        @block.scalar
        def _(act):
            nc.scalar.activation(p.zero[:, :], p.ident, ACT.Copy, scale=0.0).then_inc(sem("zeros"), 1)

            def head(n, more):
                for q in range(NH + 1):
                    if q < NH:
                        act.wait_ge(sem("dots"), n * TOPK + 2 * q + 2)
                        nc.scalar.activation(p.act16[:, 2 * q:2 * q + 2], p.dot[:, 2 * q:2 * q + 2], ACT.Gelu_apprx_tanh).then_inc(sem("gelus"), 1)
                    if more and q == 7:
                        route_gates(p, act, n + AHEAD)
                    if q >= 1:
                        act.wait_ge(sem("weights"), n * NH + q)
                        for s in (2 * q - 2, 2 * q - 1):
                            act.wait_ge(sem("row_free"), n * TOPK + s + 1)
                            nc.scalar.activation(p.diag[:, s % H, :], p.ident, ACT.Copy, scale=p.wgt[:, s:s + 1]).then_inc(sem("diags"), 1)

            with act.Fori(0, NT * NH - AHEAD) as n:
                head(n, True)
            with act.Fori(NT * NH - AHEAD, NT * NH) as n:
                head(n, False)

        @block.tensor
        def _(pe):
            def mark(inc):
                nc.tensor.matmul(ps[2][:, 0:8], p.ident, p.ident[:, 0:8], start=True, stop=True).then_inc(sem("row_free"), inc)

            mark(H)
            with pe.Fori(0, NT) as t:
                for c in range(2):
                    pe.wait_ge(sem("zeros"), 1)
                    nc.tensor.matmul(ps[c], p.zero[:, :], p.cons[:, 0:512], start=True, stop=False, skip_group_check=True)
                with pe.Fori(0, NH) as h:
                    for s in range(TOPK):
                        pe.wait_ge(sem("diags"), (t * NH + h) * TOPK + s + 1)
                        for c in range(2):
                            mm = nc.tensor.matmul(ps[c], p.diag[:, s % H, :], p.uv[:, s % H, D + 512 * c:D + 512 * c + 512],
                                                  start=False, stop=False, skip_group_check=True)
                        mm.then_inc(sem("row_free"), 1)
                for c in range(2):
                    mm = nc.tensor.matmul(ps[c], p.zero[:, :], p.cons[:, 0:512], start=False, stop=True, skip_group_check=True)
                mm.then_inc(sem("tile_sum"), 1)
                pe.wait_ge(sem("y_read"), 2 * t + 2)
                nc.tensor.matmul(ps[2][:, 0:8], p.ident, p.ident[:, 0:8], start=True, stop=True)


def finish(p):
    nc, d, sem = p.nc, p.d, p.sem
    with nc.Block() as block:
        @block.scalar
        def _(act):
            for t in range(NT):
                if t >= 1:
                    act.wait_ge(sem("square1"), t)
                nc.scalar.activation(p.junk[:, :], p.x[:, t, :], ACT.Square, accum_out=p.ss1[:, t:t + 1]).then_inc(sem("square1"), 1)
            act.wait_ge(sem("square1"), NT)
            nc.scalar.activation(p.rt1[:, 0:NT], p.ss1[:, 0:NT], ACT.Sqrt, bias=p.eps[:, 0:1], scale=1.0 / D).then_inc(sem("root1"), 1)

        @block.vector
        def _(dve):
            dve.wait_ge(sem("root1"), 1)
            own = Chain(dve, sem("dve_mod"))
            own.link(nc.vector.reciprocal(p.rt1[:, 0:NT], p.rt1[:, 0:NT]))
            dve.wait_ge(sem("load_vec"), 16)
            for t in range(NT):
                nc.vector.scalar_tensor_tensor(out=p.x[:, t, :], in0=p.x[:, t, :], scalar=p.rt1[:, t:t + 1], in1=p.tmp[:, :],
                                               op0=ALU.mult, op1=ALU.mult).then_inc(sem("y_ready"), 1)

        @block.sync
        def _(sp):
            sp.dma_start(p.tmp[:, :], d["g_final"].to_broadcast([P, D])).then_inc(sem("load_vec"), 16)
            sp.wait_ge(sem("y_ready"), 1)
            sp.dma_start(d["yp"], p.x[:, 0, :]).then_inc(sem("store_y"), 16)
            sp.wait_ge(sem("y_ready"), NT)
            sp.dma_start(d["ys"], p.x[:, 1:NT, :]).then_inc(sem("store_y"), 16)
            sp.wait_ge(sem("store_y"), 32)


def build(nc, dram):
    p = Prog(nc, dram)
    with ExitStack() as ctx:
        p.psall = ctx.enter_context(nc.psum_tensor("psall", [P, 8 * 512], F32))
        p.ps = [p.psall[:, 512 * i:512 * i + 512] for i in range(8)]
        p.score2 = lambda s, nk: p.psall[:, 512 * s:512 * s + nk]
        sb = p.sb
        p.x = sb(ctx, "x", [P, NT, D])
        p.cons = sb(ctx, "cons", [P, CONS])
        p.rope = sb(ctx, "rope", [P, 2, 4, 32])
        p.sc = sb(ctx, "sc", [P, KT, 2])
        p.vec = sb(ctx, "vec", [P, V_END])
        p.row = sb(ctx, "row", [P, R_END])
        p.mod = sb(ctx, "mod", [P, 48, 2])
        p.A1 = sb(ctx, "A1", [P, KT, 2])
        p.A2 = sb(ctx, "A2", [P, KT, 2])
        p.ss1 = sb(ctx, "ss1", [P, 8])
        p.rt1 = sb(ctx, "rt1", [P, 8])
        p.junk = sb(ctx, "junk", [P, D])
        p.ident = p.cons[:, 0:P]
        p.ones = p.cons[:, P:2 * P]
        p.imask = p.cons[:, 2 * P:4 * P].rearrange("p (d n) -> p d n", d=2)
        p.lmask = p.cons[:, 4 * P:18 * P].rearrange("p (d l n) -> p d l n", d=2, l=7)
        p.io16 = p.cons[:, 18 * P:18 * P + 16]
        p.eps = p.cons[:, 18 * P + 16:18 * P + 17]
        p.one = p.cons[:, 18 * P + 17:18 * P + 18]
        start(p)
        outer = set(p.sems)
        with nc.Fori(0, L) as lay:
            layer(p, lay)
            for name, s in p.sems.items():
                if name not in outer and not name.startswith("row_in"):
                    nc.sync.sem_clear(s)
            nc.all_engine_barrier()
        p.tmp = sb(ctx, "tmp", [P, D])
        finish(p)


def layer(p, lay):
    sb = p.sb

    with ExitStack() as whole:
        p.mixed = sb(whole, "mixed", [P, NT, D])
        with ExitStack() as c1:
            p.proj = sb(c1, "proj", [P, NT, TM])
            p.sso = sb(c1, "sso", [P, NT, 4])
            p.oC = sb(c1, "oC", [P, NT, 256])
            p.rl = sb(c1, "rl", [P, 2, NT])
            p.ssl = sb(c1, "ssl", [P, 2, NT])
            p.krp = sb(c1, "krp", [P, NT, 96])
            with ExitStack() as c2:
                p.qkv = sb(c2, "qkv", [P, NT, 768])
                with ExitStack() as c3:
                    p.qkvT = sb(c3, "qkvT", [P, 6, LINE])
                    with ExitStack() as c4:
                        p.hT = sb(c4, "hT", [P, KT, TOK])
                        p.xn = sb(c4, "xn", [P, 2, D])
                        p.mrow = sb(c4, "mrow", [2, 2, WCH])
                        p.wring = sb(c4, "wring", [P, 3, KT, WCH])
                        mod_and_project(p, lay)
                    with ExitStack() as c4:
                        p.convd = sb(c4, "convd", [P, 6, LINE - 2])
                        conv(p)
                with ExitStack() as c3:
                    p.ssd = sb(c3, "ssd", [P, NT, 8])
                    p.rd = sb(c3, "rd", [P, NT, 8])
                    p.zz = sb(c3, "zz", [P, NT, 8])
                    p.zab = sb(c3, "zab", [P, NT, 8])
                    p.sp1 = sb(c3, "sp1", [P, NT, 8])
                    p.bet = sb(c3, "bet", [P, NT, 8])
                    p.eal = sb(c3, "eal", [P, 8])
                    p.g = sb(c3, "g", [P, NT, 8])
                    p.gcol = sb(c3, "gcol", [P, NT, 8])
                    p.egc = sb(c3, "egc", [P, NT, 8])
                    p.dif = sb(c3, "dif", [P, 2, HC, P])
                    p.dec = sb(c3, "dec", [P, 2, HC, P])
                    p.lt = sb(c3, "lt", [P, 2, HC, P])
                    p.mlt = sb(c3, "mlt", [P, 2, 2, HC, P])
                    p.X = sb(c3, "X", [P, 2, HC, P])
                    p.XT = sb(c3, "XT", [P, 2, HC, P])
                    p.t1s = sb(c3, "t1s", [P, 2, HC * P])
                    p.qk = sb(c3, "qk", [P, 2, HC, P])
                    p.rv = sb(c3, "rv", [P, 2, HC, 64])
                    p.kd = sb(c3, "kd", [P, 2, HC, 64])
                    p.w = sb(c3, "w", [P, 2, HC, 64])
                    p.kT = sb(c3, "kT", [64, 2, HC * P])
                    p.qT = sb(c3, "qT", [64, 2, HC * P])
                    p.egr = sb(c3, "egr", [64, 2, HC, P])
                    p.qd = sb(c3, "qd", [64, 2, HC, P])
                    p.state = sb(c3, "state", [64, 2, HC, 64])
                    delta(p, lay)
            with ExitStack() as c2:
                p.qTa = sb(c2, "qTa", [P, 2, TOK])
                p.kTa = sb(c2, "kTa", [P, 2, KEYS])
                p.cav = sb(c2, "cav", [P, 256])
                p.lam = sb(c2, "lam", [P, 8])
                p.vb = sb(c2, "vb", [P, 6, 512])
                p.qTb = sb(c2, "qTb", [96, HB, TOK])
                p.kTb = sb(c2, "kTb", [96, HB, KEYS])
                with ExitStack() as c3:
                    p.cak = sb(c3, "cak", [P, 256])
                    p.cckv = sb(c3, "cckv", [P, 128])
                    p.ckr = sb(c3, "ckr", [P, 96])
                    p.qcT = sb(c3, "qcT", [P, 2, TOK])
                    p.ckvT = sb(c3, "ckvT", [P, KEYS])
                    p.wuq = sb(c3, "wuq", [P, 2, 768])
                    p.wukn = sb(c3, "wukn", [P, 512])
                    p.wukv = sb(c3, "wukv", [P, 512])
                    p.qb = sb(c3, "qb", [P, 2, 768])
                    p.ru = sb(c3, "ru", [P, 512])
                    p.rv2 = sb(c3, "rv2", [P, 512])
                    prepare_attention(p, lay)
                with ExitStack() as c3:
                    p.prob = sb(c3, "prob", [P, PROBS, 640])
                    p.probT = sb(c3, "probT", [P, 2, 640])
                    p.mx = sb(c3, "mx", [P, 4])
                    p.nmax = sb(c3, "nmax", [P, 4])
                    p.esum = sb(c3, "esum", [P, 4])
                    p.r01 = sb(c3, "r01", [P, 2, 2])
                    p.ssa = sb(c3, "ssa", [P, NT, 4])
                    p.gsub = sb(c3, "gsub", [P, 64])
                    attend(p)
        p.gt2 = sb(whole, "gt2", [P, 2, D])
        p.gat = sb(whole, "gat", [P, NT, SLOTS])
        p.eidx = sb(whole, "eidx", [P, NT, SLOTS], U32)
        with ExitStack() as c1:
            region = sb(c1, "region", [P, RING * 2 * D])
            p.h2T = region[:, 0:KT * TOK].rearrange("p (k n) -> p k n", k=KT)
            p.wring2 = region[:, KT * TOK:KT * TOK + 2 * KT * WCH].rearrange("p (b k n) -> p b k n", b=2, k=KT)
            p.uv = region[:, :].rearrange("p (s n) -> p s n", s=RING)
            with ExitStack() as c2:
                p.mixedT = sb(c2, "mixedT", [P, len(UNTURNED), TOK])
                p.rows = sb(c2, "rows", [P, 3, 2, D])
                p.diag4 = sb(c2, "diag4", [P, 2, 512])
                p.gated = sb(c2, "gated", [P, D])
                project_out(p, lay)
            p.sub = sb(c1, "sub", [P, NT, 2048])
            p.r_sub = sb(c1, "r_sub", [P, 2 * NK])
            p.r_top = sb(c1, "r_top", [P, 2, TOPK])
            p.r_ix = sb(c1, "r_ix", [P, 2, TOPK], U32)
            p.r_ixf = sb(c1, "r_ixf", [P, 2, TOPK])
            p.r_cand = sb(c1, "r_cand", [P, TOPK * TOPK])
            p.r_best = sb(c1, "r_best", [P, TOPK])
            p.r_pos = sb(c1, "r_pos", [P, TOPK], U32)
            p.r_ij = sb(c1, "r_ij", [P, 2, TOPK], U32)
            p.r_ijf = sb(c1, "r_ijf", [P, 2, TOPK])
            p.r_gate = sb(c1, "r_gate", [P, TOPK])
            p.r_gs = sb(c1, "r_gs", [P, 2])
            p.r_pick = sb(c1, "r_pick", [P, 2, TOPK, TOPK])
            p.r_ex = sb(c1, "r_ex", [P, 2, TOPK])
            p.r_e = sb(c1, "r_e", [P, TOPK])
            with ExitStack() as c2:
                p.qpT = sb(c2, "qpT", [P, 2, 4, TOK])
                p.keysT = sb(c2, "keysT", [P, 16 * P])
                route(p, lay)
            p.hcur = sb(c1, "hcur", [P, D])
            p.y = sb(c1, "y", [P, D])
            p.diag = sb(c1, "diag", [P, RING, P])
            p.zero = sb(c1, "zero", [P, P])
            p.dot = sb(c1, "dot", [P, TOPK])
            p.act16 = sb(c1, "act16", [P, TOPK])
            p.wgt = sb(c1, "wgt", [P, TOPK])
            p.stage = sb(c1, "stage", [P, 2, RING], U32)
            experts(p, lay)


CONS = 18 * P + 18


def constants():
    i = np.arange(P)
    c = np.zeros((P, CONS), np.float32)
    c[:, 0:P] = np.eye(P)
    c[:, P:2 * P] = 1.0
    upper = (i[:, None] <= i[None, :]).astype(np.float32)
    c[:, 2 * P:3 * P] = upper
    c[:, 3 * P:4 * P] = upper.T
    for lvl in range(LEVELS):
        b = 2 ** lvl
        join = ((i[:, None] // (2 * b) == i[None, :] // (2 * b)) & (i[:, None] // b % 2 == 0) & (i[None, :] // b % 2 == 1))
        c[:, (4 + lvl) * P:(5 + lvl) * P] = join
        c[:, (11 + lvl) * P:(12 + lvl) * P] = join.T
    c[:, 18 * P:18 * P + 16] = np.arange(16)
    c[:, 18 * P + 16] = EPS
    c[:, 18 * P + 17] = 1.0
    t = np.arange(512)
    n_freq = 8
    freqs = (np.float32(10000.0) ** (-np.arange(n_freq, dtype=np.float32) / n_freq)).astype(np.float32)
    ar = (t // 64).astype(np.float32)[:, None] * freqs
    ac = (t % 64).astype(np.float32)[:, None] * freqs
    ang = np.concatenate([ar, ar, ac, ac], axis=-1)
    sign = np.repeat([-1.0, 1.0, -1.0, 1.0], 8).astype(np.float32)
    tables = np.stack([np.cos(ang), np.sin(ang) * sign]).astype(np.float32)
    rope = tables.reshape(2, 4, P, 32).transpose(2, 0, 1, 3)
    return c, np.ascontiguousarray(rope)


def lay_out(i):
    f = {n: np.asarray(a) for n, a in i.items()}

    def kmajor(w):
        l, k, n = w.shape
        return w.reshape(l, k // P, P, n).transpose(0, 2, 1, 3)

    def fm(v):
        return v.reshape(L, -1, P).transpose(0, 2, 1)

    c_qkv, c_g = 1184, 1952
    w = f["w_in"]
    tm = np.concatenate([w[:, :, :c_qkv], w[:, :, c_g:]], axis=2)
    ukv = f["w_ukv"].reshape(L, P, HB, 2, 64)
    lam = [f[n] for n in ("lam_q1", "lam_k1", "lam_q2", "lam_k2")]
    li = [0.8 - 0.6 * math.exp(-0.3 * l) for l in range(L)]
    layer_consts = np.array([[v, 1.0 - v, l * NK * NK] for l, v in enumerate(li)], np.float32)
    rows = np.concatenate([f["g_subln"], f["g_qc"], f["g_kvc"], f["g_onorm"]] + lam
                          + [f["a_log_f"], f["a_log_b"], f["dt_bias_f"], f["dt_bias_b"], layer_consts], axis=1)
    conv_w = f["conv_c"].reshape(L, 3, 6, P).transpose(0, 3, 2, 1).reshape(L, P, 18)
    vecs = np.concatenate([fm(f["b_mod"]), fm(f["g_norm1"]), fm(f["g_norm2"]), conv_w], axis=2)
    cons, rope = constants()
    out = {
        "consts": cons, "rope": rope,
        "cond": np.stack([f["c_ctx"].reshape(KT, P).T, f["c"].reshape(KT, P).T], axis=2),
        "xp": f["x_prompt"].reshape(P, D),
        "xs": f["x_sample"].reshape(4, P, D).transpose(1, 0, 2),
        "vecs": vecs, "rows": rows,
        "w_mod": kmajor(f["w_mod"]), "w_in_tm": kmajor(tm), "w_in_fm": kmajor(w[:, :, c_qkv:c_g]),
        "cache_a_k": f["cache_a_k"].reshape(L, P, 256), "cache_a_v": f["cache_a_v"].reshape(L, P, 256),
        "cache_ckv": f["cache_b_ckv"].reshape(L, P, 128), "cache_kr": f["cache_b_krope"].reshape(L, P, 32),
        "in_sf": f["state_c_fwd"].reshape(L, HC, 64, 64), "in_sb": f["state_c_bwd"].reshape(L, HC, 64, 64),
        "w_uq": kmajor(f["w_uq"]), "w_ukn": ukv[:, :, :, 0].reshape(L, P, 512), "w_ukv": ukv[:, :, :, 1].reshape(L, P, 512),
        "w_out": kmajor(f["w_out"]), "w_pq": kmajor(f["w_pq"]),
        "keysT": f["peer_keys"].reshape(L, 16, NK, P).transpose(0, 3, 1, 2).reshape(L, P, 16 * NK),
        "peer_uv": np.concatenate([f["peer_u"], f["peer_v"]], axis=2).reshape(L * NK * NK, 2 * D),
        "g_final": f["g_final"].reshape(1, D),
    }
    return {n: np.ascontiguousarray(a, dtype=np.float32) for n, a in out.items()}


OUTS = {"yp": (P, D), "ys": (P, 4, D), "out_ak": (L, P, 256), "out_av": (L, P, 256), "out_ckv": (L, P, 128),
        "out_kr": (L, P, 32), "out_sf": (L, HC, 64, 64), "out_sb": (L, HC, 64, 64)}


def kernel(**inputs):
    import concourse.bacc as bacc
    from concourse.bass_utils import run_bass_kernel_spmd

    nc = bacc.Bacc("TRN2", target_bir_lowering=False, num_devices=1)
    arrays = lay_out(inputs)
    dram = {n: nc.dram_tensor("in_" + n, a.shape, F32, kind="ExternalInput").ap() for n, a in arrays.items()}
    dram.update({n: nc.dram_tensor("res_" + n, s, F32, kind="ExternalOutput").ap() for n, s in OUTS.items()})
    build(nc, dram)
    got = run_bass_kernel_spmd(nc, [{"in_" + n: a for n, a in arrays.items()}], core_ids=[0]).results[0]
    r = {n: got["res_" + n] for n in OUTS}
    return (r["yp"].reshape(1, P, D), r["ys"].transpose(1, 0, 2).reshape(1, 4 * P, D),
            r["out_ak"].reshape(1, L, P, HA, 2, 32), r["out_av"].reshape(1, L, P, HA, 64),
            r["out_ckv"].reshape(1, L, P, 128), r["out_kr"].reshape(1, L, P, 32),
            r["out_sf"].reshape(1, L, HC, 64, 64), r["out_sb"].reshape(1, L, HC, 64, 64))
```
